# Optimizing a Trainium2 kernel written in Bass

```python
import math
import jax, jax.numpy as jnp
from jax import lax
import numpy as np

D_MODEL = 1024
BATCH = 1
SEQ = 256
DEPTH = 2
DEC_BATCH = 8
DEC_SEQ = 1
PAST_LEN = 1024
PAGE_SIZE = 128

HEAD_DIM = 128
ROPE_THETA = 500000.0
EPS = 1e-6
QBLK = 128
NEG = -1e30
N_EVEN = (DEPTH + 1) // 2
N_ODD = DEPTH // 2
A_HEADS = 4
A_QK_DIM = HEAD_DIM // 2
A_WIDTH = A_HEADS * HEAD_DIM
B_HEADS = 4
B_WIDTH = B_HEADS * HEAD_DIM
IDX_HEADS = 4
IDX_DIM = 64
IDX_TOPK = 256
C_HEADS = 4
C_WIDTH = C_HEADS * HEAD_DIM
CMP_BLK = 32
CMP_STRIDE = 16
CMP_HIDDEN = 256
SEL_BLK = 64
N_SEL = 16
C_WINDOW = 512
FORCE_BONUS = 1e4
D_PAIRS = ((128, 1), (512, 4), (2048, 16))
D_HEADS = 4
D_WIDTH = D_HEADS * HEAD_DIM

EVEN_SPLITS = (A_WIDTH, A_WIDTH, A_WIDTH, A_WIDTH, B_WIDTH, HEAD_DIM, HEAD_DIM, B_WIDTH, IDX_HEADS * IDX_DIM, IDX_DIM, IDX_HEADS)
E_EVEN = sum(EVEN_SPLITS)
ODD_SPLITS = (C_WIDTH, HEAD_DIM, HEAD_DIM, HEAD_DIM, HEAD_DIM, HEAD_DIM, HEAD_DIM, 3 * C_HEADS, C_WIDTH) + (D_WIDTH,) * (3 * len(D_PAIRS)) + (D_WIDTH,)
E_ODD = sum(ODD_SPLITS)

kernel_name = 'hybrid_diff_dsa_nsa_dilated_step'

def rmsnorm(x, w=None):
    xf = x.astype(jnp.float32)
    y = xf * lax.rsqrt(jnp.mean(xf * xf, axis=-1, keepdims=True) + EPS)
    if w is not None:
        y = y * w.astype(jnp.float32)
    return y.astype(x.dtype)

def split_cols(z, sizes):
    offs = [int(o) for o in np.cumsum(sizes)[:-1]]
    return jnp.split(z, offs, axis=-1)

def rope(x, pos):
    dim = x.shape[-1]
    rot = dim // 4
    half = rot // 2
    freqs = ROPE_THETA ** (-jnp.arange(half, dtype=jnp.float32) / half)
    ang = pos.astype(jnp.float32)[:, None] * freqs
    ang = ang.reshape(ang.shape[0], *([1] * (x.ndim - 3)), half)
    cos, sin = jnp.cos(ang), jnp.sin(ang)
    xf = x.astype(jnp.float32)
    x1, x2, rest = xf[..., :half], xf[..., half:rot], xf[..., rot:]
    out = jnp.concatenate([x1 * cos - x2 * sin, x2 * cos + x1 * sin, rest], axis=-1)
    return out.astype(x.dtype)

def masked_softmax(s, mask):
    s = jnp.where(mask, s.astype(jnp.float32), NEG)
    m = jnp.max(s, axis=-1, keepdims=True)
    e = jnp.where(mask, jnp.exp(s - m), 0.0)
    d = jnp.sum(e, axis=-1, keepdims=True)
    return e / jnp.where(d > 0, d, 1.0), m, d

def blockwise(fn, qpos, *qs):
    T = qpos.shape[0]
    if T <= QBLK or T % QBLK:
        return fn(qpos, *qs)
    nb = T // QBLK
    def split(a):
        return jnp.moveaxis(a.reshape(a.shape[0], nb, QBLK, *a.shape[2:]), 1, 0)
    out = lax.map(lambda args: fn(*args), (qpos.reshape(nb, QBLK),) + tuple(split(a) for a in qs))
    out = jnp.moveaxis(out, 0, 1)
    return out.reshape(out.shape[0], T, *out.shape[3:])

def fetch_local(rows, pos):
    return jax.vmap(lambda r, p: r[p])(rows, jnp.clip(pos, 0, rows.shape[1] - 1))

def paged_logical(pool, page_table):
    g = pool[page_table]
    return g.reshape(g.shape[0], g.shape[1] * g.shape[2], *g.shape[3:])

def fetch_paged(pool, page_table, new_rows, pos):
    B = pos.shape[0]
    pc = jnp.clip(pos, 0, PAST_LEN - 1)
    page = jnp.take_along_axis(page_table, (pc // PAGE_SIZE).reshape(B, -1), axis=1).reshape(pos.shape)
    flat = pool.reshape(-1, *pool.shape[2:])
    past_rows = flat[page * PAGE_SIZE + pc % PAGE_SIZE]
    new = fetch_local(new_rows, pos - PAST_LEN)
    is_past = (pos < PAST_LEN).reshape(pos.shape + (1,) * (past_rows.ndim - pos.ndim))
    return jnp.where(is_past, past_rows, new)

def diff_attention(q, k, v, qpos, lam, lam_init):
    kpos = jnp.arange(k.shape[1], dtype=jnp.int32)
    def blk(qp, qb):
        s = jnp.einsum('bqhmd,bkhmd->bhmqk', qb, k) * (A_QK_DIM ** -0.5)
        p, _, _ = masked_softmax(s, kpos[None, :] <= qp[:, None])
        attn = p[:, :, 0] - lam * p[:, :, 1]
        return jnp.einsum('bhqk,bkhd->bqhd', attn.astype(v.dtype), v)
    o = blockwise(blk, qpos, q)
    return rmsnorm(o) * (1.0 - lam_init)

def dsa_attention(q, qi, wi, ki, fetch_k, fetch_v, qpos):
    L = ki.shape[1]
    n_keep = min(IDX_TOPK, L // 4)
    kpos = jnp.arange(L, dtype=jnp.int32)
    def blk(qp, qb, qib, wib):
        sc = jax.nn.relu(jnp.einsum('bqhd,bkd->bqhk', qib, ki) * (IDX_DIM ** -0.5))
        score = jnp.einsum('bqh,bqhk->bqk', wib * (IDX_HEADS ** -0.5), sc).astype(jnp.float32)
        score = jnp.where(kpos[None, None, :] <= qp[None, :, None], score, NEG)
        _, sel = lax.top_k(score, n_keep)
        ks, vs = fetch_k(sel), fetch_v(sel)
        s = jnp.einsum('bqhd,bqkd->bhqk', qb, ks) * (HEAD_DIM ** -0.5)
        p, _, _ = masked_softmax(s, (sel <= qp[None, :, None])[:, None])
        return jnp.einsum('bhqk,bqkd->bqhd', p.astype(vs.dtype), vs)
    return blockwise(blk, qpos, q, qi, wi)

def compress(rows, pos_emb, w1, w2):
    L = rows.shape[1]
    n_cmp = (L - CMP_BLK) // CMP_STRIDE + 1
    idx = jnp.arange(n_cmp, dtype=jnp.int32)[:, None] * CMP_STRIDE + jnp.arange(CMP_BLK, dtype=jnp.int32)[None, :]
    blocks = rows[:, idx] + pos_emb
    hid = jax.nn.gelu(jnp.einsum('bnrd,rdh->bnh', blocks, w1))
    return hid @ w2, idx[:, -1]

def nsa_attention(q, gate_logits, k_cmp, v_cmp, fetch_k, fetch_v, kw, vw, kw_pos0, qpos, cmp_pos, cmp_w1, cmp_w2):
    L = k_cmp.shape[1]
    kc, end_pos = compress(k_cmp, cmp_pos[0], cmp_w1[0], cmp_w2[0])
    vc, _ = compress(v_cmp, cmp_pos[1], cmp_w1[1], cmp_w2[1])
    kc = rope(kc, end_pos)
    n_sel = -(-L // SEL_BLK)
    n_top = min(N_SEL, n_sel)
    cstart = jnp.arange(kc.shape[1], dtype=jnp.int32) * CMP_STRIDE
    sstart = jnp.arange(n_sel, dtype=jnp.int32) * SEL_BLK
    overlap = ((cstart[:, None] < sstart[None, :] + SEL_BLK) & (cstart[:, None] + CMP_BLK > sstart[None, :])).astype(jnp.float32)
    kw_pad = jnp.pad(kw, ((0, 0), (C_WINDOW, 0), (0, 0)))
    vw_pad = jnp.pad(vw, ((0, 0), (C_WINDOW, 0), (0, 0)))
    scale = HEAD_DIM ** -0.5
    def blk(qp, qb, gb):
        QB = qp.shape[0]
        s = jnp.einsum('bqhd,bnd->bhqn', qb, kc) * scale
        p_c, _, _ = masked_softmax(s, end_pos[None, :] <= qp[:, None])
        o_cmp = jnp.einsum('bhqn,bnd->bqhd', p_c.astype(vc.dtype), vc)
        imp = jnp.einsum('bhqn,nj->bqj', p_c, overlap)
        j = jnp.arange(n_sel, dtype=jnp.int32)[None, :]
        cur = (qp // SEL_BLK)[:, None]
        forced = (j == 0) | (j == cur) | (j == cur - 1)
        imp = jnp.where(forced, imp + FORCE_BONUS, imp)
        imp = jnp.where(j * SEL_BLK <= qp[:, None], imp, NEG)
        _, blk_idx = lax.top_k(imp, n_top)
        sel_pos = (blk_idx[..., None] * SEL_BLK + jnp.arange(SEL_BLK, dtype=jnp.int32)).reshape(blk_idx.shape[0], QB, n_top * SEL_BLK)
        ks, vs = fetch_k(sel_pos), fetch_v(sel_pos)
        s = jnp.einsum('bqhd,bqkd->bhqk', qb, ks) * scale
        p_s, _, _ = masked_softmax(s, (sel_pos <= qp[None, :, None])[:, None])
        o_sel = jnp.einsum('bhqk,bqkd->bqhd', p_s.astype(vs.dtype), vs)
        start = qp[0] - kw_pos0
        kwb = lax.dynamic_slice_in_dim(kw_pad, start, C_WINDOW + QB, axis=1)
        vwb = lax.dynamic_slice_in_dim(vw_pad, start, C_WINDOW + QB, axis=1)
        kpos = qp[0] - C_WINDOW + jnp.arange(C_WINDOW + QB, dtype=jnp.int32)
        dist = qp[:, None] - kpos[None, :]
        wmask = (dist >= 0) & (dist <= C_WINDOW) & (kpos[None, :] >= kw_pos0)
        s = jnp.einsum('bqhd,bkd->bhqk', qb, kwb) * scale
        p_w, _, _ = masked_softmax(s, wmask)
        o_win = jnp.einsum('bhqk,bkd->bqhd', p_w.astype(vwb.dtype), vwb)
        g = jax.nn.sigmoid(gb.astype(jnp.float32)).astype(qb.dtype)
        return g[..., 0:1] * o_cmp + g[..., 1:2] * o_sel + g[..., 2:3] * o_win
    return blockwise(blk, qpos, q, gate_logits)

def dilated_attention(qs, ks, vs, pos0s, qpos):
    scale = HEAD_DIM ** -0.5
    def blk(qp, *qbs):
        outs, lses = [], []
        for (w, d), qb, k, v, p0 in zip(D_PAIRS, qbs, ks, vs, pos0s):
            kpos = qp[:, None] - d * jnp.arange(w // d + 1, dtype=jnp.int32)[None, :]
            idx = jnp.clip(kpos - p0, 0, k.shape[1] - 1)
            kg, vg = k[:, idx], v[:, idx]
            s = jnp.einsum('bqhd,bqnhd->bhqn', qb, kg) * scale
            p, m, den = masked_softmax(s, kpos >= p0)
            outs.append(jnp.einsum('bhqn,bqnhd->bqhd', p.astype(vg.dtype), vg))
            lses.append(m[..., 0] + jnp.log(den[..., 0]))
        alpha = jax.nn.softmax(jnp.stack(lses), axis=0)
        alpha = jnp.transpose(alpha, (0, 1, 3, 2))[..., None].astype(outs[0].dtype)
        return jnp.sum(alpha * jnp.stack(outs), axis=0)
    return blockwise(blk, qpos, *qs)

def even_layer(x, pos, pre_w, post_w, w_in, w_out, lam_p, lam_init, past):
    B, T, _ = x.shape
    z = rmsnorm(x, pre_w) @ w_in
    qa, ka, va, ga, qb, kb, vb, gb, qi, ki, wi = split_cols(z, EVEN_SPLITS)
    qa = rope(qa.reshape(B, T, A_HEADS, 2, A_QK_DIM), pos)
    ka = rope(ka.reshape(B, T, A_HEADS, 2, A_QK_DIM), pos)
    va = va.reshape(B, T, A_HEADS, HEAD_DIM)
    qb = rope(qb.reshape(B, T, B_HEADS, HEAD_DIM), pos)
    kb = rope(kb, pos)
    qi = rope(qi.reshape(B, T, IDX_HEADS, IDX_DIM), pos)
    ki = rope(ki, pos)
    if past is None:
        ka_all, va_all, ki_all = ka, va, ki
        fetch_k = lambda p: fetch_local(kb, p)
        fetch_v = lambda p: fetch_local(vb, p)
    else:
        pt, c_ak, c_av, c_bk, c_bv, c_bi = past
        ka_all = jnp.concatenate([paged_logical(c_ak, pt), ka], axis=1)
        va_all = jnp.concatenate([paged_logical(c_av, pt), va], axis=1)
        ki_all = jnp.concatenate([paged_logical(c_bi, pt), ki], axis=1)
        fetch_k = lambda p: fetch_paged(c_bk, pt, kb, p)
        fetch_v = lambda p: fetch_paged(c_bv, pt, vb, p)
    lq = lam_p.astype(jnp.float32)
    lam = jnp.exp(jnp.sum(lq[0] * lq[1])) - jnp.exp(jnp.sum(lq[2] * lq[3])) + lam_init
    oa = diff_attention(qa, ka_all, va_all, pos, lam, lam_init)
    ob = dsa_attention(qb, qi, wi, ki_all, fetch_k, fetch_v, pos)
    mix = jnp.concatenate([oa.reshape(B, T, A_WIDTH) * jax.nn.silu(ga), ob.reshape(B, T, B_WIDTH) * jax.nn.silu(gb)], axis=-1)
    y = x + rmsnorm(mix @ w_out, post_w)
    return y, (ka, va, kb, vb, ki)

def odd_layer(x, pos, pre_w, post_w, w_in, w_out, cmp_pos, cmp_w1, cmp_w2, past):
    B, T, _ = x.shape
    parts = split_cols(rmsnorm(x, pre_w) @ w_in, ODD_SPLITS)
    qc, kcr, vcr, ksel, vsel, kwin, vwin, gl, gc = parts[:9]
    gd = parts[-1]
    qc = rope(qc.reshape(B, T, C_HEADS, HEAD_DIM), pos)
    ksel = rope(ksel, pos)
    kwin = rope(kwin, pos)
    gl = gl.reshape(B, T, C_HEADS, 3)
    n_g = len(D_PAIRS)
    qd = [rope(parts[9 + 3 * g].reshape(B, T, D_HEADS, HEAD_DIM), pos) for g in range(n_g)]
    kd = [rope(parts[10 + 3 * g].reshape(B, T, D_HEADS, HEAD_DIM), pos) for g in range(n_g)]
    vd = [parts[11 + 3 * g].reshape(B, T, D_HEADS, HEAD_DIM) for g in range(n_g)]
    if past is None:
        kc_all, vc_all, kw_all, vw_all, kw0 = kcr, vcr, kwin, vwin, 0
        fetch_k = lambda p: fetch_local(ksel, p)
        fetch_v = lambda p: fetch_local(vsel, p)
        kd_all, vd_all, pos0s = kd, vd, [0] * n_g
    else:
        pt, c_ck, c_cv, c_sk, c_sv, s_wk, s_wv, d_bufs = past
        kc_all = jnp.concatenate([paged_logical(c_ck, pt), kcr], axis=1)
        vc_all = jnp.concatenate([paged_logical(c_cv, pt), vcr], axis=1)
        fetch_k = lambda p: fetch_paged(c_sk, pt, ksel, p)
        fetch_v = lambda p: fetch_paged(c_sv, pt, vsel, p)
        kw_all = jnp.concatenate([s_wk, kwin], axis=1)
        vw_all = jnp.concatenate([s_wv, vwin], axis=1)
        kw0 = PAST_LEN - s_wk.shape[1]
        kd_all = [jnp.concatenate([d_bufs[2 * g], kd[g]], axis=1) for g in range(n_g)]
        vd_all = [jnp.concatenate([d_bufs[2 * g + 1], vd[g]], axis=1) for g in range(n_g)]
        pos0s = [PAST_LEN - d_bufs[2 * g].shape[1] for g in range(n_g)]
    oc = nsa_attention(qc, gl, kc_all, vc_all, fetch_k, fetch_v, kw_all, vw_all, kw0, pos, cmp_pos, cmp_w1, cmp_w2)
    od = dilated_attention(qd, kd_all, vd_all, pos0s, pos)
    mix = jnp.concatenate([oc.reshape(B, T, C_WIDTH) * jax.nn.silu(gc), od.reshape(B, T, D_WIDTH) * jax.nn.silu(gd)], axis=-1)
    y = x + rmsnorm(mix @ w_out, post_w)
    keep = lambda a, w: a[:, a.shape[1] - min(w, a.shape[1]):]
    d_new = []
    for g, (w, _) in enumerate(D_PAIRS):
        d_new += [keep(kd_all[g], w), keep(vd_all[g], w)]
    return y, (kcr, vcr, ksel, vsel, keep(kw_all, C_WINDOW), keep(vw_all, C_WINDOW), *d_new)

def setup_inputs(seed: int = 0) -> dict:
    key = jax.random.key(seed)
    ks = jax.random.split(key, 40)
    cnt = [0]
    def nxt():
        k = ks[cnt[0]]
        cnt[0] += 1
        return k
    def nrm(shape, scale=1.0):
        return scale * jax.random.normal(nxt(), shape, dtype=jnp.float32)
    n_pages = PAST_LEN // PAGE_SIZE
    n_pool = (DEC_BATCH * n_pages * 5) // 4
    c_win = min(C_WINDOW, PAST_LEN)
    inp = {}
    inp['x_prompt'] = nrm((BATCH, SEQ, D_MODEL))
    inp['x_sample'] = nrm((DEC_BATCH, DEC_SEQ, D_MODEL))
    inp['cache_a_k'] = nrm((N_EVEN, n_pool, PAGE_SIZE, A_HEADS, 2, A_QK_DIM))
    inp['cache_a_v'] = nrm((N_EVEN, n_pool, PAGE_SIZE, A_HEADS, HEAD_DIM))
    inp['cache_b_k'] = nrm((N_EVEN, n_pool, PAGE_SIZE, HEAD_DIM))
    inp['cache_b_v'] = nrm((N_EVEN, n_pool, PAGE_SIZE, HEAD_DIM))
    inp['cache_b_idx'] = nrm((N_EVEN, n_pool, PAGE_SIZE, IDX_DIM))
    inp['cache_c_cmp_k'] = nrm((N_ODD, n_pool, PAGE_SIZE, HEAD_DIM))
    inp['cache_c_cmp_v'] = nrm((N_ODD, n_pool, PAGE_SIZE, HEAD_DIM))
    inp['cache_c_sel_k'] = nrm((N_ODD, n_pool, PAGE_SIZE, HEAD_DIM))
    inp['cache_c_sel_v'] = nrm((N_ODD, n_pool, PAGE_SIZE, HEAD_DIM))
    inp['state_c_win_k'] = nrm((N_ODD, DEC_BATCH, c_win, HEAD_DIM))
    inp['state_c_win_v'] = nrm((N_ODD, DEC_BATCH, c_win, HEAD_DIM))
    for g, (w, _) in enumerate(D_PAIRS):
        inp['state_d_k%d' % g] = nrm((N_ODD, DEC_BATCH, min(w, PAST_LEN), D_HEADS, HEAD_DIM))
        inp['state_d_v%d' % g] = nrm((N_ODD, DEC_BATCH, min(w, PAST_LEN), D_HEADS, HEAD_DIM))
    perm = jax.random.permutation(nxt(), n_pool)
    inp['page_table'] = perm[:DEC_BATCH * n_pages].reshape(DEC_BATCH, n_pages).astype(jnp.int32)
    inp['pre_norm'] = 1.0 + nrm((DEPTH, D_MODEL), 0.05)
    inp['post_norm'] = 1.0 + nrm((DEPTH, D_MODEL), 0.05)
    inp['w_in_even'] = nrm((N_EVEN, D_MODEL, E_EVEN), D_MODEL ** -0.5)
    inp['w_out_even'] = nrm((N_EVEN, A_WIDTH + B_WIDTH, D_MODEL), (A_WIDTH + B_WIDTH) ** -0.5)
    inp['diff_lambda'] = nrm((N_EVEN, 4, A_QK_DIM), 0.1)
    inp['w_in_odd'] = nrm((N_ODD, D_MODEL, E_ODD), D_MODEL ** -0.5)
    inp['w_out_odd'] = nrm((N_ODD, C_WIDTH + D_WIDTH, D_MODEL), (C_WIDTH + D_WIDTH) ** -0.5)
    inp['cmp_pos'] = nrm((N_ODD, 2, CMP_BLK, HEAD_DIM), 0.1)
    inp['cmp_w1'] = nrm((N_ODD, 2, CMP_BLK, HEAD_DIM, CMP_HIDDEN), (CMP_BLK * HEAD_DIM) ** -0.5)
    inp['cmp_w2'] = nrm((N_ODD, 2, CMP_HIDDEN, HEAD_DIM), CMP_HIDDEN ** -0.5)
    return inp

def reference(x_prompt, x_sample, cache_a_k, cache_a_v, cache_b_k, cache_b_v, cache_b_idx, cache_c_cmp_k, cache_c_cmp_v, cache_c_sel_k, cache_c_sel_v, state_c_win_k, state_c_win_v, state_d_k0, state_d_v0, state_d_k1, state_d_v1, state_d_k2, state_d_v2, page_table, pre_norm, post_norm, w_in_even, w_out_even, diff_lambda, w_in_odd, w_out_odd, cmp_pos, cmp_w1, cmp_w2):
    pos_p = jnp.arange(SEQ, dtype=jnp.int32)
    pos_s = PAST_LEN + jnp.arange(DEC_SEQ, dtype=jnp.int32)
    y_prompt, y_sample = x_prompt, x_sample
    ev_p, ev_s, od_p, od_s = [], [], [], []
    for layer in range(DEPTH):
        i = layer // 2
        if layer % 2 == 0:
            lam_init = 0.8 - 0.6 * math.exp(-0.3 * layer)
            w = (pre_norm[layer], post_norm[layer], w_in_even[i], w_out_even[i], diff_lambda[i], lam_init)
            y_prompt, st = even_layer(y_prompt, pos_p, *w, None)
            ev_p.append(st)
            past = (page_table, cache_a_k[i], cache_a_v[i], cache_b_k[i], cache_b_v[i], cache_b_idx[i])
            y_sample, st = even_layer(y_sample, pos_s, *w, past)
            ev_s.append(st)
        else:
            w = (pre_norm[layer], post_norm[layer], w_in_odd[i], w_out_odd[i], cmp_pos[i], cmp_w1[i], cmp_w2[i])
            y_prompt, st = odd_layer(y_prompt, pos_p, *w, None)
            od_p.append(st)
            d_bufs = (state_d_k0[i], state_d_v0[i], state_d_k1[i], state_d_v1[i], state_d_k2[i], state_d_v2[i])
            past = (page_table, cache_c_cmp_k[i], cache_c_cmp_v[i], cache_c_sel_k[i], cache_c_sel_v[i], state_c_win_k[i], state_c_win_v[i], d_bufs)
            y_sample, st = odd_layer(y_sample, pos_s, *w, past)
            od_s.append(st)
    stack = lambda sts: [jnp.stack(t) for t in zip(*sts)]
    p_a_k, p_a_v, p_b_k, p_b_v, p_b_idx = stack(ev_p)
    s_a_k, s_a_v, s_b_k, s_b_v, s_b_idx = stack(ev_s)
    p_c_cmp_k, p_c_cmp_v, p_c_sel_k, p_c_sel_v, p_c_win_k, p_c_win_v, p_d_k0, p_d_v0, p_d_k1, p_d_v1, p_d_k2, p_d_v2 = stack(od_p)
    s_c_cmp_k, s_c_cmp_v, s_c_sel_k, s_c_sel_v, s_c_win_k, s_c_win_v, s_d_k0, s_d_v0, s_d_k1, s_d_v1, s_d_k2, s_d_v2 = stack(od_s)
    return (y_prompt, y_sample, p_a_k, p_a_v, p_b_k, p_b_v, p_b_idx, p_c_cmp_k, p_c_cmp_v, p_c_sel_k, p_c_sel_v, p_c_win_k, p_c_win_v, p_d_k0, p_d_v0, p_d_k1, p_d_v1, p_d_k2, p_d_v2, s_a_k, s_a_v, s_b_k, s_b_v, s_b_idx, s_c_cmp_k, s_c_cmp_v, s_c_sel_k, s_c_sel_v, s_c_win_k, s_c_win_v, s_d_k0, s_d_v0, s_d_k1, s_d_v1, s_d_k2, s_d_v2)


_drawn_inputs = setup_inputs


def setup_inputs(seed=0):
    import zlib

    import numpy as np

    out = dict(_drawn_inputs(seed))
    spreads = {}
    factors = {}
    for name, (base, spread) in spreads.items():
        noise = np.random.default_rng([zlib.crc32(name.encode()), seed]).standard_normal(out[name].shape)
        drawn = base * np.exp(spread * noise) if base else spread * noise
        out[name] = __import__('jax').numpy.asarray(drawn.astype(out[name].dtype))
    for name, factor in factors.items():
        out[name] = (out[name] * factor).astype(out[name].dtype)
    return out
```

```python
import math
from contextlib import ExitStack

import numpy as np
import concourse.bass as bass
from concourse import mybir

F32 = mybir.dt.float32
I32 = mybir.dt.int32
ALU = mybir.AluOpType
ACT = mybir.ActivationFunctionType
AX = mybir.AxisListType

D = 1024
KT = D // 128
HD = 128
H = 4
NB = 8
L = 1024
PAGE = 128
ROWS = 8
SUB = PAGE // ROWS
NPG = L // PAGE
EPS = 1e-6
NEG = -1e30
BIG = 3e38
TOK = ((0, 128), (128, 128), (256, 8))
EVEN = dict(qa=0, ka=512, va=1024, ga=1536, qb=2048, kb=2560, vb=2688, gb=2816, qi=3328, ki=3584, wi=3648)
E_EVEN = 3652
ODD = dict(qc=0, kcr=512, vcr=640, ksel=768, vsel=896, kwin=1024, vwin=1152, gl=1280, gc=1292, gd=6412)
for _g in range(3):
    ODD[f"qd{_g}"], ODD[f"kd{_g}"], ODD[f"vd{_g}"] = (1804 + 1536 * _g + 512 * _j for _j in range(3))
E_ODD = 6924
PAIRS = ((128, 1), (512, 4), (2048, 16))
DW = tuple(min(w, L) for w, _ in PAIRS)
DN = tuple(w // d for w, (_, d) in zip(DW, PAIRS))
CB, CS, CH = 32, 16, 256
NC_S, NC_P = 63, 15
NSEL = 17
WIN = 512
TOPK_P, TOPK_S = 64, 256
LAM_INIT = 0.8 - 0.6 * math.exp(0.0)
GELU_C = math.sqrt(2.0 / math.pi)
SLOTS = 3
SLOT = 4096

CONST = {}


def _layout():
    at = 0
    for name, n in (("ident", 128), ("causal0", 128), ("causal1", 256), ("dil0", 384), ("dil1", 768),
                    ("cmp0", 15), ("cmp1", 15), ("cmpok", 2), ("rope", 144), ("ropec", 32), ("ropecp", 32),
                    ("e64", 64), ("e32", 32), ("hm64", 8), ("bm64", 8), ("hm32", 4), ("bm32", 8),
                    ("one8", 8), ("mzero", 1), ("mone", 1), ("overlap", 17), ("bonus", 17), ("sub", 1)):
        CONST[name] = (at, n)
        at += n
    return at


N_CONST = _layout()


def constants():
    c = np.zeros((128, N_CONST), np.float32)

    def put(name, a):
        at, n = CONST[name]
        c[:a.shape[0], at:at + n] = a

    def table(pos, half):
        freqs = np.float32(500000.0) ** (-np.arange(half, dtype=np.float32) / np.float32(half))
        ang = (pos.astype(np.float32)[:, None] * freqs.astype(np.float32)).astype(np.float32)
        return np.concatenate([np.cos(ang), np.sin(ang)], 1)

    p = np.arange(128)
    put("ident", np.eye(128))
    for t in range(2):
        q, k = p[:, None] + 128 * t, np.arange(128 * (t + 1))[None]
        put(f"causal{t}", np.where(k <= q, 0.0, NEG))
        put(f"dil{t}", np.concatenate(
            [np.where((k <= q) & ((q - k) % d == 0) & (q - k <= w), 0.0, NEG) for w, d in PAIRS], 1))
        put(f"cmp{t}", np.where(np.arange(NC_P)[None] * CS + CB - 1 <= q, 0.0, NEG))
    put("cmpok", np.stack([(p >= CB - 1), p >= 0], 1))
    put("rope", np.concatenate([np.concatenate([table(pos, 8), table(pos, 16)], 1)
                                for pos in (p, p + 128, np.full(128, L))], 1))
    put("ropec", table(np.arange(NC_S) * CS + CB - 1, 16))
    put("ropecp", table(np.arange(NC_P) * CS + CB - 1, 16))
    b = np.arange(NB)
    put("e64", b[:, None] == np.arange(64)[None] // 8)
    put("e32", b[:, None] == np.arange(32)[None] // 4)
    r = np.arange(64)
    put("hm64", r[:, None] % 8 == b[None])
    put("bm64", r[:, None] // 8 == b[None])
    put("mzero", (r[:, None] % 2 == 0))
    put("mone", (r[:, None] % 2 == 1))
    r = np.arange(32)
    put("hm32", r[:, None] % 4 == np.arange(4)[None])
    put("bm32", r[:, None] // 4 == b[None])
    put("one8", np.eye(8))
    cs, ss = np.arange(NC_S)[:, None] * CS, np.arange(NSEL)[None] * 64
    put("overlap", (cs < ss + 64) & (cs + CB > ss))
    j = np.arange(NSEL)
    put("bonus", np.broadcast_to(np.where((j == 0) | (j >= NSEL - 2), 1e4, 0.0), (8, NSEL)))
    put("sub", p[:, None] % SUB)
    return c


class Ring:

    def __init__(self, full, free, view, banks):
        self.full, self.free, self.view, self.banks = full, free, view, banks
        self.made = self.read = 0

    def claim(self, k=1):
        at = self.made % self.banks
        self.made += k
        self.filling = self.view[:, at * 512:(at + k) * 512]
        return max(0, self.made - self.banks)

    def arrive(self, k=1):
        at = self.read % self.banks
        self.read += k
        self.reading = self.view[:, at * 512:(at + k) * 512]
        return self.read


def ap(view, *dims, at=0):
    return bass.AP(view.tensor, view.offset + at, [list(view.ap[0])] + [list(d) for d in dims])


def build(nc, ins, outs):
    ctx = ExitStack()
    with ctx:
        def sb(name, shape, dt=F32):
            return ctx.enter_context(nc.sbuf_tensor(name, shape, dt))

        sems = {}

        def sem(name):
            if name not in sems:
                sems[name] = ctx.enter_context(nc.semaphore(name))
            return sems[name]

        const = sb("const", [128, N_CONST])

        def C(name, rows=128):
            at, n = CONST[name]
            return const[0:rows, at:at + n]

        ring = sb("ring", [128, SLOTS * SLOT])
        Z = sb("Z", [128, 3 * E_ODD])
        xT = sb("xT", [128, KT, 264])
        X = sb("X", [128, 3, D])
        NW = sb("NW", [128, D])
        PD = sb("PD", [128, 2048])
        QD = sb("QD", [128, NB, 32])
        QF = sb("QF", [128, 32])
        KN = sb("KN", [128, 8])
        QK = sb("QK", [128, 6, 512])
        flat = QK[:, :, :].rearrange("p a b -> p (a b)")
        SR = flat[0:64, 0:1040]
        SA = flat[:, 1040:1552]
        KTs = flat[:, 1552:2576].rearrange("p (a b) -> p a b", a=2)
        SM = sb("SM", [128, 2, 768])
        PT = sb("PT", [128, 768])
        BM = sb("BM", [128, 384])
        kcT = sb("kcT", [128, NB, 64])
        VC = sb("VC", [64, NB, HD])
        kcTp = sb("kcTp", [128, 16])
        VCp = sb("VCp", [16, HD])
        posT = sb("posT", [128, 64])
        W2 = sb("W2", [128, 2, 2, HD])
        bias1 = sb("bias1", [128, 2, 2])
        lamr = sb("lamr", [128, 256])
        lam = sb("lam", [128, 8])
        coef = sb("coef", [64, 2])
        stat = sb("stat", [128, 80])
        small = sb("small", [64, 64])
        PN = sb("PN", [64, 3, 8])
        PNT = sb("PNT", [8, 3, 64])
        RT = sb("RT", [128, 256])
        ptab = sb("ptab", [128, NB], I32)
        index = sb("index", [128, NB], I32)
        posr = RT[0:64, 0:128]

        psum = ctx.enter_context(nc.psum_tensor("psum", [128, 8 * 512], F32))
        T = Ring(sem("T_full"), sem("T_free"), psum[:, 0:1024], 2)
        S = Ring(sem("S_full"), sem("S_free"), psum[:, 1024:2048], 2)
        P = Ring(sem("P_full"), sem("P_free"), psum[:, 2048:3072], 2)
        O = Ring(sem("O_full"), sem("O_free"), psum[:, 3072:4096], 2)

        items, place, released = [], {}, {}

        def item(name, queue, parts):
            place[name] = (len(items) % SLOTS, None)
            items.append((name, queue, parts))

        def direct(src, rows, cols):
            return ("direct", src, rows, 0, cols)

        w_in = {0: ins["w_in_even"], 1: ins["w_in_odd"]}
        w_out = {0: ins["w_out_even"], 1: ins["w_out_odd"]}
        width = {0: E_EVEN, 1: E_ODD}

        def chunks(l):
            return [(c, min(512, width[l] - c)) for c in range(0, width[l], 512)]

        def weights(kind, l, w, cs):
            for c, n in cs:
                src = w[0].rearrange("(k p) n -> p k n", p=128)[:, :, c:c + n]
                item(f"{kind}{l}_{c}", "sp", [("w", src, n)])

        def gathered(name, cache, cols, per_slot):
            for s in range(0, NB, per_slot):
                item(f"{name}_{s // per_slot}", "pool",
                     [("gather", cache, b, (b - s) * ROWS * cols, ROWS * cols) for b in range(s, s + per_slot)])

        def w1(tag, kv):
            for half in range(2):
                src = ins["cmp_w1"][0, kv, half * 16:half * 16 + 16].rearrange("r d h -> d r h")
                item(f"{tag}{kv}_{half}", "sp", [("full", src)])

        for kv, cache in enumerate(("cache_c_cmp_k", "cache_c_cmp_v")):
            gathered(f"rows{kv}", ins[cache], HD, 4)
            w1("w1s", kv)
        weights("win", 0, w_in[0], chunks(0))
        gathered("idx", ins["cache_b_idx"], 64, 8)
        gathered("ak", ins["cache_a_k"], 512, 1)
        gathered("av", ins["cache_a_v"], 512, 1)
        gathered("bk", ins["cache_b_k"], HD, 4)
        gathered("bv", ins["cache_b_v"], HD, 4)
        weights("wout", 0, w_out[0], [(0, 512), (512, 512)])
        weights("win", 1, w_in[1], chunks(1))
        w1("w1p", 0)
        w1("w1p", 1)
        gathered("ck", ins["cache_c_sel_k"], HD, 4)
        gathered("cv", ins["cache_c_sel_v"], HD, 4)
        for n, w in (("wk", "state_c_win_k"), ("wv", "state_c_win_v")):
            item(n + "_0", "sp", [("full", ins[w][0].rearrange("b (p r) d -> p b (r d)", r=4))])
        for kv in "kv":
            for g, (_, d) in enumerate(PAIRS):
                src = ins[f"state_d_{kv}{g}"][0].rearrange("b (n j) h e -> n j b (h e)", j=d)[:, 0]
                item(f"d{kv}_{g}", "sp", [("rows", src, DN[g])])
        weights("wout", 1, w_out[1], [(0, 512), (512, 512)])
        order = {n: i for i, (n, _, _) in enumerate(items)}
        arrival, arrived = {}, {}
        for i, (n, queue, parts) in enumerate(items):
            s = f"slot_{'loaded' if queue == 'sp' else 'gathered'}{i % SLOTS}"
            arrived[s] = arrived.get(s, 0) + 16 * len(parts)
            arrival[n] = (sem(s), arrived[s])


        def slot_of(name):
            s = order[name] % SLOTS
            return ring[:, s * SLOT:(s + 1) * SLOT]

        level, seen, marks, latest = {}, {}, {}, [None, 0]

        def count(s, by=1):
            level[s.name] = level.get(s.name, 0) + by
            latest[:] = [s, level[s.name]]
            return level[s.name]

        def due(who, name, k=1):
            seen[who, name] = seen.get((who, name), 0) + k
            return seen[who, name]

        def mark(name, s, value):
            marks[name] = (s, value)


        def release(name, s, value):
            released[name] = (s, value)



        zt = {0: [Z[:, t * E_EVEN:(t + 1) * E_EVEN] for t in range(3)],
              1: [Z[:, t * E_ODD:(t + 1) * E_ODD] for t in range(3)]}
        R0 = 3 * E_EVEN
        rowsT = Z[:, R0:R0 + 8208]
        Y = [Z[:, R0 + t * D:R0 + (t + 1) * D] for t in range(3)]
        kc_rows = Z[:, 2048:3072]

        preps, units = {0: [], 1: []}, {0: [], 1: []}
        prep_n = [0]

        def prep(l, blocks, rows):
            n = prep_n[0]
            prep_n[0] += 1
            preps[l].append(dict(n=n, at=len(units[l]), blocks=blocks, rows=rows, slot=n % 6))
            return n % 6, n

        def unit(l, **u):
            u["deps"] = sorted(set(u["deps"]))
            units[l].append(u)

        sc = HD ** -0.5
        for h in range(H):
            s, n = prep(0, [(t, EVEN["qa"] + 128 * h, 128) for t in (0, 1)]
                        + [(t, EVEN["ka"] + 128 * h, 128) for t in (0, 1)], 128)
            for t in (0, 1):
                nk = 128 * (t + 1)
                unit(0, kind="a", t=t, h=h, nk=nk, maps=2, banks=2, scale=0.125, mask=C(f"causal{t}"),
                     scores=[(m * 512, QK[64 * m:64 * m + 64, s, t * 128:t * 128 + 128],
                              QK[64 * m:64 * m + 64, s, 256:256 + nk]) for m in (0, 1)],
                     deps=[n], pmaps=1, kt=t + 1, kw=128,
                     v=[[zt[0][k][:, EVEN["va"] + 128 * h:EVEN["va"] + 128 * h + 128] for k in range(t + 1)]])

        def pair_units(l, kind, q, k, v, mask, deps_k):
            ks, kn = deps_k
            for h in (0, 2):
                s, n = prep(l, [(t, q + 128 * (h + j), 128) for j in (0, 1) for t in (0, 1)], 128)
                for t in (0, 1):
                    nk = 128 * (t + 1)
                    unit(l, kind=kind, t=t, h=h, nk=nk, maps=2, banks=1, scale=sc, mask=mask[t],
                         scores=[(m * nk, QK[:, s, m * 256 + t * 128:m * 256 + t * 128 + 128],
                                  QK[:, ks, 0:nk]) for m in (0, 1)],
                         deps=[n, kn], pmaps=2, kt=t + 1, kw=128,
                         v=[[zt[l][kk][:, v:v + 128] for kk in range(t + 1)]] * 2)

        kb_dep = prep(0, [(t, EVEN["kb"], 128) for t in (0, 1)], 128)
        pair_units(0, "b", EVEN["qb"], EVEN["kb"], EVEN["vb"], [BM[:, 0:128], BM[:, 128:384]], kb_dep)
        cs = [prep(1, [(t, ODD["qc"] + 128 * (h + j), 128) for j in (0, 1) for t in (0, 1)], 128) for h in (0, 2)]
        for t in (0, 1):
            unit(1, kind="cmp", t=t, h=0, nk=NC_P, maps=4, banks=1, scale=sc, mask=C(f"cmp{t}"),
                 scores=[(h * NC_P, QK[:, cs[h // 2][0], (h % 2) * 256 + t * 128:(h % 2) * 256 + t * 128 + 128],
                          kcTp[:, 0:NC_P]) for h in range(H)],
                 deps=[cs[0][1], cs[1][1]], pmaps=4, kt=1, kw=NC_P, v=[[VCp[0:NC_P, :]]] * 4)
        mc = [C("causal0"), C("causal1")]
        for kind in ("sel", "win"):
            kd = prep(1, [(t, ODD["k" + kind], 128) for t in (0, 1)], 128)
            ks, kn = kd
            for h in (0, 2):
                s, n = cs[h // 2]
                for t in (0, 1):
                    nk = 128 * (t + 1)
                    unit(1, kind=kind, t=t, h=h, nk=nk, maps=2, banks=1, scale=sc, mask=mc[t],
                         scores=[(m * nk, QK[:, s, m * 256 + t * 128:m * 256 + t * 128 + 128],
                                  QK[:, ks, 0:nk]) for m in (0, 1)],
                         deps=[n, kn], pmaps=2, kt=t + 1, kw=128,
                         v=[[zt[1][kk][:, ODD["v" + kind]:ODD["v" + kind] + 128] for kk in range(t + 1)]] * 2)
        while prep_n[0] % 6:
            prep_n[0] += 1
        for h in range(H):
            s3 = [prep(1, [(t, ODD[f"qd{g}"] + 128 * h, 128) for t in (0, 1)]
                       + [(t, ODD[f"kd{g}"] + 128 * h, 128) for t in (0, 1)], 128) for g in range(3)]
            for t in (0, 1):
                nk = 128 * (t + 1)
                unit(1, kind="d", t=t, h=h, nk=3 * nk, maps=1, banks=2, scale=sc, mask=C(f"dil{t}"),
                     scores=[(g * nk, QK[:, s3[g][0], t * 128:t * 128 + 128], QK[:, s3[g][0], 256:256 + nk])
                             for g in range(3)],
                     deps=[n for _, n in s3], pmaps=1, kt=3 * (t + 1), kw=128,
                     v=[[zt[1][kk][:, ODD[f"vd{g}"] + 128 * h:ODD[f"vd{g}"] + 128 * h + 128]
                         for g in range(3) for kk in range(t + 1)]])

        FIRST_UNIT = {0: 0, 8: 8, 12: 0}

        def wait_slot(eng, i):
            if i >= SLOTS:
                eng.wait_ge(*released[items[i - SLOTS][0]])

        def stream(eng, i, name, parts):
            wait_slot(eng, i)
            slot = ring[:, (i % SLOTS) * SLOT:(i % SLOTS + 1) * SLOT]
            arrived = arrival[name][0]
            for part in parts:
                if part[0] == "w":
                    _, src, n = part
                    eng.dma_start(ap(slot[:, 0:1], [n, KT], [1, n]), src).then_inc(arrived, 16)
                elif part[0] == "full":
                    _, src = part
                    a, b = src.shape[1:]
                    eng.dma_start(ap(slot[:, 0:1], [b, a], [1, b]), src).then_inc(arrived, 16)
                elif part[0] == "rows":
                    _, src, n = part
                    eng.dma_start(ap(slot[0:n, 0:1], [512, NB], [1, 512]), src).then_inc(arrived, 16)
                else:
                    _, cache, b, at, n = part
                    rows = bass.AP(cache.tensor, cache.offset, [[n, cache.shape[1] * SUB], [1, n]])
                    nc.gpsimd.indirect_dma_start(out=slot[:, at:at + n], out_offset=None, in_=rows,
                                                 in_offset=bass.IndirectOffsetOnAxis(ap=index[:, b:b + 1], axis=0))\
                        .then_inc(arrived, 16)

        SMALL = [(const[:, :], ins["const"]),
                 (X[:, 0:2, :], ins["x_prompt"][0].rearrange("(t p) d -> p t d", p=128)),
                 (X[0:8, 2, :], ins["x_sample"].rearrange("b o d -> b (o d)")),
                 (W2[:, :, :, :].rearrange("p k h d -> p (k h) d"),
                  ins["cmp_w2"][0].rearrange("k (h p) d -> p (k h) d", p=128)),
                 (posr, ins["cmp_pos"][0].rearrange("k r d -> (k r) d")),
                 (lamr[:, :], bass.AP(ins["diff_lambda"].tensor, ins["diff_lambda"].offset, [[0, 128], [1, 256]]))]
        table = ins["page_table"]
        for pg in range(NPG):
            SMALL.append((ptab[pg * SUB:(pg + 1) * SUB, :],
                          bass.AP(table.tensor, table.offset + pg, [[0, SUB], [NPG, NB]])))
        N_SMALL = len(SMALL)

        OUTS = {0: [], 1: []}

        def state(l, name, c, n):
            o = outs["p_" + name]
            keep = o.shape[2]
            o2 = bass.AP(o.tensor, o.offset, [[n, keep], [1, n]])
            for t in range(2):
                if keep == 128 and t == 0:
                    continue
                at = t * 128 - (256 - keep)
                OUTS[l].append((o2[at:at + 128, :], zt[l][t][:, c:c + n]))
            o = outs["s_" + name]
            rows = o.shape[2]
            OUTS[l].append((bass.AP(o.tensor, o.offset + (rows - 1) * n, [[rows * n, NB], [1, n]]),
                            zt[l][2][0:8, c:c + n]))

        for name, c, n in (("a_k", "ka", 512), ("a_v", "va", 512), ("b_k", "kb", 128), ("b_v", "vb", 128),
                           ("b_idx", "ki", 64)):
            state(0, name, EVEN[c], n)
        for name, c in (("c_cmp_k", "kcr"), ("c_cmp_v", "vcr"), ("c_sel_k", "ksel"), ("c_sel_v", "vsel"),
                        ("c_win_k", "kwin"), ("c_win_v", "vwin")):
            state(1, name, ODD[c], 128)
        for g in range(3):
            state(1, f"d_k{g}", ODD[f"kd{g}"], 512)
            state(1, f"d_v{g}", ODD[f"vd{g}"], 512)
        OUTS0, OUTS1 = OUTS[0], OUTS[1]

        MOVES = []
        for name, n in [(f"d_{kv}{g}", 512) for g in range(3) for kv in "kv"] + [("c_win_k", 128), ("c_win_v", 128)]:
            src, dst = ins["state_" + name], outs["s_" + name]
            old, new = src.shape[2], dst.shape[2]
            kept = new - 1
            for b in range(NB):
                m = kept * n // 16
                MOVES.append((bass.AP(dst.tensor, dst.offset + b * new * n, [[m, 16], [1, m]]),
                              bass.AP(src.tensor, src.offset + (b * old + old - kept) * n, [[m, 16], [1, m]])))

        block = ctx.enter_context(nc.Block())

        @block.tensor
        def _(pe):
            mm = nc.tensor.matmul

            def tr(out, in_):
                n = in_.shape[0]
                return nc.tensor.transpose(out, in_, C("ident", n)[:, 0:n])

            def compress(kv, tag, source, n, base):
                pe.wait_ge(*arrival[f"{tag}{kv}_0"])
                a = slot_of(f"{tag}{kv}_0")
                pe.wait_ge(*arrival[f"{tag}{kv}_1"])
                b = slot_of(f"{tag}{kv}_1")
                for h in range(2):
                    pe.wait_ge(P.free, P.claim())
                    hp = P.filling
                    for r in range(CB):
                        w = (a if r < 16 else b)[:, (r % 16) * CH + h * 128:(r % 16) * CH + h * 128 + 128]
                        last = mm(hp[:, 0:n], w, ap(source[:, r:r + 1], [CS, n]), start=r == 0, stop=r == CB - 1)
                    last.then_inc(P.full, 1)
                if base:
                    pe.wait_ge(O.free, O.claim())
                    bp = O.filling
                    for h in range(2):
                        for r in range(CB):
                            w = (a if r < 16 else b)[:, (r % 16) * CH + h * 128:(r % 16) * CH + h * 128 + 128]
                            last = mm(bp[:, h:h + 1], w, posT[:, kv * CB + r:kv * CB + r + 1],
                                      start=r == 0, stop=r == CB - 1)
                    last.then_inc(O.full, 1)
                    release(f"{tag}{kv}_0", O.full, O.made)
                    release(f"{tag}{kv}_1", O.full, O.made)
                else:
                    release(f"{tag}{kv}_0", P.full, P.made)
                    release(f"{tag}{kv}_1", P.full, P.made)
                mark(f"hid{tag}{kv}", P.full, P.made)

            def second(kv, hid, step, nb, n):
                pe.wait_ge(sem("gelu"), due("pe", "gelu"))
                pe.wait_ge(S.free, S.claim(2))
                out = S.filling
                for b in range(nb):
                    for h in range(2):
                        last = mm(out[0:n, b * HD:(b + 1) * HD], hid[:, h * step + b * 64:h * step + b * 64 + n],
                                  W2[:, kv, h, :], start=h == 0, stop=h == 1)
                last.then_inc(S.full, 2)
                mark(f"second{kv}_{nb}", S.full, S.made)

            def to_xT(l, what, view_of):
                for t, (_, n) in enumerate(TOK):
                    pe.wait_ge(sem(what), due("pe", what))
                    for half in range(2):
                        pe.wait_ge(T.free, T.claim())
                        tp = T.filling
                        for j in range(4):
                            last = tr(tp[:, j * 128:j * 128 + n], view_of(t, half * 4 + j)[0:n])
                        last.then_inc(T.full, 1)
                    mark(f"{what}_read{l}_{t}", T.full, T.made)
                pe.wait_ge(T.free, T.made)

            def project(kind, l, cs):
                for c, n in cs:
                    pe.wait_ge(*arrival[f"{kind}{l}_{c}"])
                    w = slot_of(f"{kind}{l}_{c}")
                    for t0, m in TOK:
                        pe.wait_ge(P.free, P.claim())
                        out = P.filling
                        for k in range(KT):
                            last = mm(out[0:m, 0:n], xT[:, k, t0:t0 + m], w[:, k * n:(k + 1) * n],
                                      start=k == 0, stop=k == KT - 1)
                        last.then_inc(P.full, 1)
                    release(f"{kind}{l}_{c}", P.full, P.made)
                mark(f"{kind}{l}_done", P.full, P.made)

            evacuated = {}

            def do_prep(l, p):
                pe.wait_ge(T.free, T.claim())
                tp = T.filling
                for j, (t, c, w) in enumerate(p["blocks"]):
                    last = tr(tp[0:w, j * 128:(j + 1) * 128], zt[l][t][:, c:c + w])
                last.then_inc(T.full, 1)
                evacuated[p["n"]] = T.made

            def scores(u, n):
                for d in u["deps"]:
                    pe.wait_ge(T.free, evacuated[d])
                pe.wait_ge(S.free, S.claim(u["banks"]))
                out = S.filling
                for i, (c, q, k) in enumerate(u["scores"]):
                    w = k.shape[-1]
                    last = mm(out[:, c:c + w], q, k, start=True, stop=True)
                last.then_inc(S.full, u["banks"])
                mark(("s", n), S.free, S.made)
                for d in u["deps"]:
                    mark(("qk", d), S.full, S.made)

            def output(u, n):
                pe.wait_ge(sem("probs" if u["kind"] != "a" else "diffs"), due("pe", "probs" if u["kind"] != "a" else "diffs"))
                blocks = [(m, k) for m in range(u["pmaps"]) for k in range(u["kt"])]
                for i0 in range(0, len(blocks), 4):
                    pe.wait_ge(T.free, T.claim())
                    tp = T.filling
                    for j, (m, k) in enumerate(blocks[i0:i0 + 4]):
                        c = m * u["nk"] + k * u["kw"]
                        last = tr(tp[0:u["kw"], j * 128:(j + 1) * 128], SM[:, n % 2, c:c + u["kw"]])
                    last.then_inc(T.full, 1)
                mark(("p", n), T.full, T.made)
                pe.wait_ge(T.free, T.made)
                pe.wait_ge(O.free, O.claim())
                out = O.filling
                for m in range(u["pmaps"]):
                    for k in range(u["kt"]):
                        i = m * u["kt"] + k
                        last = mm(out[:, m * HD:(m + 1) * HD], PT[0:u["kw"], i * 128:(i + 1) * 128],
                                  u["v"][m][k], start=k == 0, stop=k == u["kt"] - 1)
                last.then_inc(O.full, 1)
                mark(("o", n), O.full, O.made)

            def attention(l, us, n0):
                for i in range(len(us) + 1):
                    for p in preps[l]:
                        if p["at"] == FIRST_UNIT[n0] + i and i < len(us):
                            do_prep(l, p)
                    if i < len(us):
                        scores(us[i], n0 + i)
                    if i:
                        output(us[i - 1], n0 + i - 1)

            def index_prompt():
                z = zt[0]
                for j in (0, 1):
                    pe.wait_ge(T.free, T.claim())
                    tp = T.filling
                    for i in range(4):
                        h, t = 2 * j + i // 2, i % 2
                        last = tr(tp[0:64, i * 128:(i + 1) * 128],
                                  z[t][:, EVEN["qi"] + 64 * h:EVEN["qi"] + 64 * h + 64])
                    last.then_inc(T.full, 1)
                pe.wait_ge(T.free, T.claim())
                tp = T.filling
                for t in (0, 1):
                    last = tr(tp[0:64, t * 128:(t + 1) * 128], z[t][:, EVEN["ki"]:EVEN["ki"] + 64])
                last.then_inc(T.full, 1)
                pe.wait_ge(T.free, T.made)
                for t in (0, 1):
                    nk = 128 * (t + 1)
                    for j in (0, 1):
                        pe.wait_ge(S.free, S.claim())
                        out = S.filling
                        for i in (0, 1):
                            last = mm(out[:, i * nk:(i + 1) * nk], QK[0:64, j, i * 256 + t * 128:i * 256 + t * 128 + 128],
                                      QK[0:64, 2, 0:nk], start=True, stop=True)
                        last.then_inc(S.full, 1)
                mark("index_prompt", S.full, S.made)

            def dec_query(z, q, w, k, wk):
                pe.wait_ge(T.free, T.claim())
                tp = T.filling
                for h in range(H):
                    last = tr(tp[0:w, h * 8:h * 8 + 8], z[0:8, q + w * h:q + w * h + w])
                if k is not None:
                    last = tr(tp[0:w, 32:40], z[0:8, k:k + wk])
                last.then_inc(T.full, 1)
                pe.wait_ge(T.free, T.made)

            def dec_own_key(w):
                pe.wait_ge(O.free, O.claim())
                out = O.filling
                mm(out[0:32, 0:8], QF[0:w, :], KN[0:w, :], start=True, stop=True).then_inc(O.full, 1)

            def dec_scores(name, per_slot, tiles, w, masked):
                pe.wait_ge(S.free, S.claim(2))
                out = S.filling
                if masked:
                    pe.wait_ge(sem("dec_mask"), due("pe", "dec_mask"))
                    for half in range(2):
                        mm(out[0:32, half * 512:(half + 1) * 512], C("e32", 8),
                           SR[0:8, half * 512:(half + 1) * 512], start=True, stop=False)
                jobs = [(b, half) for b in range(NB) for half in range(tiles // 4)]
                filled = [None] * len(jobs)
                for i in range(len(jobs) + 1):
                    if i < len(jobs):
                        b, half = jobs[i]
                        pe.wait_ge(*arrival[f"{name}_{b // per_slot}"])
                        slot = slot_of(f"{name}_{b // per_slot}")
                        pe.wait_ge(T.free, T.claim())
                        tp = T.filling
                        for j in range(4):
                            c = (b % per_slot) * tiles * w + (half * 4 + j) * w
                            last = tr(tp[0:w, j * 128:(j + 1) * 128], slot[:, c:c + w])
                        last.then_inc(T.full, 1)
                        filled[i] = T.made
                        if b % per_slot == per_slot - 1 and half == tiles // 4 - 1:
                            release(f"{name}_{b // per_slot}", T.full, T.made)
                    if i:
                        b, half = jobs[i - 1]
                        pe.wait_ge(T.free, filled[i - 1])
                        last = mm(out[0:32, half * 512:(half + 1) * 512], QD[0:w, b, :],
                                  KTs[0:w, (i - 1) % 2, :], start=b == 0 and not masked, stop=b == NB - 1)
                        if i < len(jobs):
                            last.then_inc(sem("keys_used"), 1)
                last.then_inc(S.full, 2)

            def dec_probs_T(rows, tiles):
                pe.wait_ge(sem("dec_probs"), due("pe", "dec_probs"))
                pe.wait_ge(T.free, T.claim())
                tp = T.filling
                for j, (c, n) in enumerate(tiles):
                    last = tr(tp[0:n, j * rows:(j + 1) * rows], SR[0:rows, c:c + n])
                last.then_inc(T.full, 1)

            def dec_new_T(rows, n):
                pe.wait_ge(T.free, T.claim())
                tp = T.filling
                for g in range(n):
                    last = tr(tp[0:8, g * rows:(g + 1) * rows], PN[0:rows, g, :])
                last.then_inc(T.full, 1)

            def spread(kind):
                pe.wait_ge(sem("dec_head"), due("pe", "dec_head"))
                pe.wait_ge(O.free, O.claim())
                out = O.filling
                mm(out[0:8, :], C("bm32", 32), SM[0:32, 0, 0:512], start=True, stop=True).then_inc(O.full, 1)

            def dec_values(name, per_slot, tiles, z, v):
                pe.wait_ge(sem("dec_pd"), due("pe", "dec_pd"))
                pe.wait_ge(O.free, O.claim())
                out = O.filling
                for b in range(NB):
                    pe.wait_ge(*arrival[f"{name}_{b // per_slot}"])
                    slot = slot_of(f"{name}_{b // per_slot}")
                    for r in range(tiles):
                        c = ((b % per_slot) * tiles + r) * HD
                        last = mm(out[0:32, 0:HD], PD[:, r * 256 + b * 32:r * 256 + b * 32 + 32],
                                  slot[:, c:c + HD], start=b == 0 and r == 0, stop=False)
                mm(out[0:32, 0:HD], PNT[0:8, 0, 0:32], z[0:8, v:v + HD], start=False, stop=True).then_inc(O.full, 1)
                for s in range(NB // per_slot):
                    release(f"{name}_{s}", O.full, O.made)
                spread(name)

            def dec_shared(z, name, per_slot, tiles, q, k, v, masked, new_query, vper):
                if new_query:
                    dec_query(z, q, HD, k, HD)
                else:
                    pe.wait_ge(T.free, T.claim())
                    tp = T.filling
                    tr(tp[0:HD, 0:8], z[0:8, k:k + HD]).then_inc(T.full, 1)
                    pe.wait_ge(T.free, T.made)
                dec_own_key(HD)
                dec_scores(name + "k", per_slot, tiles, HD, masked)
                dec_probs_T(32, [(r * 128, 128) for r in range(tiles)])
                dec_new_T(32, 1)
                dec_values(name + "v", vper, tiles, z, v)

            pe.wait_ge(sem("const_in"), 16 * N_SMALL)
            pe.wait_ge(T.free, T.claim())
            tp = T.filling
            tr(tp[:, 0:64], posr).then_inc(T.full, 1)
            for kv in range(2):
                for half in range(2):
                    pe.wait_ge(*arrival[f"rows{kv}_{half}"])
                    slot = slot_of(f"rows{kv}_{half}")
                    for i in range(8):
                        b, rq = i // 2, i % 2
                        pe.wait_ge(T.free, T.claim())
                        tp = T.filling
                        for j in range(4):
                            last = tr(tp[:, j * 128:(j + 1) * 128],
                                      slot[:, b * 1024 + (rq * 4 + j) * 128:b * 1024 + (rq * 4 + j) * 128 + 128])
                        last.then_inc(T.full, 1)
                    release(f"rows{kv}_{half}", T.full, T.made)
                pe.wait_ge(T.free, T.made)
                if kv == 0:
                    pe.wait_ge(sem("rows_tail"), due("pe", "rows_tail"))
                compress(kv, "w1s", rowsT, NB * 64, True)
                second(kv, Z[:, 0:1024], 512, NB, NC_S)
                if kv == 0:
                    pe.wait_ge(sem("kc_roped"), due("pe", "kc_roped"))
                    for half in range(2):
                        pe.wait_ge(T.free, T.claim())
                        tp = T.filling
                        for j in range(4):
                            b = half * 4 + j
                            last = tr(tp[:, j * 128:j * 128 + NC_S], kc_rows[0:NC_S, b * HD:(b + 1) * HD])
                        last.then_inc(T.full, 1)
                    pe.wait_ge(T.free, T.made)
                    mark("kc_read", T.full, T.made)

            for l in (0, 1):
                z, zs = zt[l], zt[l][2]
                to_xT(l, "xn", lambda t, k: PD[:, k * 128:(k + 1) * 128])
                project("win", l, chunks(l))
                pe.wait_ge(sem("roped"), due("pe", "roped"))
                if l == 0:
                    attention(0, units[0][0:8], 0)
                    index_prompt()
                    pe.wait_ge(sem("topk_prompt"), due("pe", "topk_prompt"))
                    attention(0, units[0][8:12], 8)
                    dec_query(zs, EVEN["qi"], 64, EVEN["ki"], 64)
                    dec_own_key(64)
                    pe.wait_ge(O.free, O.claim())
                    out = O.filling
                    mm(out[0:32, 0:4], C("e32", 8), zs[0:8, EVEN["wi"]:EVEN["wi"] + 4],
                       start=True, stop=True).then_inc(O.full, 1)
                    dec_scores("idx", 8, 8, 64, False)
                    pe.wait_ge(sem("relu_rows"), due("pe", "relu_rows"))
                    pe.wait_ge(S.free, S.claim(2))
                    out = S.filling
                    for half in range(2):
                        last = mm(out[0:8, half * 512:(half + 1) * 512], small[0:32, 16:24],
                                  SR[0:32, half * 512:(half + 1) * 512], start=True, stop=True)
                    last.then_inc(S.full, 2)
                    pe.wait_ge(O.free, O.claim())
                    out = O.filling
                    mm(out[0:8, 0:1], small[0:32, 16:24], SR[0:32, 1024:1025], start=True, stop=True)\
                        .then_inc(O.full, 1)
                    pe.wait_ge(O.free, O.claim())
                    out = O.filling
                    pe.wait_ge(sem("own_a"), due("pe", "own_a"))
                    mm(out[0:64, 0:8], C("e64", 8), small[0:8, 32:40], start=True, stop=True).then_inc(O.full, 1)
                    for b in range(NB):
                        pe.wait_ge(O.free, O.claim())
                        out = O.filling
                        mm(out[:, :], ap(C("one8", 8)[:, b:b + 1], [0, 128]), zs[0:8, 0:512],
                           start=True, stop=True).then_inc(O.full, 1)
                    pe.wait_ge(sem("scores_a"), due("pe", "scores_a"))
                    pe.wait_ge(S.free, S.claim(2))
                    out = S.filling
                    for r in range(ROWS):
                        last = tr(out[0:64, r * 128:(r + 1) * 128], SA[:, r * 64:(r + 1) * 64])
                    last.then_inc(S.full, 2)
                    dec_probs_T(64, [(r * 128, 128) for r in range(ROWS)])
                    dec_new_T(64, 1)
                    pe.wait_ge(sem("pd_pairs"), due("pe", "pd_pairs"))
                    pe.wait_ge(O.free, O.claim())
                    out = O.filling
                    for b in range(NB):
                        pe.wait_ge(*arrival[f"av_{b}"])
                        slot = slot_of(f"av_{b}")
                        for r in range(ROWS):
                            last = mm(out[0:32, :], PD[:, r * 256 + b * 32:r * 256 + b * 32 + 32],
                                      slot[:, r * 512:(r + 1) * 512], start=b == 0 and r == 0, stop=False)
                        last.then_inc(sem("av_used"), 1)
                        release(f"av_{b}", sem("av_used"), b + 1)
                    mm(out[0:32, :], PNT[0:8, 1, 0:32], zs[0:8, EVEN["va"]:EVEN["va"] + 512],
                       start=False, stop=True).then_inc(O.full, 1)
                    spread("a")
                    pe.wait_ge(O.free, O.claim())
                    out = O.filling
                    pe.wait_ge(sem("own_mask"), due("pe", "own_mask"))
                    mm(out[0:32, 0:1], C("e32", 8), small[0:8, 50:51], start=True, stop=True).then_inc(O.full, 1)
                    dec_shared(zs, "b", 4, 8, EVEN["qb"], EVEN["kb"], EVEN["vb"], True, True, 4)
                else:
                    pe.wait_ge(T.free, T.claim())
                    tp = T.filling
                    for j in range(4):
                        c = ODD["kcr"] if j < 2 else ODD["vcr"]
                        last = tr(tp[:, j * 128:(j + 1) * 128], z[j % 2][:, c:c + 128])
                    last.then_inc(T.full, 1)
                    pe.wait_ge(T.free, T.made)
                    for kv in range(2):
                        compress(kv, "w1p", QK[:, 5, kv * 256:kv * 256 + 256], NC_P, False)
                        second(kv, SM[:, 0, 0:128], 64, 1, NC_P)
                    pe.wait_ge(sem("kcp_roped"), due("pe", "kcp_roped"))
                    pe.wait_ge(T.free, T.claim())
                    tp = T.filling
                    tr(tp[:, 0:NC_P], SM[0:NC_P, 1, 0:128]).then_inc(T.full, 1)
                    mark("kcp_done", T.full, T.made)
                    pe.wait_ge(T.free, T.made)
                    attention(1, units[1], 12)
                    dec_query(zs, ODD["qc"], HD, None, 0)
                    pe.wait_ge(S.free, S.claim(2))
                    out = S.filling
                    for b in range(NB):
                        last = mm(out[0:32, 0:NC_S], QD[:, b, :], kcT[:, b, 0:NC_S], start=b == 0, stop=b == NB - 1)
                    last.then_inc(S.full, 2)
                    dec_probs_T(32, [(0, NC_S)])
                    pe.wait_ge(sem("imp_in"), due("pe", "imp_in"))
                    pe.wait_ge(O.free, O.claim())
                    out = O.filling
                    mm(out[0:8, 0:NSEL], small[0:NC_S, 24:32], C("overlap", NC_S), start=True, stop=True)\
                        .then_inc(O.full, 1)
                    pe.wait_ge(sem("dec_pd"), due("pe", "dec_pd"))
                    pe.wait_ge(O.free, O.claim())
                    out = O.filling
                    for b in range(NB):
                        last = mm(out[0:32, 0:HD], PD[0:NC_S, b * 32:b * 32 + 32], VC[0:NC_S, b, :],
                                  start=b == 0, stop=b == NB - 1)
                    last.then_inc(O.full, 1)
                    spread("cmp")
                    dec_shared(zs, "c", 4, 8, None, ODD["ksel"], ODD["vsel"], True, False, 4)
                    dec_shared(zs, "w", 8, 4, None, ODD["kwin"], ODD["vwin"], False, False, 8)
                    pe.wait_ge(O.free, O.claim())
                    out = O.filling
                    pe.wait_ge(sem("own_d"), due("pe", "own_d"))
                    mm(out[0:32, 0:12], C("e32", 8), small[0:8, 32:44], start=True, stop=True).then_inc(O.full, 1)
                    for g in range(3):
                        for b in range(NB):
                            pe.wait_ge(O.free, O.claim())
                            out = O.filling
                            mm(out[:, :], ap(C("one8", 8)[:, b:b + 1], [0, 128]),
                               zs[0:8, ODD[f"qd{g}"]:ODD[f"qd{g}"] + 512], start=True, stop=True).then_inc(O.full, 1)
                    pe.wait_ge(sem("scores_d"), due("pe", "scores_d"))
                    pe.wait_ge(S.free, S.claim(2))
                    out = S.filling
                    for g in range(3):
                        last = tr(out[0:32, g * 128:g * 128 + DN[g]], SA[0:DN[g], g * 32:(g + 1) * 32])
                    last.then_inc(S.full, 2)
                    dec_probs_T(32, [(g * 128, DN[g]) for g in range(3)])
                    dec_new_T(32, 3)
                    pe.wait_ge(sem("dec_pd"), due("pe", "dec_pd"))
                    pe.wait_ge(O.free, O.claim())
                    out = O.filling
                    for g in range(3):
                        pe.wait_ge(*arrival[f"dv_{g}"])
                        slot = slot_of(f"dv_{g}")
                        n = DN[g]
                        for b in range(NB):
                            mm(out[0:32, :], PD[0:n, g * 256 + b * 32:g * 256 + b * 32 + 32],
                               slot[0:n, b * 512:(b + 1) * 512], start=g == 0 and b == 0, stop=False)
                        last = mm(out[0:32, :], PNT[0:8, g, 0:32], zs[0:8, ODD[f"vd{g}"]:ODD[f"vd{g}"] + 512],
                                  start=False, stop=g == 2)
                        if g < 2:
                            last.then_inc(sem("dv_used"), 1)
                            release(f"dv_{g}", sem("dv_used"), g + 1)
                    last.then_inc(O.full, 1)
                    release("dv_2", O.full, O.made)
                    spread("d")
                gates = (EVEN["ga"], EVEN["gb"]) if l == 0 else (ODD["gc"], ODD["gd"])
                to_xT(l, "mix", lambda t, k: z[t][:, gates[k // 4] + (k % 4) * 128:gates[k // 4] + (k % 4) * 128 + 128])
                project("wout", l, [(0, 512), (512, 512)])

        @block.scalar
        def _(eng):
            act = nc.scalar.activation
            copy = nc.scalar.copy


            def hidden(kv, n, out, first, tag):
                if first:
                    eng.wait_ge(sem("bias1"), due("act", "bias1"))
                for h in range(2):
                    eng.wait_ge(P.full, P.arrive())
                    hp = P.reading
                    act(out[h], hp[:, 0:n], ACT.Identity, bias=bias1[:, kv, h:h + 1]).then_inc(P.free, 1)
                    eng.wait_ge(P.free, count(P.free))
                eng.sem_inc(sem("hid"), 1)
                count(sem("hid"))
                eng.wait_ge(sem("gelu_in"), due("act", "gelu_in"))

            def squares(t, n, src, junk):
                act(junk[0:n], src[0:n], ACT.Square, accum_out=stat[0:n, 60 + t:61 + t]).then_inc(sem("squares"), 1)
                eng.wait_ge(sem("squares"), count(sem("squares")))

            def norm(l, what, src, junk):
                for t, (_, n) in enumerate(TOK):
                    if what == "pre" and t == 0 and l == 0:
                        eng.wait_ge(sem("const_in"), 16 * N_SMALL)
                    squares(t, n, src(t), junk)
                eng.wait_ge(sem(f"{what}_ms"), due("act", f"{what}_ms"))
                for t, (_, n) in enumerate(TOK):
                    act(stat[0:n, 56 + t:57 + t], stat[0:n, 52 + t:53 + t], ACT.Sqrt).then_inc(sem("rms"), 1)
                    eng.wait_ge(sem("rms"), count(sem("rms")))

            def to_xT(l, what):
                for t, (t0, n) in enumerate(TOK):
                    for half in range(2):
                        eng.wait_ge(T.full, T.arrive())
                        tp = T.reading
                        if half == 0 and t == 0 and l is not None:
                            if what == "mix":
                                eng.wait_ge(*marks[f"win{l}_done"])
                            elif l == 1:
                                eng.wait_ge(*marks["wout0_done"])
                        copy(xT[:, half * 4:half * 4 + 4, t0:t0 + n], ap(tp[:, 0:1], [128, 4], [1, n]))\
                            .then_inc(T.free, 1)
                        eng.wait_ge(T.free, count(T.free))

            def project(outs_of, cs):
                for c, n in cs:
                    for t, (_, m) in enumerate(TOK):
                        eng.wait_ge(P.full, P.arrive())
                        pp = P.reading
                        copy(outs_of(t)[0:m, c:c + n], pp[0:m, 0:n]).then_inc(P.free, 1)
                        eng.wait_ge(P.free, count(P.free))

            def gates(l):
                cs = (EVEN["ga"], EVEN["gb"]) if l == 0 else (ODD["gc"], ODD["gd"])
                for t, (_, n) in enumerate(TOK):
                    for c in cs:
                        eng.wait_ge(sem("gate_next"), due("act", "gate_next"))
                        act(SM[0:n, 0, 0:512], zt[l][t][0:n, c:c + 512], ACT.Tanh, scale=0.5)\
                            .then_inc(sem("gate_tanh"), 1)
                        eng.wait_ge(sem("gate_tanh"), count(sem("gate_tanh")))
                    if l:
                        g = zt[l][t][0:n, ODD["gl"]:ODD["gl"] + 12]
                        act(g, g, ACT.Tanh, scale=0.5).then_inc(sem("gl_tanh"), 1)
                        eng.wait_ge(sem("gl_tanh"), count(sem("gl_tanh")))

            def do_prep(l, p):
                eng.wait_ge(T.full, T.arrive())
                tp = T.reading
                n = p["n"]
                if ("qk", n - 6) in marks:
                    eng.wait_ge(*marks[("qk", n - 6)])
                if n == 6:
                    eng.wait_ge(*marks["index_prompt"])
                w = 128 * len(p["blocks"])
                copy(QK[0:p["rows"], p["slot"], 0:w], tp[0:p["rows"], 0:w]).then_inc(T.free, 1)
                eng.wait_ge(T.free, count(T.free))

            def exps(u, n):
                eng.wait_ge(*marks[("s", n)])
                nk = u["nk"]
                for m in range(u["maps"]):
                    x = SM[:, n % 2, m * nk:(m + 1) * nk]
                    signal, by = (sem("exp_a" if u["kind"] == "a" else "probs"), 1) if m == u["maps"] - 1 else (sem("act_chain"), 1)
                    act(x, x, ACT.Exp, scale=-1.0, bias=stat[:, (n % 2) * 4 + m:(n % 2) * 4 + m + 1],
                        accum_out=stat[:, 64 + (n % 4) * 4 + m:65 + (n % 4) * 4 + m]).then_inc(signal, by)
                    eng.wait_ge(signal, count(signal, by))

            def probs_T(u, n):
                blocks = u["pmaps"] * u["kt"]
                for i0 in range(0, blocks, 4):
                    k = min(4, blocks - i0)
                    eng.wait_ge(T.full, T.arrive())
                    tp = T.reading
                    if i0 == 0 and n:
                        eng.wait_ge(*marks[("o", n - 1)])
                    copy(PT[0:u["kw"], i0 * 128:(i0 + k) * 128], tp[0:u["kw"], 0:k * 128]).then_inc(T.free, 1)
                    eng.wait_ge(T.free, count(T.free))

            def attention(l, us, n0):
                for i in range(len(us) + 1):
                    for p in preps[l]:
                        if p["at"] == FIRST_UNIT[n0] + i and i < len(us):
                            do_prep(l, p)
                    if i:
                        probs_T(us[i - 1], n0 + i - 1)
                    if i < len(us):
                        exps(us[i], n0 + i)

            def dec_query(w, with_key, dense=True):
                eng.wait_ge(T.full, T.arrive())
                tp = T.reading
                copy(ap(QD[0:w, 0, 0:1], [36, NB], [1, H]), ap(tp[0:w, 0:1], [1, NB], [8, H]))\
                    .then_inc(sem("act_chain"), 1)
                eng.wait_ge(sem("act_chain"), count(sem("act_chain")))
                signal, by = (sem("act_chain"), 1) if with_key else (T.free, 1)
                copy(ap(QF[0:w, 0:1], [4, NB], [1, H]), ap(tp[0:w, 0:1], [1, NB], [8, H])).then_inc(signal, by)
                eng.wait_ge(signal, count(signal, by))
                if with_key:
                    copy(KN[0:w, :], tp[0:w, 32:40]).then_inc(T.free, 1)
                    eng.wait_ge(T.free, count(T.free))

            def dec_scores(tiles, w):
                n = NB * tiles // 4
                base = seen.get(("act", "keys_used"), 0)
                for i in range(n):
                    eng.wait_ge(T.full, T.arrive())
                    tp = T.reading
                    if i >= 2:
                        eng.wait_ge(sem("keys_used"), base + i - 1)
                    copy(KTs[0:w, i % 2, :], tp[0:w, :]).then_inc(T.free, 1)
                    eng.wait_ge(T.free, count(T.free))
                seen["act", "keys_used"] = base + n - 1

            def dec_exp(rows, n):
                eng.wait_ge(sem("dec_scaled"), due("act", "dec_scaled"))
                act(SR[0:rows, 0:n], SR[0:rows, 0:n], ACT.Exp, scale=-1.0, bias=stat[0:rows, 20:21],
                    accum_out=stat[0:rows, 21:22]).then_inc(sem("dec_exp"), 1)
                eng.wait_ge(sem("dec_exp"), count(sem("dec_exp")))

            def dec_pd(tiles):
                eng.wait_ge(T.full, T.arrive())
                tp = T.reading
                eng.wait_ge(sem("pd_zero"), due("act", "pd_zero"))
                copy(ap(PD[:, 0:1], [256, tiles], [36, NB], [1, H]),
                     ap(tp[:, 0:1], [32, tiles], [4, NB], [1, H])).then_inc(T.free, 1)
                eng.wait_ge(T.free, count(T.free))

            def dec_new(rows, n, s):
                eng.wait_ge(T.full, T.arrive())
                tp = T.reading
                copy(PNT[:, 0:n, 0:rows], ap(tp[0:8, 0:1], [rows, n], [1, rows])).then_inc(T.free, 1)
                eng.wait_ge(T.free, count(T.free))
                eng.sem_inc(sem(s), 1)
                count(sem(s))

            def dec_shared(tiles, n, new_query):
                if new_query:
                    dec_query(HD, True)
                else:
                    eng.wait_ge(T.full, T.arrive())
                    tp = T.reading
                    copy(KN[:, :], tp[:, 0:8]).then_inc(T.free, 1)
                    eng.wait_ge(T.free, count(T.free))
                dec_scores(tiles, HD)
                dec_exp(32, n)
                dec_pd(tiles)
                dec_new(32, 1, "dec_pd")

            eng.wait_ge(sem("stat_zero"), due("act", "stat_zero"))
            eng.wait_ge(T.full, T.arrive())
            tp = T.reading
            copy(posT[:, :], tp[:, 0:64]).then_inc(T.free, 1)
            eng.wait_ge(T.free, count(T.free))
            for kv in range(2):
                for b in range(NB):
                    for rq in range(2):
                        eng.wait_ge(T.full, T.arrive())
                        tp = T.reading
                        if kv and b == 0 and rq == 0:
                            eng.wait_ge(*marks["hidw1s0"])
                        copy(ap(rowsT[:, b * 1024 + rq * 4:b * 1024 + rq * 4 + 1], [1, 4], [8, 128]),
                             ap(tp[:, 0:1], [128, 4], [1, 128])).then_inc(T.free, 1)
                        eng.wait_ge(T.free, count(T.free))
                if kv:
                    eng.wait_ge(sem("hid_free"), due("act", "hid_free"))
                hidden(kv, 512, [Z[:, 0:512], Z[:, 512:1024]], True, "w1s")
                act(Z[:, 1024:2048], Z[:, 1024:2048], ACT.Tanh, scale=GELU_C).then_inc(sem("gelu_tanh"), 1)
                eng.wait_ge(sem("gelu_tanh"), count(sem("gelu_tanh")))
                if kv == 0:
                    for half in range(2):
                        eng.wait_ge(T.full, T.arrive())
                        tp = T.reading
                        copy(kcT[:, half * 4:half * 4 + 4, 0:NC_S],
                             ap(tp[:, 0:1], [128, 4], [1, NC_S])).then_inc(T.free, 1)
                        eng.wait_ge(T.free, count(T.free))
            eng.wait_ge(sem("lam_in"), due("act", "lam_in"))
            act(lam[:, 2:4], lam[:, 0:2], ACT.Exp).then_inc(sem("lam_exp"), 1)
            eng.wait_ge(sem("lam_exp"), count(sem("lam_exp")))
            for l in (0, 1):
                z, zs = zt[l], zt[l][2]
                if l:
                    eng.wait_ge(sem("x_next"), due("act", "x_next"))
                norm(l, "pre", lambda t: X[:, t, :], PD[:, 1024:2048])
                to_xT(l, "xn")
                if l == 0:
                    eng.wait_ge(sem("comp_done"), due("act", "comp_done"))
                if l == 1:
                    eng.wait_ge(sem("out0"), 16 * len(OUTS0))
                    eng.wait_ge(sem("y_read"), due("act", "y_read"))
                project(lambda t: z[t], chunks(l))
                eng.sem_inc(sem("z_in"), 1)
                count(sem("z_in"))
                gates(l)
                if l == 0:
                    attention(0, units[0][0:8], 0)
                    for j in range(3):
                        eng.wait_ge(T.full, T.arrive())
                        tp = T.reading
                        w = 512 if j < 2 else 256
                        if j == 0:
                            eng.wait_ge(*marks[("qk", 2)])
                        copy(QK[0:64, j, 0:w], tp[0:64, 0:w]).then_inc(T.free, 1)
                        eng.wait_ge(T.free, count(T.free))
                    attention(0, units[0][8:12], 8)
                    dec_query(64, True)
                    dec_scores(8, 64)
                    dec_exp(64, 1025)
                    eng.wait_ge(T.full, T.arrive())
                    tp = T.reading
                    copy(SA[:, :], tp[:, :]).then_inc(T.free, 1)
                    eng.wait_ge(T.free, count(T.free))
                    dec_new(64, 1, "pair_in")
                    dec_shared(8, 1025, True)
                else:
                    eng.wait_ge(T.full, T.arrive())
                    tp = T.reading
                    copy(QK[:, 5, :], tp[:, :]).then_inc(T.free, 1)
                    eng.wait_ge(T.free, count(T.free))
                    for kv in range(2):
                        if kv:
                            eng.wait_ge(sem("hid_free"), due("act", "hid_free"))
                        hidden(kv, NC_P, [SM[:, 0, 0:NC_P], SM[:, 0, 64:64 + NC_P]], False, "w1p")
                        for h in range(2):
                            x = SM[:, 0, 128 + 64 * h:128 + 64 * h + NC_P]
                            signal, by = (sem("gelu_tanh"), 1) if h else (sem("act_chain"), 1)
                            act(x, x, ACT.Tanh, scale=GELU_C).then_inc(signal, by)
                            eng.wait_ge(signal, count(signal, by))
                    eng.wait_ge(T.full, T.arrive())
                    tp = T.reading
                    copy(kcTp[:, 0:NC_P], tp[:, 0:NC_P]).then_inc(T.free, 1)
                    eng.wait_ge(T.free, count(T.free))
                    attention(1, units[1], 12)
                    dec_query(HD, False)
                    dec_exp(32, NC_S)
                    eng.wait_ge(T.full, T.arrive())
                    tp = T.reading
                    eng.wait_ge(sem("pd_zero"), due("act", "pd_zero"))
                    copy(ap(PD[0:NC_S, 0:1], [36, NB], [1, H]), ap(tp[0:NC_S, 0:1], [4, NB], [1, H]))\
                        .then_inc(sem("act_chain"), 1)
                    eng.wait_ge(sem("act_chain"), count(sem("act_chain")))
                    copy(SA[0:NC_S, 0:32], tp[0:NC_S, 0:32]).then_inc(T.free, 1)
                    eng.wait_ge(T.free, count(T.free))
                    eng.sem_inc(sem("imp_T"), 1)
                    count(sem("imp_T"))
                    eng.sem_inc(sem("dec_pd"), 1)
                    count(sem("dec_pd"))
                    dec_shared(8, 1025, False)
                    dec_shared(4, 513, False)
                    dec_exp(32, 387)
                    eng.wait_ge(T.full, T.arrive())
                    tp = T.reading
                    eng.wait_ge(sem("pd_zero"), due("act", "pd_zero"))
                    for g in range(3):
                        n = DN[g]
                        signal, by = (T.free, 1) if g == 2 else (sem("act_chain"), 1)
                        copy(ap(PD[0:n, g * 256:g * 256 + 1], [36, NB], [1, H]),
                             ap(tp[0:n, g * 32:g * 32 + 1], [4, NB], [1, H])).then_inc(signal, by)
                        eng.wait_ge(signal, count(signal, by))
                    dec_new(32, 3, "dec_pd")
                if l == 0:
                    eng.wait_ge(sem("o_a"), due("act", "o_a"))
                    for t, (_, n) in enumerate(TOK):
                        act(stat[0:n, 44:48], stat[0:n, 24 + t * 4:28 + t * 4], ACT.Sqrt)\
                            .then_inc(sem("act_chain"), 1)
                        eng.wait_ge(sem("act_chain"), count(sem("act_chain")))
                        copy(stat[0:n, 24 + t * 4:28 + t * 4], stat[0:n, 44:48]).then_inc(sem("a_rms"), 1)
                        eng.wait_ge(sem("a_rms"), count(sem("a_rms")))
                to_xT(l, "mix")
                eng.wait_ge(sem("y_free"), due("act", "y_free"))
                if l == 1:
                    eng.wait_ge(sem("out0"), 16 * (len(OUTS0) + len(OUTS1)))
                project(lambda t: Y[t], [(0, 512), (512, 512)])
                norm(l, "post", lambda t: Y[t], PD[:, 1024:2048])

        @block.vector
        def _(eng):
            V = nc.vector
            tt, ts, stt = V.tensor_tensor, V.tensor_scalar, V.scalar_tensor_tensor
            mul, add, sub = ALU.mult, ALU.add, ALU.subtract


            def rope(x, heads, step, half, table):
                n = x.shape[0]
                both = ap(x, [step, heads], [half, 2], [1, half])
                lo, hi = ap(x, [step, heads], [1, half]), ap(x, [step, heads], [1, half], at=half)
                cos = ap(table[:, 0:1], [0, heads], [0, 2], [1, half])
                sin = ap(table[:, half:half + 1], [0, heads], [0, 2], [1, half])
                tmp = RT[0:n, 0:heads * 2 * half]
                w = 2 * half
                tt(ap(tmp, [w, heads], [half, 2], [1, half]), both, sin, mul).then_inc(sem("dve_chain"), 1)
                eng.wait_ge(sem("dve_chain"), count(sem("dve_chain")))
                tt(both, both, cos, mul).then_inc(sem("dve_chain"), 1)
                eng.wait_ge(sem("dve_chain"), count(sem("dve_chain")))
                tt(lo, lo, ap(RT[0:n, half:half + 1], [w, heads], [1, half]), sub).then_inc(sem("dve_chain"), 1)
                eng.wait_ge(sem("dve_chain"), count(sem("dve_chain")))
                tt(hi, hi, ap(RT[0:n, 0:1], [w, heads], [1, half]), add).then_inc(sem("dve_chain"), 1)
                eng.wait_ge(sem("dve_chain"), count(sem("dve_chain")))

            def gelu(hx, x2, both):
                eng.wait_ge(sem("hid"), due("dve", "hid"))
                for x, y in zip(hx, x2):
                    tt(y, x, x, mul).then_inc(sem("dve_chain"), 1)
                    eng.wait_ge(sem("dve_chain"), count(sem("dve_chain")))
                    ts(y, y, 0.044715, 1.0, mul, add).then_inc(sem("dve_chain"), 1)
                    eng.wait_ge(sem("dve_chain"), count(sem("dve_chain")))
                    tt(y, y, x, mul).then_inc(sem("dve_chain"), 1)
                    eng.wait_ge(sem("dve_chain"), count(sem("dve_chain")))
                eng.sem_inc(sem("gelu_in"), 1)
                count(sem("gelu_in"))
                eng.wait_ge(sem("gelu_tanh"), due("dve", "gelu_tanh"))
                for x, y in zip(hx, x2):
                    ts(y, y, 1.0, 0.5, add, mul).then_inc(sem("dve_chain"), 1)
                    eng.wait_ge(sem("dve_chain"), count(sem("dve_chain")))
                    tt(x, x, y, mul).then_inc(sem("dve_chain"), 1)
                    eng.wait_ge(sem("dve_chain"), count(sem("dve_chain")))
                eng.sem_inc(sem("gelu"), 1)
                count(sem("gelu"))

            def norm_pre(l):
                eng.wait_ge(sem("squares"), due("dve", "squares", 3))
                for t, (_, n) in enumerate(TOK):
                    ts(stat[0:n, 52 + t:53 + t], stat[0:n, 60 + t:61 + t], 1.0 / D, EPS, mul, add)\
                        .then_inc(sem("dve_chain"), 1)
                    eng.wait_ge(sem("dve_chain"), count(sem("dve_chain")))

            def norm(l, what, src, finish):
                norm_pre(l)
                eng.sem_inc(sem(f"{what}_ms"), 1)
                count(sem(f"{what}_ms"))
                eng.wait_ge(sem("rms"), due("dve", "rms", 3))
                eng.wait_ge(sem("nw_in"), 16 * (2 * l + (1 if what == "pre" else 2)))
                for t, (_, n) in enumerate(TOK):
                    V.reciprocal(stat[0:n, 52 + t:53 + t], stat[0:n, 56 + t:57 + t]).then_inc(sem("dve_chain"), 1)
                    eng.wait_ge(sem("dve_chain"), count(sem("dve_chain")))
                    finish(t, n)
                mark(f"nw_used{2 * l + (what != 'pre')}", *latest)

            def soft(u, n):
                eng.wait_ge(S.full, S.arrive(u["banks"]))
                s = S.reading
                if n >= 2:
                    eng.wait_ge(*marks[("p", n - 2)])
                nk = u["nk"]
                step = 512 if u["kind"] == "a" else nk
                for m in range(u["maps"]):
                    signal, by = (S.free, u["banks"]) if m == u["maps"] - 1 else (sem("dve_chain"), 1)
                    V.tensor_tensor_reduce(out=SM[:, n % 2, m * nk:(m + 1) * nk], in0=s[:, m * step:m * step + nk],
                                           in1=u["mask"], scale=-u["scale"], scalar=BIG, op0=add, op1=ALU.min,
                                           accum_out=stat[:, (n % 2) * 4 + m:(n % 2) * 4 + m + 1]).then_inc(signal, by)
                    eng.wait_ge(signal, count(signal, by))

            def combine(u, n):
                eng.wait_ge(sem("exp_a"), due("dve", "exp_a"))
                nk, x = u["nk"], SM[:, n % 2, :]
                den = stat[:, 64 + (n % 4) * 4:66 + (n % 4) * 4]
                V.reciprocal(stat[:, 16:18], den).then_inc(sem("dve_chain"), 1)
                eng.wait_ge(sem("dve_chain"), count(sem("dve_chain")))
                ts(stat[:, 17:18], stat[:, 17:18], lam[:, 5:6], None, mul).then_inc(sem("dve_chain"), 1)
                eng.wait_ge(sem("dve_chain"), count(sem("dve_chain")))
                ts(x[:, nk:2 * nk], x[:, nk:2 * nk], stat[:, 17:18], None, mul).then_inc(sem("dve_chain"), 1)
                eng.wait_ge(sem("dve_chain"), count(sem("dve_chain")))
                stt(x[:, 0:nk], x[:, 0:nk], stat[:, 16:17], x[:, nk:2 * nk], mul, add).then_inc(sem("diffs"), 1)
                eng.wait_ge(sem("diffs"), count(sem("diffs")))

            def finish(u, n, l):
                eng.wait_ge(O.full, O.arrive())
                o = O.reading
                t, h, kind, z = u["t"], u["h"], u["kind"], zt[l][u["t"]]
                k = u["pmaps"]
                den = stat[:, 64 + (n % 4) * 4:64 + (n % 4) * 4 + k]
                if kind == "a":
                    V.tensor_copy(z[:, EVEN["qa"] + 128 * h:EVEN["qa"] + 128 * h + 128], o[:, 0:128])\
                        .then_inc(O.free, 1)
                    eng.wait_ge(O.free, count(O.free))
                    return
                r = stat[:, 16:16 + k]
                V.reciprocal(r, den).then_inc(sem("dve_chain"), 1)
                eng.wait_ge(sem("dve_chain"), count(sem("dve_chain")))
                if kind in ("cmp", "sel", "win"):
                    j = ("cmp", "sel", "win").index(kind)
                    tt(r, r, ap(z[:, ODD["gl"] + 3 * h + j:ODD["gl"] + 3 * h + j + 1], [3, k]), mul)\
                        .then_inc(sem("dve_chain"), 1)
                    eng.wait_ge(sem("dve_chain"), count(sem("dve_chain")))
                if kind == "cmp":
                    ts(r, r, C("cmpok")[:, t:t + 1], None, mul).then_inc(sem("dve_chain"), 1)
                    eng.wait_ge(sem("dve_chain"), count(sem("dve_chain")))
                rb = ap(stat[:, 16:17], [1, k], [0, 128])
                ov = ap(o[:, 0:1], [128, k], [1, 128])
                if kind == "cmp":
                    acc = z[:, ODD["qc"]:ODD["qc"] + 512]
                    tt(ap(acc[:, 0:1], [128, 4], [1, 128]), ov, rb, mul).then_inc(O.free, 1)
                    eng.wait_ge(O.free, count(O.free))
                    return
                tt(ap(RT[:, 0:1], [128, k], [1, 128]), ov, rb, mul).then_inc(O.free, 1)
                eng.wait_ge(O.free, count(O.free))
                if kind in ("sel", "win"):
                    acc = z[:, ODD["qc"] + 128 * h:ODD["qc"] + 128 * h + 128 * k]
                    tt(acc, acc, RT[:, 0:128 * k], add).then_inc(sem("dve_chain"), 1)
                    eng.wait_ge(sem("dve_chain"), count(sem("dve_chain")))
                else:
                    c = (EVEN["gb"] if kind == "b" else ODD["gd"]) + 128 * h
                    g = z[:, c:c + 128 * k]
                    tt(g, g, RT[:, 0:128 * k], mul).then_inc(sem("dve_chain"), 1)
                    eng.wait_ge(sem("dve_chain"), count(sem("dve_chain")))

            def attention(l, us, n0):
                for i in range(len(us) + 2):
                    if i < len(us):
                        soft(us[i], n0 + i)
                    if 1 <= i <= len(us) and us[i - 1]["kind"] == "a":
                        combine(us[i - 1], n0 + i - 1)
                    if i >= 2:
                        finish(us[i - 2], n0 + i - 2, l)

            def topk(work, k, w8):
                for _ in range(0, k, 8):
                    V.max(w8, work).then_inc(sem("dve_chain"), 1)
                    eng.wait_ge(sem("dve_chain"), count(sem("dve_chain")))
                    V.match_replace(work, w8, work, -BIG).then_inc(sem("dve_chain"), 1)
                    eng.wait_ge(sem("dve_chain"), count(sem("dve_chain")))

            def dec_own(w, dst):
                eng.wait_ge(O.full, O.arrive())
                o = O.reading
                V.tensor_tensor_reduce(out=small[0:32, 0:8], in0=o[0:32, 0:8], in1=C("bm32", 32), scale=1.0,
                                       scalar=0.0, op0=mul, op1=add, accum_out=dst)\
                    .then_inc(O.free, 1)
                eng.wait_ge(O.free, count(O.free))

            def dec_soft(rows, src, n, scale, own):
                k, o = own
                m = n - k
                if src is not None:
                    ts(SR[0:rows, 0:m], src, -scale, None, mul).then_inc(S.free, 2)
                    eng.wait_ge(S.free, count(S.free, 2))
                if k:
                    ts(SR[0:rows, m:n], o, -scale, None, mul).then_inc(sem("dve_chain"), 1)
                    eng.wait_ge(sem("dve_chain"), count(sem("dve_chain")))
                V.tensor_reduce(stat[0:rows, 20:21], SR[0:rows, 0:n], AX.X, ALU.min).then_inc(sem("dec_scaled"), 1)
                eng.wait_ge(sem("dec_scaled"), count(sem("dec_scaled")))
                eng.wait_ge(sem("dec_exp"), due("dve", "dec_exp"))
                V.reciprocal(stat[0:rows, 22:23], stat[0:rows, 21:22]).then_inc(sem("dve_chain"), 1)
                eng.wait_ge(sem("dve_chain"), count(sem("dve_chain")))

            def dec_new(rows, cols, bm):
                for g, c in enumerate(cols):
                    ts(PN[0:rows, g, :], bm, SR[0:rows, c:c + 1], None, mul).then_inc(sem("dve_chain"), 1)
                    eng.wait_ge(sem("dve_chain"), count(sem("dve_chain")))

            def zero_pd():
                V.memset(PD[:, :], 0.0).then_inc(sem("pd_zero"), 1)
                eng.wait_ge(sem("pd_zero"), count(sem("pd_zero")))

            def head_rows(kind, wide):
                eng.wait_ge(O.full, O.arrive())
                o = O.reading
                src = ap(o[0:32, 0:1], [128 if wide else 0, H], [1, 128])
                hm = ap(C("hm32", 32)[:, 0:1], [1, H], [0, 128])
                tt(ap(SM[0:32, 0, 0:1], [128, H], [1, 128]), src, hm, mul).then_inc(O.free, 1)
                eng.wait_ge(O.free, count(O.free))
                eng.sem_inc(sem("dec_head"), 1)
                count(sem("dec_head"))

            def dec_finish(kind, z):
                eng.wait_ge(O.full, O.arrive())
                o = O.reading
                z = z[0:8]
                o = o[0:8, :]
                if kind == "a":
                    V.tensor_copy(z[:, 0:512], o).then_inc(O.free, 1)
                    eng.wait_ge(O.free, count(O.free))
                elif kind in ("cmp", "c", "w"):
                    j = ("cmp", "c", "w").index(kind)
                    g = ap(z[:, ODD["gl"] + j:ODD["gl"] + j + 1], [3, H], [0, 128])
                    acc = z[:, ODD["qc"]:ODD["qc"] + 512]
                    dst = acc if kind == "cmp" else SM[0:8, 0, 0:512]
                    tt(ap(dst[:, 0:1], [128, H], [1, 128]), ap(o[:, 0:1], [128, H], [1, 128]), g, mul)\
                        .then_inc(O.free, 1)
                    eng.wait_ge(O.free, count(O.free))
                    if kind != "cmp":
                        tt(acc, acc, dst, add).then_inc(sem("dve_chain"), 1)
                        eng.wait_ge(sem("dve_chain"), count(sem("dve_chain")))
                else:
                    c = EVEN["gb"] if kind == "b" else ODD["gd"]
                    tt(z[:, c:c + 512], z[:, c:c + 512], o, mul).then_inc(O.free, 1)
                    eng.wait_ge(O.free, count(O.free))

            def dec_shared(kind, z, tiles, masked):
                n = tiles * 128
                dec_own(HD, small[0:32, 8:9])
                if kind == "b":
                    tt(small[0:32, 8:9], small[0:32, 8:9], small[0:32, 51:52], add).then_inc(sem("dve_chain"), 1)
                    eng.wait_ge(sem("dve_chain"), count(sem("dve_chain")))
                eng.wait_ge(S.full, S.arrive(2))
                s = S.reading
                dec_soft(32, s[0:32, 0:n], n + 1, HD ** -0.5, (1, small[0:32, 8:9]))
                ts(SR[0:32, 0:n + 1], SR[0:32, 0:n + 1], stat[0:32, 22:23], None, mul).then_inc(sem("dve_chain"), 1)
                eng.wait_ge(sem("dve_chain"), count(sem("dve_chain")))
                dec_new(32, [n], C("bm32", 32))
                eng.sem_inc(sem("dec_probs"), 1)
                count(sem("dec_probs"))
                zero_pd()
                head_rows(kind, False)
                dec_finish(kind, z)

            eng.wait_ge(sem("const_in"), 16 * N_SMALL)
            ts(index[:, :], ptab[:, :], float(SUB), C("sub"), mul, add).then_inc(sem("index"), 1)
            eng.wait_ge(sem("index"), count(sem("index")))
            V.memset(rowsT[:, 8192:8208], 0.0).then_inc(sem("rows_tail"), 1)
            eng.wait_ge(sem("rows_tail"), count(sem("rows_tail")))
            V.memset(QD[:, :, :], 0.0).then_inc(sem("dve_chain"), 1)
            eng.wait_ge(sem("dve_chain"), count(sem("dve_chain")))
            V.memset(small[:, :], 0.0).then_inc(sem("dve_chain"), 1)
            eng.wait_ge(sem("dve_chain"), count(sem("dve_chain")))
            V.memset(stat[:, :], 0.0).then_inc(sem("stat_zero"), 1)
            eng.wait_ge(sem("stat_zero"), count(sem("stat_zero")))
            for j in range(2):
                V.tensor_tensor_reduce(out=RT[:, 128:192], in0=lamr[:, j * 128:j * 128 + 64],
                                       in1=lamr[:, j * 128 + 64:j * 128 + 128], scale=1.0, scalar=0.0,
                                       op0=mul, op1=add, accum_out=lam[:, j:j + 1])\
                    .then_inc(sem("dve_chain"), 1)
                eng.wait_ge(sem("dve_chain"), count(sem("dve_chain")))
            eng.sem_inc(sem("lam_in"), 1)
            count(sem("lam_in"))
            for kv in range(2):
                eng.wait_ge(O.full, O.arrive())
                b = O.reading
                V.tensor_copy(bias1[:, kv, :], b[:, 0:2]).then_inc(O.free, 1)
                eng.wait_ge(O.free, count(O.free))
                eng.sem_inc(sem("bias1"), 1)
                count(sem("bias1"))
                gelu([Z[:, 0:1024]], [Z[:, 1024:2048]], True)
                eng.wait_ge(S.full, S.arrive(2))
                s = S.reading
                if kv == 0:
                    V.tensor_copy(kc_rows[0:NC_S, :], s[0:NC_S, :]).then_inc(S.free, 2)
                    eng.wait_ge(S.free, count(S.free, 2))
                    eng.sem_inc(sem("hid_free"), 1)
                    count(sem("hid_free"))
                    rope(kc_rows[0:NC_S, 0:1], NB, HD, 16, C("ropec", NC_S))
                    eng.sem_inc(sem("kc_roped"), 1)
                    count(sem("kc_roped"))
                else:
                    V.tensor_copy(VC[0:NC_S, :, :], ap(s[0:NC_S, 0:1], [HD, NB], [1, HD])).then_inc(S.free, 2)
                    eng.wait_ge(S.free, count(S.free, 2))
            eng.wait_ge(*marks["kc_read"])
            eng.sem_inc(sem("comp_done"), 1)
            count(sem("comp_done"))
            eng.wait_ge(sem("lam_exp"), due("dve", "lam_exp"))
            tt(lam[:, 4:5], lam[:, 2:3], lam[:, 3:4], sub).then_inc(sem("dve_chain"), 1)
            eng.wait_ge(sem("dve_chain"), count(sem("dve_chain")))
            ts(lam[:, 5:6], lam[:, 4:5], LAM_INIT, -1.0, add, mul).then_inc(sem("dve_chain"), 1)
            eng.wait_ge(sem("dve_chain"), count(sem("dve_chain")))
            ts(coef[:, 0:1], C("mone", 64), lam[0:64, 5:6], None, mul).then_inc(sem("dve_chain"), 1)
            eng.wait_ge(sem("dve_chain"), count(sem("dve_chain")))
            tt(coef[:, 1:2], coef[:, 0:1], C("mzero", 64), add).then_inc(sem("dve_chain"), 1)
            eng.wait_ge(sem("dve_chain"), count(sem("dve_chain")))

            for l in (0, 1):
                z, zs = zt[l], zt[l][2]

                def xn(t, n):
                    if t:
                        eng.wait_ge(*marks[f"xn_read{l}_{t - 1}"])
                    stt(PD[0:n, 0:1024], X[0:n, t, :], stat[0:n, 52 + t:53 + t], NW[0:n, :], mul, mul)\
                        .then_inc(sem("xn"), 1)
                    eng.wait_ge(sem("xn"), count(sem("xn")))
                norm(l, "pre", None, xn)
                eng.wait_ge(sem("z_in"), due("dve", "z_in"))
                cs = (EVEN["ga"], EVEN["gb"]) if l == 0 else (ODD["gc"], ODD["gd"])
                for t, (_, n) in enumerate(TOK):
                    for c in cs:
                        eng.sem_inc(sem("gate_next"), 1)
                        count(sem("gate_next"))
                        eng.wait_ge(sem("gate_tanh"), due("dve", "gate_tanh"))
                        g = z[t][0:n, c:c + 512]
                        ts(SM[0:n, 0, 0:512], SM[0:n, 0, 0:512], 1.0, 0.5, add, mul).then_inc(sem("dve_chain"), 1)
                        eng.wait_ge(sem("dve_chain"), count(sem("dve_chain")))
                        tt(g, g, SM[0:n, 0, 0:512], mul).then_inc(sem("dve_chain"), 1)
                        eng.wait_ge(sem("dve_chain"), count(sem("dve_chain")))
                    if l:
                        eng.wait_ge(sem("gl_tanh"), due("dve", "gl_tanh"))
                        g = z[t][0:n, ODD["gl"]:ODD["gl"] + 12]
                        ts(g, g, 1.0, 0.5, add, mul).then_inc(sem("dve_chain"), 1)
                        eng.wait_ge(sem("dve_chain"), count(sem("dve_chain")))
                    tab = C("rope", n)[:, 48 * t:48 * t + 48]
                    t8, t16 = tab[:, 0:16], tab[:, 16:48]
                    if l == 0:
                        rope(z[t][0:n, EVEN["qa"]:EVEN["qa"] + 1], 16, 64, 8, t8)
                        rope(z[t][0:n, EVEN["qb"]:EVEN["qb"] + 1], 5, 128, 16, t16)
                        rope(z[t][0:n, EVEN["qi"]:EVEN["qi"] + 1], 5, 64, 8, t8)
                    else:
                        rope(z[t][0:n, ODD["qc"]:ODD["qc"] + 1], 4, 128, 16, t16)
                        rope(z[t][0:n, ODD["ksel"]:ODD["ksel"] + 1], 2, 256, 16, t16)
                        for g in range(3):
                            rope(z[t][0:n, ODD[f"qd{g}"]:ODD[f"qd{g}"] + 1], 8, 128, 16, t16)
                eng.sem_inc(sem("roped"), 1)
                count(sem("roped"))
                mark(f"roped{l}", *latest)
                if l == 0:
                    attention(0, units[0][0:8], 0)
                    for t in (0, 1):
                        nk = 128 * (t + 1)
                        acc = SM[:, 0, 0:nk]
                        for j in (0, 1):
                            eng.wait_ge(S.full, S.arrive())
                            s = S.reading
                            for i in (0, 1):
                                w = z[t][:, EVEN["wi"] + 2 * j + i:EVEN["wi"] + 2 * j + i + 1]
                                dst = acc if j + i == 0 else SM[:, 0, 256:256 + nk]
                                signal, by = (S.free, 1) if i else (sem("dve_chain"), 1)
                                ts(dst, s[:, i * nk:(i + 1) * nk], 0.0, w, ALU.max, mul).then_inc(signal, by)
                                eng.wait_ge(signal, count(signal, by))
                                if j + i:
                                    tt(acc, acc, dst, add).then_inc(sem("dve_chain"), 1)
                                    eng.wait_ge(sem("dve_chain"), count(sem("dve_chain")))
                        tt(acc, acc, C(f"causal{t}"), add).then_inc(sem("dve_chain"), 1)
                        eng.wait_ge(sem("dve_chain"), count(sem("dve_chain")))
                        topk(acc, TOPK_P, stat[:, 32:40])
                        bm = BM[:, 0:128] if t == 0 else BM[:, 128:384]
                        ts(bm, acc, -2e38, NEG, ALU.is_gt, mul).then_inc(sem("dve_chain"), 1)
                        eng.wait_ge(sem("dve_chain"), count(sem("dve_chain")))
                        tt(bm, bm, C(f"causal{t}"), add).then_inc(sem("dve_chain"), 1)
                        eng.wait_ge(sem("dve_chain"), count(sem("dve_chain")))
                    eng.sem_inc(sem("topk_prompt"), 1)
                    count(sem("topk_prompt"))
                    attention(0, units[0][8:12], 8)
                    dec_own(64, small[0:32, 9:10])
                    eng.wait_ge(O.full, O.arrive())
                    o = O.reading
                    V.tensor_tensor_reduce(out=small[0:32, 0:4], in0=o[0:32, 0:4], in1=C("hm32", 32), scale=1.0,
                                           scalar=0.0, op0=mul, op1=add, accum_out=small[0:32, 10:11])\
                        .then_inc(O.free, 1)
                    eng.wait_ge(O.free, count(O.free))
                    ts(small[0:32, 16:24], C("bm32", 32), small[0:32, 10:11], None, mul).then_inc(sem("dve_chain"), 1)
                    eng.wait_ge(sem("dve_chain"), count(sem("dve_chain")))
                    eng.wait_ge(S.full, S.arrive(2))
                    s = S.reading
                    ts(ap(SR[0:32, 0:1], [1, ROWS], [ROWS, 128]), ap(s[0:32, 0:1], [128, ROWS], [1, 128]),
                       0.0, None, ALU.max).then_inc(S.free, 2)
                    eng.wait_ge(S.free, count(S.free, 2))
                    ts(SR[0:32, 1024:1025], small[0:32, 9:10], 0.0, None, ALU.max).then_inc(sem("relu_rows"), 1)
                    eng.wait_ge(sem("relu_rows"), count(sem("relu_rows")))
                    eng.wait_ge(S.full, S.arrive(2))
                    s = S.reading
                    work = PD[0:8, 0:1025]
                    V.tensor_copy(work[:, 0:1024], s[0:8, :]).then_inc(S.free, 2)
                    eng.wait_ge(S.free, count(S.free, 2))
                    eng.wait_ge(O.full, O.arrive())
                    o = O.reading
                    V.tensor_copy(work[:, 1024:1025], o[0:8, 0:1]).then_inc(O.free, 1)
                    eng.wait_ge(O.free, count(O.free))
                    topk(work, TOPK_S, stat[0:8, 32:40])
                    kept = Y[2][0:8, 0:1024]
                    ts(ap(kept[:, 0:1], [128, ROWS], [1, 128]), ap(work[:, 0:1], [1, ROWS], [ROWS, 128]),
                       -2e38, NEG, ALU.is_gt, mul).then_inc(sem("dve_chain"), 1)
                    eng.wait_ge(sem("dve_chain"), count(sem("dve_chain")))
                    ts(small[0:8, 50:51], work[:, 1024:1025], -2e38, NEG, ALU.is_gt, mul)\
                        .then_inc(sem("dve_chain"), 1)
                    eng.wait_ge(sem("dve_chain"), count(sem("dve_chain")))
                    tt(SM[0:8, 0, 0:512], zs[0:8, 0:512], zs[0:8, 512:1024], mul).then_inc(sem("dve_chain"), 1)
                    eng.wait_ge(sem("dve_chain"), count(sem("dve_chain")))
                    V.tensor_reduce(small[0:8, 32:40], ap(SM[0:8, 0, 0:1], [64, 8], [1, 64]), AX.X, add)\
                        .then_inc(sem("own_a"), 1)
                    eng.wait_ge(sem("own_a"), count(sem("own_a")))
                    eng.wait_ge(O.full, O.arrive())
                    o = O.reading
                    V.tensor_tensor_reduce(out=small[0:64, 0:8], in0=o[0:64, 0:8], in1=C("hm64", 64), scale=1.0,
                                           scalar=0.0, op0=mul, op1=add, accum_out=small[0:64, 11:12])\
                        .then_inc(O.free, 1)
                    eng.wait_ge(O.free, count(O.free))
                    for b in range(NB):
                        eng.wait_ge(*arrival[f"ak_{b}"])
                        slot = slot_of(f"ak_{b}")
                        eng.wait_ge(O.full, O.arrive())
                        o = O.reading
                        kv3 = ap(slot[:, 0:1], [512, ROWS], [1, 512])
                        tt(kv3, kv3, ap(o[:, 0:1], [0, ROWS], [1, 512]), mul).then_inc(O.free, 1)
                        eng.wait_ge(O.free, count(O.free))
                        V.tensor_reduce(ap(SA[:, b * 8:b * 8 + 1], [64, ROWS], [1, 8]),
                                        ap(slot[:, 0:1], [512, ROWS], [64, 8], [1, 64]), AX.X, add)\
                            .then_inc(sem("dve_chain"), 1)
                        eng.wait_ge(sem("dve_chain"), count(sem("dve_chain")))
                        release(f"ak_{b}", *latest)
                    eng.sem_inc(sem("scores_a"), 1)
                    count(sem("scores_a"))
                    eng.wait_ge(S.full, S.arrive(2))
                    s = S.reading
                    dec_soft(64, s[0:64, :], 1025, 0.125, (1, small[0:64, 11:12]))
                    tt(stat[0:64, 22:23], stat[0:64, 22:23], coef[:, 1:2], mul).then_inc(sem("dve_chain"), 1)
                    eng.wait_ge(sem("dve_chain"), count(sem("dve_chain")))
                    ts(SR[0:64, 0:1025], SR[0:64, 0:1025], stat[0:64, 22:23], None, mul).then_inc(sem("dve_chain"), 1)
                    eng.wait_ge(sem("dve_chain"), count(sem("dve_chain")))
                    dec_new(64, [1024], C("bm64", 64))
                    eng.sem_inc(sem("dec_probs"), 1)
                    count(sem("dec_probs"))
                    V.memset(PD[:, :], 0.0).then_inc(sem("dve_chain"), 1)
                    eng.wait_ge(sem("dve_chain"), count(sem("dve_chain")))
                    eng.wait_ge(sem("pair_in"), due("dve", "pair_in"))
                    tt(ap(PD[:, 0:1], [256, ROWS], [36, NB], [1, H]),
                       ap(SA[:, 0:1], [64, ROWS], [8, NB], [2, H]),
                       ap(SA[:, 1:2], [64, ROWS], [8, NB], [2, H]), add)\
                        .then_inc(sem("dve_chain"), 1)
                    eng.wait_ge(sem("dve_chain"), count(sem("dve_chain")))
                    tt(PNT[:, 1, 0:32], ap(PNT[:, 0, 0:1], [2, 32]), ap(PNT[:, 0, 1:2], [2, 32]), add)\
                        .then_inc(sem("pd_pairs"), 1)
                    eng.wait_ge(sem("pd_pairs"), count(sem("pd_pairs")))
                    head_rows("a", True)
                    dec_finish("a", zs)
                    eng.sem_inc(sem("own_mask"), 1)
                    count(sem("own_mask"))
                    eng.wait_ge(O.full, O.arrive())
                    o = O.reading
                    V.tensor_copy(small[0:32, 51:52], o[0:32, 0:1]).then_inc(O.free, 1)
                    eng.wait_ge(O.free, count(O.free))
                    V.tensor_copy(SR[0:8, 0:1024], kept).then_inc(sem("dec_mask"), 1)
                    eng.wait_ge(sem("dec_mask"), count(sem("dec_mask")))
                    dec_shared("b", zs, 8, True)
                    for t, (_, n) in enumerate(TOK):
                        o = z[t][0:n, 0:512]
                        tt(SM[0:n, 0, 0:512], o, o, mul).then_inc(sem("dve_chain"), 1)
                        eng.wait_ge(sem("dve_chain"), count(sem("dve_chain")))
                        V.tensor_reduce(stat[0:n, 24 + 4 * t:28 + 4 * t], ap(SM[0:n, 0, 0:1], [128, H], [1, 128]),
                                        AX.X, add).then_inc(sem("dve_chain"), 1)
                        eng.wait_ge(sem("dve_chain"), count(sem("dve_chain")))
                        ts(stat[0:n, 24 + 4 * t:28 + 4 * t], stat[0:n, 24 + 4 * t:28 + 4 * t], 1.0 / HD, EPS,
                           mul, add).then_inc(sem("dve_chain"), 1)
                        eng.wait_ge(sem("dve_chain"), count(sem("dve_chain")))
                    eng.sem_inc(sem("o_a"), 1)
                    count(sem("o_a"))
                    eng.wait_ge(sem("a_rms"), due("dve", "a_rms", 3))
                    for t, (_, n) in enumerate(TOK):
                        r = stat[0:n, 24 + 4 * t:28 + 4 * t]
                        V.reciprocal(r, r).then_inc(sem("dve_chain"), 1)
                        eng.wait_ge(sem("dve_chain"), count(sem("dve_chain")))
                        ts(r, r, 1.0 - LAM_INIT, None, mul).then_inc(sem("dve_chain"), 1)
                        eng.wait_ge(sem("dve_chain"), count(sem("dve_chain")))
                        o = ap(z[t][0:n, 0:1], [128, H], [1, 128])
                        tt(o, o, ap(r[:, 0:1], [1, H], [0, 128]), mul).then_inc(sem("dve_chain"), 1)
                        eng.wait_ge(sem("dve_chain"), count(sem("dve_chain")))
                        g = z[t][0:n, EVEN["ga"]:EVEN["ga"] + 512]
                        tt(g, g, z[t][0:n, 0:512], mul).then_inc(sem("dve_chain"), 1)
                        eng.wait_ge(sem("dve_chain"), count(sem("dve_chain")))
                else:
                    hx = [SM[:, 0, 0:NC_P], SM[:, 0, 64:64 + NC_P]]
                    x2 = [SM[:, 0, 128:128 + NC_P], SM[:, 0, 192:192 + NC_P]]
                    for kv in range(2):
                        gelu(hx, x2, False)
                        eng.wait_ge(S.full, S.arrive(2))
                        s = S.reading
                        if kv == 0:
                            V.tensor_copy(SM[0:NC_P, 1, 0:128], s[0:NC_P, 0:128]).then_inc(S.free, 2)
                            eng.wait_ge(S.free, count(S.free, 2))
                            eng.sem_inc(sem("hid_free"), 1)
                            count(sem("hid_free"))
                            rope(SM[0:NC_P, 1, 0:1], 1, HD, 16, C("ropecp", NC_P))
                        else:
                            V.tensor_copy(VCp[0:NC_P, :], s[0:NC_P, 0:128]).then_inc(S.free, 2)
                            eng.wait_ge(S.free, count(S.free, 2))
                    eng.sem_inc(sem("kcp_roped"), 1)
                    count(sem("kcp_roped"))
                    eng.wait_ge(*marks["kcp_done"])
                    attention(1, units[1], 12)
                    eng.wait_ge(S.full, S.arrive(2))
                    s = S.reading
                    dec_soft(32, s[0:32, 0:NC_S], NC_S, HD ** -0.5, (0, None))
                    ts(SR[0:32, 0:NC_S], SR[0:32, 0:NC_S], stat[0:32, 22:23], None, mul).then_inc(sem("dec_probs"), 1)
                    eng.wait_ge(sem("dec_probs"), count(sem("dec_probs")))
                    zero_pd()
                    eng.wait_ge(sem("imp_T"), due("dve", "imp_T"))
                    V.tensor_reduce(small[0:NC_S, 24:32], ap(SA[0:NC_S, 0:1], [4, NB], [1, H]), AX.X, add)\
                        .then_inc(sem("imp_in"), 1)
                    eng.wait_ge(sem("imp_in"), count(sem("imp_in")))
                    eng.wait_ge(O.full, O.arrive())
                    o = O.reading
                    imp = RT[0:8, 0:NSEL]
                    tt(imp, o[0:8, 0:NSEL], C("bonus", 8), add).then_inc(O.free, 1)
                    eng.wait_ge(O.free, count(O.free))
                    topk(imp, 16, stat[0:8, 32:40])
                    ts(imp, imp, -2e38, NEG, ALU.is_gt, mul).then_inc(sem("dve_chain"), 1)
                    eng.wait_ge(sem("dve_chain"), count(sem("dve_chain")))
                    kept = SR[0:8, 0:1024]
                    V.tensor_copy(ap(kept[:, 0:1], [128, ROWS], [8, 16], [1, 8]),
                                  ap(imp[:, 0:1], [0, ROWS], [1, 16], [0, 8]))\
                        .then_inc(sem("dve_chain"), 1)
                    eng.wait_ge(sem("dve_chain"), count(sem("dve_chain")))
                    head_rows("cmp", False)
                    dec_finish("cmp", zs)
                    eng.sem_inc(sem("dec_mask"), 1)
                    count(sem("dec_mask"))
                    dec_shared("c", zs, 8, True)
                    dec_shared("w", zs, 4, False)
                    for g in range(3):
                        q, k = ODD[f"qd{g}"], ODD[f"kd{g}"]
                        tt(SM[0:8, 0, 0:512], zs[0:8, q:q + 512], zs[0:8, k:k + 512], mul)\
                            .then_inc(sem("dve_chain"), 1)
                        eng.wait_ge(sem("dve_chain"), count(sem("dve_chain")))
                        V.tensor_reduce(small[0:8, 32 + 4 * g:36 + 4 * g],
                                        ap(SM[0:8, 0, 0:1], [128, H], [1, 128]), AX.X, add)\
                            .then_inc(sem("dve_chain"), 1)
                        eng.wait_ge(sem("dve_chain"), count(sem("dve_chain")))
                    eng.sem_inc(sem("own_d"), 1)
                    count(sem("own_d"))
                    eng.wait_ge(O.full, O.arrive())
                    o = O.reading
                    tt(ap(small[0:32, 0:1], [4, 3], [1, H]), ap(o[0:32, 0:1], [4, 3], [1, H]),
                       ap(C("hm32", 32)[:, 0:1], [0, 3], [1, H]), mul).then_inc(O.free, 1)
                    eng.wait_ge(O.free, count(O.free))
                    V.tensor_reduce(small[0:32, 12:15], ap(small[0:32, 0:1], [4, 3], [1, H]), AX.X, add)\
                        .then_inc(sem("dve_chain"), 1)
                    eng.wait_ge(sem("dve_chain"), count(sem("dve_chain")))
                    for g in range(3):
                        eng.wait_ge(*arrival[f"dk_{g}"])
                        slot = slot_of(f"dk_{g}")
                        n = DN[g]
                        for b in range(NB):
                            eng.wait_ge(O.full, O.arrive())
                            o = O.reading
                            k = slot[0:n, b * 512:(b + 1) * 512]
                            tt(k, k, o[0:n, :], mul).then_inc(O.free, 1)
                            eng.wait_ge(O.free, count(O.free))
                        V.tensor_reduce(SA[0:n, g * 32:(g + 1) * 32], ap(slot[0:n, 0:1], [128, 32], [1, 128]),
                                        AX.X, add).then_inc(sem("dve_chain"), 1)
                        eng.wait_ge(sem("dve_chain"), count(sem("dve_chain")))
                        release(f"dk_{g}", *latest)
                    eng.sem_inc(sem("scores_d"), 1)
                    count(sem("scores_d"))
                    eng.wait_ge(S.full, S.arrive(2))
                    s = S.reading
                    V.memset(SR[0:32, 0:384], BIG).then_inc(sem("dve_chain"), 1)
                    eng.wait_ge(sem("dve_chain"), count(sem("dve_chain")))
                    for g in range(3):
                        signal, by = (S.free, 2) if g == 2 else (sem("dve_chain"), 1)
                        ts(SR[0:32, g * 128:g * 128 + DN[g]], s[0:32, g * 128:g * 128 + DN[g]], -(HD ** -0.5),
                           None, mul).then_inc(signal, by)
                        eng.wait_ge(signal, count(signal, by))
                    dec_soft(32, None, 387, HD ** -0.5, (3, small[0:32, 12:15]))
                    ts(SR[0:32, 0:387], SR[0:32, 0:387], stat[0:32, 22:23], None, mul).then_inc(sem("dve_chain"), 1)
                    eng.wait_ge(sem("dve_chain"), count(sem("dve_chain")))
                    dec_new(32, [384, 385, 386], C("bm32", 32))
                    eng.sem_inc(sem("dec_probs"), 1)
                    count(sem("dec_probs"))
                    zero_pd()
                    head_rows("d", True)
                    dec_finish("d", zs)
                    for t, (_, n) in enumerate(TOK):
                        g = z[t][0:n, ODD["gc"]:ODD["gc"] + 512]
                        tt(g, g, z[t][0:n, 0:512], mul).then_inc(sem("dve_chain"), 1)
                        eng.wait_ge(sem("dve_chain"), count(sem("dve_chain")))
                for t in range(3):
                    eng.sem_inc(sem("mix"), 1)
                    count(sem("mix"))
                eng.sem_inc(sem("y_free"), 1)
                count(sem("y_free"))

                def post(t, n):
                    stt(Y[t][0:n], Y[t][0:n], stat[0:n, 52 + t:53 + t], NW[0:n, :], mul, mul)\
                        .then_inc(sem("dve_chain"), 1)
                    eng.wait_ge(sem("dve_chain"), count(sem("dve_chain")))
                    tt(X[0:n, t, :], X[0:n, t, :], Y[t][0:n], add).then_inc(sem("dve_chain"), 1)
                    eng.wait_ge(sem("dve_chain"), count(sem("dve_chain")))
                norm(l, "post", None, post)
                eng.sem_inc(sem("y_read"), 1)
                count(sem("y_read"))
                eng.sem_inc(sem("x_next"), 1)
                count(sem("x_next"))
                mark(f"x_done{l}", *latest)

        @block.sync
        def _(sp):
            small_in = sem("const_in")
            for out, src in SMALL:
                sp.dma_start(out, src, allow_slow_non_contiguous=True).then_inc(small_in, 16)
            norms = [ins["pre_norm"][0], ins["post_norm"][0], ins["pre_norm"][1], ins["post_norm"][1]]

            def load_norm(j):
                if j:
                    sp.wait_ge(*marks[f"nw_used{j - 1}"])
                sp.dma_start(NW[:, :], bass.AP(norms[j].tensor, norms[j].offset, [[0, 128], [1, D]]))\
                    .then_inc(sem("nw_in"), 16)

            load_norm(0)
            for i, (name, queue, parts) in enumerate(items):
                if name == "wout0_0":
                    load_norm(1)
                if name == "wout1_0":
                    load_norm(3)
                if queue == "sp":
                    stream(sp, i, name, parts)
                if name == f"win0_{chunks(0)[-1][0]}":
                    sp.wait_ge(*marks["roped0"])
                    for out, src in OUTS0:
                        sp.dma_start(out, src).then_inc(sem("out0"), 16)
                if name == "win1_1024":
                    load_norm(2)
                if name == f"win1_{chunks(1)[-1][0]}":
                    sp.wait_ge(*marks["roped1"])
                    for out, src in OUTS1:
                        sp.dma_start(out, src).then_inc(sem("out0"), 16)
            sp.wait_ge(*marks["x_done1"])
            for t in range(2):
                sp.dma_start(outs["y_prompt"][0, t * 128:(t + 1) * 128, :], X[:, t, :]).then_inc(sem("out1"), 16)
            sp.dma_start(outs["y_sample"].rearrange("b o d -> b (o d)"), X[0:8, 2, :]).then_inc(sem("out1"), 16)
            sp.wait_ge(sem("out1"), 48)
            sp.wait_ge(sem("out0"), 16 * (len(OUTS0) + len(OUTS1)))
            sp.wait_ge(sem("moved"), 16 * len(MOVES))

        @block.gpsimd
        def _(pool):
            pool.wait_ge(sem("index"), 1)
            moves = list(MOVES)
            for i, (name, queue, parts) in enumerate(items):
                if queue == "pool":
                    stream(pool, i, name, parts)
                if name.startswith("win"):
                    wait_slot(pool, i)
                    for _ in range(3):
                        if moves:
                            dst, src = moves.pop(0)
                            pool.dma_start(dst, src).then_inc(sem("moved"), 16)
            for dst, src in moves:
                pool.dma_start(dst, src).then_inc(sem("moved"), 16)


NAMES = ("x_prompt", "x_sample", "cache_a_k", "cache_a_v", "cache_b_k", "cache_b_v", "cache_b_idx",
         "cache_c_cmp_k", "cache_c_cmp_v", "cache_c_sel_k", "cache_c_sel_v", "state_c_win_k", "state_c_win_v",
         "state_d_k0", "state_d_v0", "state_d_k1", "state_d_v1", "state_d_k2", "state_d_v2", "page_table",
         "pre_norm", "post_norm", "w_in_even", "w_out_even", "diff_lambda", "w_in_odd", "w_out_odd", "cmp_pos",
         "cmp_w1", "cmp_w2")


def out_shapes():
    seq, dec = 256, NB
    o = [("y_prompt", (1, seq, D)), ("y_sample", (dec, 1, D))]
    for tag, n, t in (("p_", 1, seq), ("s_", dec, 1)):
        even = [("a_k", (1, n, t, H, 2, 64)), ("a_v", (1, n, t, H, HD)), ("b_k", (1, n, t, HD)),
                ("b_v", (1, n, t, HD)), ("b_idx", (1, n, t, 64))]
        o += [(tag + a, s) for a, s in even]
    def odd(tag, n, t, win, ds):
        r = [(tag + a, (1, n, t, HD)) for a in ("c_cmp_k", "c_cmp_v", "c_sel_k", "c_sel_v")]
        r += [(tag + a, (1, n, win, HD)) for a in ("c_win_k", "c_win_v")]
        for g, w in enumerate(ds):
            r += [(tag + f"d_{kv}{g}", (1, n, w, H, HD)) for kv in "kv"]
        return r
    p_even = [x for x in o if x[0].startswith("p_")]
    s_even = [x for x in o if x[0].startswith("s_")]
    head = o[:2]
    p_odd = odd("p_", 1, seq, min(WIN, seq), [min(w, seq) for w, _ in PAIRS])
    s_odd = odd("s_", dec, 1, WIN, [min(w, DW[g] + 1) for g, (w, _) in enumerate(PAIRS)])
    return head + p_even + p_odd + s_even + s_odd


def kernel(**inputs):
    import concourse.bacc as bacc
    from concourse.bass_utils import run_bass_kernel_spmd

    nc = bacc.Bacc("TRN2", target_bir_lowering=False, num_devices=1)
    arrays, ins, outs = {}, {}, {}
    for name in NAMES + ("const",):
        a = constants() if name == "const" else np.ascontiguousarray(inputs[name])
        arrays[f"in_{name}"] = a
        ins[name] = nc.dram_tensor(f"in_{name}", a.shape, mybir.dt.from_np(a.dtype), kind="ExternalInput").ap()
    shapes = out_shapes()
    for name, shape in shapes:
        outs[name] = nc.dram_tensor(f"out_{name}", shape, F32, kind="ExternalOutput").ap()
    build(nc, ins, outs)
    r = run_bass_kernel_spmd(nc, [arrays], core_ids=[0])
    return tuple(r.results[0][f"out_{name}"] for name, _ in shapes)
```

```python
import math
from contextlib import ExitStack

import numpy as np
import concourse.bass as bass
from concourse import mybir

F32 = mybir.dt.float32
I32 = mybir.dt.int32
ALU = mybir.AluOpType
ACT = mybir.ActivationFunctionType
AX = mybir.AxisListType

D = 1024
KT = D // 128
HD = 128
H = 4
NB = 8
L = 1024
PAGE = 128
ROWS = 8
SUB = PAGE // ROWS
NPG = L // PAGE
EPS = 1e-6
NEG = -1e30
BIG = 3e38
TOK = ((0, 128), (128, 128), (256, 8))
EVEN = dict(qa=0, ka=512, va=1024, ga=1536, qb=2048, kb=2560, vb=2688, gb=2816, qi=3328, ki=3584, wi=3648)
E_EVEN = 3652
ODD = dict(qc=0, kcr=512, vcr=640, ksel=768, vsel=896, kwin=1024, vwin=1152, gl=1280, gc=1292, gd=6412)
for _g in range(3):
    ODD[f"qd{_g}"], ODD[f"kd{_g}"], ODD[f"vd{_g}"] = (1804 + 1536 * _g + 512 * _j for _j in range(3))
E_ODD = 6924
PAIRS = ((128, 1), (512, 4), (2048, 16))
DW = tuple(min(w, L) for w, _ in PAIRS)
DN = tuple(w // d for w, (_, d) in zip(DW, PAIRS))
CB, CS, CH = 32, 16, 256
NC_S, NC_P = 63, 15
NSEL = 17
WIN = 512
TOPK_P, TOPK_S = 64, 256
CMP_AT = 4
LAM_INIT = 0.8 - 0.6 * math.exp(0.0)
GELU_C = math.sqrt(2.0 / math.pi)
SLOTS = 3
SLOT = 4096

CONST = {}


def _layout():
    at = 0
    for name, n in (("ident", 128), ("causal0", 128), ("causal1", 256), ("dil0", 384), ("dil1", 768),
                    ("cmp0", 15), ("cmp1", 15), ("cmpok", 2), ("rope", 144), ("ropec", 32), ("ropecp", 32),
                    ("e64", 64), ("e32", 32), ("hm64", 8), ("bm64", 8), ("hm32", 4), ("bm32", 8),
                    ("one8", 8), ("fold", 16), ("mzero", 1), ("mone", 1), ("overlap", 17), ("bonus", 17), ("sub", 1)):
        CONST[name] = (at, n)
        at += n
    return at


N_CONST = _layout()


def constants():
    c = np.zeros((128, N_CONST), np.float32)

    def put(name, a):
        at, n = CONST[name]
        c[:a.shape[0], at:at + n] = a

    def table(pos, half):
        freqs = np.float32(500000.0) ** (-np.arange(half, dtype=np.float32) / np.float32(half))
        ang = (pos.astype(np.float32)[:, None] * freqs.astype(np.float32)).astype(np.float32)
        return np.concatenate([np.cos(ang), np.sin(ang)], 1)

    p = np.arange(128)
    put("ident", np.eye(128))
    for t in range(2):
        q, k = p[:, None] + 128 * t, np.arange(128 * (t + 1))[None]
        put(f"causal{t}", np.where(k <= q, 0.0, NEG))
        put(f"dil{t}", np.concatenate(
            [np.where((k <= q) & ((q - k) % d == 0) & (q - k <= w), 0.0, NEG) for w, d in PAIRS], 1))
        put(f"cmp{t}", np.where(np.arange(NC_P)[None] * CS + CB - 1 <= q, 0.0, NEG))
    put("cmpok", np.stack([(p >= CB - 1), p >= 0], 1))
    put("rope", np.concatenate([np.concatenate([table(pos, 8), table(pos, 16)], 1)
                                for pos in (p, p + 128, np.full(128, L))], 1))
    put("ropec", table(np.arange(NC_S) * CS + CB - 1, 16))
    put("ropecp", table(np.arange(NC_P) * CS + CB - 1, 16))
    b = np.arange(NB)
    put("e64", b[:, None] == np.arange(64)[None] // 8)
    put("e32", b[:, None] == np.arange(32)[None] // 4)
    r = np.arange(64)
    put("hm64", r[:, None] % 8 == b[None])
    put("bm64", r[:, None] // 8 == b[None])
    put("mzero", (r[:, None] % 2 == 0))
    put("mone", (r[:, None] % 2 == 1))
    r = np.arange(32)
    put("hm32", r[:, None] % 4 == np.arange(4)[None])
    put("bm32", r[:, None] // 4 == b[None])
    put("one8", np.eye(8))
    put("fold", p[:, None] % 32 == np.arange(16)[None])
    cs, ss = np.arange(NC_S)[:, None] * CS, np.arange(NSEL)[None] * 64
    put("overlap", (cs < ss + 64) & (cs + CB > ss))
    j = np.arange(NSEL)
    put("bonus", np.broadcast_to(np.where((j == 0) | (j >= NSEL - 2), 1e4, 0.0), (8, NSEL)))
    put("sub", p[:, None] % SUB)
    return c


class Ring:

    def __init__(self, full, free, view, banks):
        self.full, self.free, self.view, self.banks = full, free, view, banks
        self.made = self.read = 0

    def claim(self, k=1):
        at = self.made % self.banks
        self.made += k
        self.filling = self.view[:, at * 512:(at + k) * 512]
        return max(0, self.made - self.banks)

    def arrive(self, k=1):
        at = self.read % self.banks
        self.read += k
        self.reading = self.view[:, at * 512:(at + k) * 512]
        return self.read


def ap(view, *dims, at=0):
    return bass.AP(view.tensor, view.offset + at, [list(view.ap[0])] + [list(d) for d in dims])


def build(nc, ins, outs):
    ctx = ExitStack()
    with ctx:
        def sb(name, shape, dt=F32):
            return ctx.enter_context(nc.sbuf_tensor(name, shape, dt))

        sems = {}

        def sem(name):
            if name not in sems:
                sems[name] = ctx.enter_context(nc.semaphore(name))
            return sems[name]

        const = sb("const", [128, N_CONST])

        def C(name, rows=128):
            at, n = CONST[name]
            return const[0:rows, at:at + n]

        ring = sb("ring", [128, SLOTS * SLOT])
        Z = sb("Z", [128, 3 * E_ODD])
        xT = sb("xT", [128, KT, 256])
        xTs = sb("xTs", [128, KT, 32])
        X = sb("X", [128, 3, D])
        NW = sb("NW", [128, D])
        PD = sb("PD", [128, 2048])
        QD = sb("QD", [128, NB, 32])
        QF = sb("QF", [128, 32])
        KN = sb("KN", [128, 8])
        QK = sb("QK", [128, 6, 512])
        flat = QK[:, :, :].rearrange("p a b -> p (a b)")
        SR = flat[0:64, 0:1040]
        KTs = flat[:, 1040:2064].rearrange("p (a b) -> p a b", a=2)
        NWP = flat[:, 2048:3072]
        SM = sb("SM", [128, 2, 768])
        SA = sb("SA", [128, 512])
        PT = sb("PT", [128, 768])
        BM = sb("BM", [128, 384])
        kcT = sb("kcT", [128, NB, 64])
        VC = sb("VC", [64, NB, HD])
        kcTp = sb("kcTp", [128, 16])
        VCp = sb("VCp", [16, HD])
        posT = sb("posT", [128, 64])
        W2 = sb("W2", [128, 2, 2, HD])
        bias1 = sb("bias1", [128, 2, 2])
        lamr = SA[:, 0:256]
        lam = sb("lam", [128, 8])
        coef = sb("coef", [64, 2])
        stat = sb("stat", [128, 80])
        small = sb("small", [64, 64])
        PN = sb("PN", [64, 3, 8])
        PNT = sb("PNT", [8, 3, 64])
        RT = sb("RT", [128, 256])
        ptab = sb("ptab", [128, NB], I32)
        index = sb("index", [128, NB], I32)
        posr = RT[0:64, 0:128]

        psum = ctx.enter_context(nc.psum_tensor("psum", [128, 8 * 512], F32))
        T = Ring(sem("T_full"), sem("T_free"), psum[:, 0:1024], 2)
        S = Ring(sem("S_full"), sem("S_free"), psum[:, 1024:2048], 2)
        P = Ring(sem("P_full"), sem("P_free"), psum[:, 2048:3072], 2)
        O = Ring(sem("O_full"), sem("O_free"), psum[:, 3072:4096], 2)

        items, place, released = [], {}, {}

        def item(name, queue, parts):
            place[name] = (len(items) % SLOTS, None)
            items.append((name, queue, parts))

        def direct(src, rows, cols):
            return ("direct", src, rows, 0, cols)

        w_in = {0: ins["w_in_even"], 1: ins["w_in_odd"]}
        w_out = {0: ins["w_out_even"], 1: ins["w_out_odd"]}
        width = {0: E_EVEN, 1: E_ODD}

        def chunks(l):
            return [(c, min(512, width[l] - c)) for c in range(0, width[l], 512)]

        def weights(kind, l, w, cs):
            for c, n in cs:
                src = w[0].rearrange("(k p) n -> p k n", p=128)[:, :, c:c + n]
                item(f"{kind}{l}_{c}", "sp", [("w", src, n)])

        def gathered(name, cache, cols, per_slot):
            for s in range(0, NB, per_slot):
                item(f"{name}_{s // per_slot}", "pool",
                     [("gather", cache, b, (b - s) * ROWS * cols, ROWS * cols) for b in range(s, s + per_slot)])

        def w1(tag, kv):
            for half in range(2):
                src = ins["cmp_w1"][0, kv, half * 16:half * 16 + 16].rearrange("r d h -> d r h")
                item(f"{tag}{kv}_{half}", "sp", [("full", src)])

        gathered("rows0", ins["cache_c_cmp_k"], HD, 4)
        def gathered_one(name, cache, b):
            item(f"{name}_{b}", "pool", [("gather", cache, b, 0, ROWS * 512)])

        for i, c in enumerate(chunks(0)):
            weights("win", 0, w_in[0], [c])
            if i >= 2:
                gathered_one("ak", ins["cache_a_k"], i - 2)
        gathered("idx", ins["cache_b_idx"], 64, 8)
        gathered_one("ak", ins["cache_a_k"], 6)
        gathered_one("ak", ins["cache_a_k"], 7)
        w1("w1s", 0)
        gathered("rows1", ins["cache_c_cmp_v"], HD, 4)
        w1("w1s", 1)
        gathered("av", ins["cache_a_v"], 512, 1)
        gathered("bk", ins["cache_b_k"], HD, 4)
        gathered("bv", ins["cache_b_v"], HD, 4)
        weights("wout", 0, w_out[0], [(0, 512), (512, 512)])
        for i, c in enumerate(chunks(1)):
            weights("win", 1, w_in[1], [c])
            if i == CMP_AT:
                w1("w1p", 0)
                w1("w1p", 1)
        gathered("ck", ins["cache_c_sel_k"], HD, 4)
        gathered("cv", ins["cache_c_sel_v"], HD, 4)
        for n, w in (("wk", "state_c_win_k"), ("wv", "state_c_win_v")):
            item(n + "_0", "sp", [("full", ins[w][0].rearrange("b (p r) d -> p b (r d)", r=4))])
        for kv in "kv":
            for g, (_, d) in enumerate(PAIRS):
                src = ins[f"state_d_{kv}{g}"][0].rearrange("b (n j) h e -> n j b (h e)", j=d)[:, 0]
                item(f"d{kv}_{g}", "sp", [("rows", src, DN[g])])
        weights("wout", 1, w_out[1], [(0, 512), (512, 512)])
        order = {n: i for i, (n, _, _) in enumerate(items)}
        arrival, arrived = {}, {}
        for i, (n, queue, parts) in enumerate(items):
            s = f"slot_{'loaded' if queue == 'sp' else 'gathered'}{i % SLOTS}"
            arrived[s] = arrived.get(s, 0) + 16 * len(parts)
            arrival[n] = (sem(s), arrived[s])


        def slot_of(name):
            s = order[name] % SLOTS
            return ring[:, s * SLOT:(s + 1) * SLOT]

        level, seen, marks, latest = {}, {}, {}, [None, 0]

        def count(s, by=1):
            level[s.name] = level.get(s.name, 0) + by
            latest[:] = [s, level[s.name]]
            return level[s.name]

        def due(who, name, k=1):
            seen[who, name] = seen.get((who, name), 0) + k
            return seen[who, name]

        def mark(name, s, value):
            marks[name] = (s, value)


        def release(name, s, value):
            released[name] = (s, value)



        zt = {0: [Z[:, t * E_EVEN:(t + 1) * E_EVEN] for t in range(3)],
              1: [Z[:, t * E_ODD:(t + 1) * E_ODD] for t in range(3)]}
        R0 = 3 * E_EVEN
        rowsT = Z[:, R0:R0 + 8208]
        Y = [Z[:, R0 + t * D:R0 + (t + 1) * D] for t in range(3)]
        kc_rows = Z[:, R0 + 8208:R0 + 8208 + 1024]
        hid = xT[:, :, :].rearrange("p k c -> p (k c)")[:, 0:1024]
        hid2 = xT[:, :, :].rearrange("p k c -> p (k c)")[:, 1024:2048]
        kept_keys = SM[:, :, :].rearrange("p a c -> p (a c)")[0:8, 512:1536]

        preps, units = {0: [], 1: []}, {0: [], 1: []}
        prep_n = [0]

        def prep(l, blocks, rows):
            n = prep_n[0]
            prep_n[0] += 1
            preps[l].append(dict(n=n, at=len(units[l]), blocks=blocks, rows=rows, slot=n % 6))
            return n % 6, n

        def unit(l, **u):
            u["deps"] = sorted(set(u["deps"]))
            units[l].append(u)

        sc = HD ** -0.5
        for h in range(H):
            s, n = prep(0, [(t, EVEN["qa"] + 128 * h, 128) for t in (0, 1)]
                        + [(t, EVEN["ka"] + 128 * h, 128) for t in (0, 1)], 128)
            for t in (0, 1):
                nk = 128 * (t + 1)
                unit(0, kind="a", t=t, h=h, nk=nk, maps=2, banks=2, scale=0.125, mask=C(f"causal{t}"),
                     scores=[(m * 512, QK[64 * m:64 * m + 64, s, t * 128:t * 128 + 128],
                              QK[64 * m:64 * m + 64, s, 256:256 + nk]) for m in (0, 1)],
                     deps=[n], pmaps=1, kt=t + 1, kw=128,
                     v=[[zt[0][k][:, EVEN["va"] + 128 * h:EVEN["va"] + 128 * h + 128] for k in range(t + 1)]])

        def pair_units(l, kind, q, k, v, mask, deps_k):
            ks, kn = deps_k
            for h in (0, 2):
                s, n = prep(l, [(t, q + 128 * (h + j), 128) for j in (0, 1) for t in (0, 1)], 128)
                for t in (0, 1):
                    nk = 128 * (t + 1)
                    unit(l, kind=kind, t=t, h=h, nk=nk, maps=2, banks=1, scale=sc, mask=mask[t],
                         scores=[(m * nk, QK[:, s, m * 256 + t * 128:m * 256 + t * 128 + 128],
                                  QK[:, ks, 0:nk]) for m in (0, 1)],
                         deps=[n, kn], pmaps=2, kt=t + 1, kw=128,
                         v=[[zt[l][kk][:, v:v + 128] for kk in range(t + 1)]] * 2)

        kb_dep = prep(0, [(t, EVEN["kb"], 128) for t in (0, 1)], 128)
        pair_units(0, "b", EVEN["qb"], EVEN["kb"], EVEN["vb"], [BM[:, 0:128], BM[:, 128:384]], kb_dep)
        cs = [prep(1, [(t, ODD["qc"] + 128 * (h + j), 128) for j in (0, 1) for t in (0, 1)], 128) for h in (0, 2)]
        for t in (0, 1):
            unit(1, kind="cmp", t=t, h=0, nk=NC_P, maps=4, banks=1, scale=sc, mask=C(f"cmp{t}"),
                 scores=[(h * NC_P, QK[:, cs[h // 2][0], (h % 2) * 256 + t * 128:(h % 2) * 256 + t * 128 + 128],
                          kcTp[:, 0:NC_P]) for h in range(H)],
                 deps=[cs[0][1], cs[1][1]], pmaps=4, kt=1, kw=NC_P, v=[[VCp[0:NC_P, :]]] * 4)
        mc = [C("causal0"), C("causal1")]
        for kind in ("sel", "win"):
            kd = prep(1, [(t, ODD["k" + kind], 128) for t in (0, 1)], 128)
            ks, kn = kd
            for h in (0, 2):
                s, n = cs[h // 2]
                for t in (0, 1):
                    nk = 128 * (t + 1)
                    unit(1, kind=kind, t=t, h=h, nk=nk, maps=2, banks=1, scale=sc, mask=mc[t],
                         scores=[(m * nk, QK[:, s, m * 256 + t * 128:m * 256 + t * 128 + 128],
                                  QK[:, ks, 0:nk]) for m in (0, 1)],
                         deps=[n, kn], pmaps=2, kt=t + 1, kw=128,
                         v=[[zt[1][kk][:, ODD["v" + kind]:ODD["v" + kind] + 128] for kk in range(t + 1)]] * 2)
        while prep_n[0] % 6:
            prep_n[0] += 1
        for h in range(H):
            s3 = [prep(1, [(t, ODD[f"qd{g}"] + 128 * h, 128) for t in (0, 1)]
                       + [(t, ODD[f"kd{g}"] + 128 * h, 128) for t in (0, 1)], 128) for g in range(3)]
            for t in (0, 1):
                nk = 128 * (t + 1)
                unit(1, kind="d", t=t, h=h, nk=3 * nk, maps=1, banks=2, scale=sc, mask=C(f"dil{t}"),
                     scores=[(g * nk, QK[:, s3[g][0], t * 128:t * 128 + 128], QK[:, s3[g][0], 256:256 + nk])
                             for g in range(3)],
                     deps=[n for _, n in s3], pmaps=1, kt=3 * (t + 1), kw=128,
                     v=[[zt[1][kk][:, ODD[f"vd{g}"] + 128 * h:ODD[f"vd{g}"] + 128 * h + 128]
                         for g in range(3) for kk in range(t + 1)]])

        GATES = {0: {3: ["ga"], 6: ["gb"]}, 1: {3: ["gc"], 13: ["gd"]}}
        ROTATED = {0: {1: [(EVEN["qa"], 16, 64, 8)], 5: [(EVEN["qb"], 5, 128, 16)], 7: [(EVEN["qi"], 5, 64, 8)]},
                   1: {0: [(ODD["qc"], 4, 128, 16)], 2: [(ODD["ksel"], 2, 256, 16)], 5: [(ODD["qd0"], 8, 128, 16)],
                       8: [(ODD["qd1"], 8, 128, 16)], 11: [(ODD["qd2"], 8, 128, 16)]}}
        FIRST_UNIT = {0: 0, 8: 8, 12: 0}

        def wait_slot(eng, i):
            if i >= SLOTS:
                eng.wait_ge(*released[items[i - SLOTS][0]])

        def stream(eng, i, name, parts):
            wait_slot(eng, i)
            slot = ring[:, (i % SLOTS) * SLOT:(i % SLOTS + 1) * SLOT]
            arrived = arrival[name][0]
            for part in parts:
                if part[0] == "w":
                    _, src, n = part
                    eng.dma_start(ap(slot[:, 0:1], [n, KT], [1, n]), src).then_inc(arrived, 16)
                elif part[0] == "full":
                    _, src = part
                    a, b = src.shape[1:]
                    eng.dma_start(ap(slot[:, 0:1], [b, a], [1, b]), src).then_inc(arrived, 16)
                elif part[0] == "rows":
                    _, src, n = part
                    eng.dma_start(ap(slot[0:n, 0:1], [512, NB], [1, 512]), src).then_inc(arrived, 16)
                else:
                    _, cache, b, at, n = part
                    rows = bass.AP(cache.tensor, cache.offset, [[n, cache.shape[1] * SUB], [1, n]])
                    nc.gpsimd.indirect_dma_start(out=slot[:, at:at + n], out_offset=None, in_=rows,
                                                 in_offset=bass.IndirectOffsetOnAxis(ap=index[:, b:b + 1], axis=0))\
                        .then_inc(arrived, 16)

        SMALL = [(const[:, :], ins["const"]),
                 (X[:, 0:2, :], ins["x_prompt"][0].rearrange("(t p) d -> p t d", p=128)),
                 (X[0:8, 2, :], ins["x_sample"].rearrange("b o d -> b (o d)")),
                 (W2[:, :, :, :].rearrange("p k h d -> p (k h) d"),
                  ins["cmp_w2"][0].rearrange("k (h p) d -> p (k h) d", p=128)),
                 (posr, ins["cmp_pos"][0].rearrange("k r d -> (k r) d")),
                 (lamr[:, :], bass.AP(ins["diff_lambda"].tensor, ins["diff_lambda"].offset, [[0, 128], [1, 256]]))]
        table = ins["page_table"]
        for pg in range(NPG):
            SMALL.append((ptab[pg * SUB:(pg + 1) * SUB, :],
                          bass.AP(table.tensor, table.offset + pg, [[0, SUB], [NPG, NB]])))
        N_SMALL = len(SMALL)

        OUTS = {0: [], 1: []}

        def state(l, name, c, n):
            o = outs["p_" + name]
            keep = o.shape[2]
            o2 = bass.AP(o.tensor, o.offset, [[n, keep], [1, n]])
            for t in range(2):
                if keep == 128 and t == 0:
                    continue
                at = t * 128 - (256 - keep)
                OUTS[l].append((o2[at:at + 128, :], zt[l][t][:, c:c + n]))
            o = outs["s_" + name]
            rows = o.shape[2]
            OUTS[l].append((bass.AP(o.tensor, o.offset + (rows - 1) * n, [[rows * n, NB], [1, n]]),
                            zt[l][2][0:8, c:c + n]))

        for name, c, n in (("a_k", "ka", 512), ("a_v", "va", 512), ("b_k", "kb", 128), ("b_v", "vb", 128),
                           ("b_idx", "ki", 64)):
            state(0, name, EVEN[c], n)
        for name, c in (("c_cmp_k", "kcr"), ("c_cmp_v", "vcr"), ("c_sel_k", "ksel"), ("c_sel_v", "vsel"),
                        ("c_win_k", "kwin"), ("c_win_v", "vwin")):
            state(1, name, ODD[c], 128)
        for g in range(3):
            state(1, f"d_k{g}", ODD[f"kd{g}"], 512)
            state(1, f"d_v{g}", ODD[f"vd{g}"], 512)
        OUTS0, OUTS1 = OUTS[0], OUTS[1]

        MOVES = []
        for name, n in [(f"d_{kv}{g}", 512) for g in range(3) for kv in "kv"] + [("c_win_k", 128), ("c_win_v", 128)]:
            src, dst = ins["state_" + name], outs["s_" + name]
            old, new = src.shape[2], dst.shape[2]
            kept = new - 1
            for b in range(NB):
                m = kept * n // 16
                MOVES.append((bass.AP(dst.tensor, dst.offset + b * new * n, [[m, 16], [1, m]]),
                              bass.AP(src.tensor, src.offset + (b * old + old - kept) * n, [[m, 16], [1, m]])))

        block = ctx.enter_context(nc.Block())

        @block.tensor
        def _(pe):
            mm = nc.tensor.matmul

            def tr(out, in_):
                n = in_.shape[0]
                return nc.tensor.transpose(out, in_, C("ident", n)[:, 0:n])

            def folded(kv, tag, lhs, m):
                pe.wait_ge(*arrival[f"{tag}{kv}_0"])
                a = slot_of(f"{tag}{kv}_0")
                pe.wait_ge(*arrival[f"{tag}{kv}_1"])
                b = slot_of(f"{tag}{kv}_1")
                pe.wait_ge(P.free, P.claim())
                out = P.filling
                for r in range(CB):
                    g = 32 * (r % 4)
                    last = mm(out[g:g + m, 0:CH], lhs(r), (a if r < 16 else b)[:, (r % 16) * CH:(r % 16 + 1) * CH],
                              start=r < 4, stop=r >= CB - 4)
                last.then_inc(P.full, 1)
                pe.wait_ge(sem("hid_partials"), due("pe", "hid_partials"))
                pe.wait_ge(P.free, P.claim())
                out = P.filling
                for h in range(2):
                    last = mm(out[:, h * 16:h * 16 + m], PT[:, 512 + h * 128:512 + (h + 1) * 128], C("fold")[:, 0:m],
                              start=True, stop=True)
                last.then_inc(P.full, 1)

            def compress(kv):
                pe.wait_ge(*arrival[f"w1s{kv}_0"])
                a = slot_of(f"w1s{kv}_0")
                pe.wait_ge(*arrival[f"w1s{kv}_1"])
                b = slot_of(f"w1s{kv}_1")
                for h in range(2):
                    pe.wait_ge(P.free, P.claim())
                    hp = P.filling
                    for r in range(CB):
                        w = (a if r < 16 else b)[:, (r % 16) * CH + h * 128:(r % 16) * CH + h * 128 + 128]
                        last = mm(hp[:, 0:512], w, ap(rowsT[:, r:r + 1], [CS, 512]), start=r == 0, stop=r == CB - 1)
                        if r == CB - 1:
                            last.then_inc(P.full, 1)
                            release(f"w1s{kv}_0", P.full, P.made)
                            release(f"w1s{kv}_1", P.full, P.made)
                        yield

            def fill(steps, n=1000):
                for _ in range(n):
                    if next(steps, "end") == "end":
                        break

            def second(kv, hid, step, nb, n):
                pe.wait_ge(sem("gelu"), due("pe", "gelu"))
                pe.wait_ge(S.free, S.claim(2))
                out = S.filling
                for b in range(nb):
                    for h in range(2):
                        last = mm(out[0:n, b * HD:(b + 1) * HD], hid[:, h * step + b * 64:h * step + b * 64 + n],
                                  W2[:, kv, h, :], start=h == 0, stop=h == 1)
                last.then_inc(S.full, 2)
                mark(f"second{kv}_{nb}", S.full, S.made)

            def to_xT(l, what, view_of, t):
                n = TOK[t][1]
                pe.wait_ge(sem(what), due("pe", what))
                for half in range(2):
                    pe.wait_ge(T.free, T.claim())
                    tp = T.filling
                    for j in range(4):
                        last = tr(tp[:, j * 128:j * 128 + n], view_of(t, half * 4 + j)[0:n])
                    last.then_inc(T.full, 1)
                mark(f"{what}_read{l}_{t}", T.full, T.made)

            def prompt_rows(t, w, n):
                pe.wait_ge(P.free, P.claim())
                out = P.filling
                for k in range(KT):
                    last = mm(out[:, 0:n], xT[:, k, t * 128:(t + 1) * 128], w[:, k * n:(k + 1) * n],
                              start=k == 0, stop=k == KT - 1)
                last.then_inc(P.full, 1)

            def decode_rows(w, n):
                pe.wait_ge(P.free, P.claim())
                out = P.filling
                for k in range(KT):
                    g = 32 * (k % 4)
                    last = mm(out[g:g + 32, 0:n], xTs[:, k, :], w[:, k * n:(k + 1) * n], start=k < 4, stop=k >= 4)
                last.then_inc(P.full, 1)

            def decode_sum(n):
                pe.wait_ge(sem("partials"), due("pe", "partials"))
                pe.wait_ge(P.free, P.claim())
                out = P.filling
                mm(out[0:8, 0:n], C("fold")[:, 0:8], PT[:, 0:n], start=True, stop=True).then_inc(P.full, 1)

            def project(l, between):
                cs = chunks(l)
                for i, (c, n) in enumerate(cs):
                    pe.wait_ge(*arrival[f"win{l}_{c}"])
                    w = slot_of(f"win{l}_{c}")
                    prompt_rows(0, w, n)
                    if i:
                        decode_sum(cs[i - 1][1])
                    prompt_rows(1, w, n)
                    decode_rows(w, n)
                    release(f"win{l}_{c}", P.full, P.made)
                    between(i)
                decode_sum(cs[-1][1])

            def project_out(l, tile_done):
                ws = []
                for c in (0, 512):
                    pe.wait_ge(*arrival[f"wout{l}_{c}"])
                    w = slot_of(f"wout{l}_{c}")
                    ws.append(w)
                for t in (0, 1):
                    for w in ws:
                        prompt_rows(t, w, 512)
                    tile_done(t)
                for i, w in enumerate(ws):
                    decode_rows(w, 512)
                    release(f"wout{l}_{i * 512}", P.full, P.made)
                    decode_sum(512)
                tile_done(2)

            evacuated = {}

            def do_prep(l, p):
                pe.wait_ge(T.free, T.claim())
                tp = T.filling
                for j, (t, c, w) in enumerate(p["blocks"]):
                    last = tr(tp[0:w, j * 128:(j + 1) * 128], zt[l][t][:, c:c + w])
                last.then_inc(T.full, 1)
                evacuated[p["n"]] = T.made

            def scores(u, n):
                for d in u["deps"]:
                    pe.wait_ge(T.free, evacuated[d])
                pe.wait_ge(S.free, S.claim(u["banks"]))
                out = S.filling
                for i, (c, q, k) in enumerate(u["scores"]):
                    w = k.shape[-1]
                    last = mm(out[:, c:c + w], q, k, start=True, stop=True)
                last.then_inc(S.full, u["banks"])
                mark(("s", n), S.free, S.made)
                for d in u["deps"]:
                    mark(("qk", d), S.full, S.made)

            def output(u, n):
                pe.wait_ge(sem("probs" if u["kind"] != "a" else "diffs"), due("pe", "probs" if u["kind"] != "a" else "diffs"))
                blocks = [(m, k) for m in range(u["pmaps"]) for k in range(u["kt"])]
                for i0 in range(0, len(blocks), 4):
                    pe.wait_ge(T.free, T.claim())
                    tp = T.filling
                    for j, (m, k) in enumerate(blocks[i0:i0 + 4]):
                        c = m * u["nk"] + k * u["kw"]
                        last = tr(tp[0:u["kw"], j * 128:(j + 1) * 128], SM[:, n % 2, c:c + u["kw"]])
                    last.then_inc(T.full, 1)
                mark(("p", n), T.full, T.made)
                pe.wait_ge(T.free, T.made)
                pe.wait_ge(O.free, O.claim())
                out = O.filling
                for m in range(u["pmaps"]):
                    for k in range(u["kt"]):
                        i = m * u["kt"] + k
                        last = mm(out[:, m * HD:(m + 1) * HD], PT[0:u["kw"], i * 128:(i + 1) * 128],
                                  u["v"][m][k], start=k == 0, stop=k == u["kt"] - 1)
                last.then_inc(O.full, 1)
                mark(("o", n), O.full, O.made)

            def attention(l, us, n0, between):
                for i in range(len(us) + 1):
                    for p in preps[l]:
                        if p["at"] == FIRST_UNIT[n0] + i and i < len(us):
                            do_prep(l, p)
                    if i < len(us):
                        scores(us[i], n0 + i)
                    if i:
                        between()
                        output(us[i - 1], n0 + i - 1)

            def index_prompt():
                z = zt[0]
                for j in (0, 1):
                    pe.wait_ge(T.free, T.claim())
                    tp = T.filling
                    for i in range(4):
                        h, t = 2 * j + i // 2, i % 2
                        last = tr(tp[0:64, i * 128:(i + 1) * 128],
                                  z[t][:, EVEN["qi"] + 64 * h:EVEN["qi"] + 64 * h + 64])
                    last.then_inc(T.full, 1)
                pe.wait_ge(T.free, T.claim())
                tp = T.filling
                for t in (0, 1):
                    last = tr(tp[0:64, t * 128:(t + 1) * 128], z[t][:, EVEN["ki"]:EVEN["ki"] + 64])
                last.then_inc(T.full, 1)
                pe.wait_ge(T.free, T.made)
                for t in (0, 1):
                    nk = 128 * (t + 1)
                    for j in (0, 1):
                        pe.wait_ge(S.free, S.claim())
                        out = S.filling
                        for i in (0, 1):
                            last = mm(out[:, i * nk:(i + 1) * nk], QK[0:64, j, i * 256 + t * 128:i * 256 + t * 128 + 128],
                                      QK[0:64, 2, 0:nk], start=True, stop=True)
                        last.then_inc(S.full, 1)
                mark("index_prompt", S.full, S.made)

            def dec_query(z, q, w, k, wk):
                pe.wait_ge(T.free, T.claim())
                tp = T.filling
                for h in range(H):
                    last = tr(tp[0:w, h * 8:h * 8 + 8], z[0:8, q + w * h:q + w * h + w])
                if k is not None:
                    last = tr(tp[0:w, 32:40], z[0:8, k:k + wk])
                last.then_inc(T.full, 1)
                pe.wait_ge(T.free, T.made)

            def dec_own_key(w):
                pe.wait_ge(O.free, O.claim())
                out = O.filling
                mm(out[0:32, 0:8], QF[0:w, :], KN[0:w, :], start=True, stop=True).then_inc(O.full, 1)

            def dec_scores(name, per_slot, tiles, w, masked):
                pe.wait_ge(S.free, S.claim(2))
                out = S.filling
                if masked:
                    pe.wait_ge(sem("dec_mask"), due("pe", "dec_mask"))
                    for half in range(2):
                        mm(out[0:32, half * 512:(half + 1) * 512], C("e32", 8),
                           SR[0:8, half * 512:(half + 1) * 512], start=True, stop=False)
                jobs = [(b, half) for b in range(NB) for half in range(tiles // 4)]
                filled = [None] * len(jobs)
                for i in range(len(jobs) + 1):
                    if i < len(jobs):
                        b, half = jobs[i]
                        pe.wait_ge(*arrival[f"{name}_{b // per_slot}"])
                        slot = slot_of(f"{name}_{b // per_slot}")
                        pe.wait_ge(T.free, T.claim())
                        tp = T.filling
                        for j in range(4):
                            c = (b % per_slot) * tiles * w + (half * 4 + j) * w
                            last = tr(tp[0:w, j * 128:(j + 1) * 128], slot[:, c:c + w])
                        last.then_inc(T.full, 1)
                        filled[i] = T.made
                        if b % per_slot == per_slot - 1 and half == tiles // 4 - 1:
                            release(f"{name}_{b // per_slot}", T.full, T.made)
                    if i:
                        b, half = jobs[i - 1]
                        pe.wait_ge(T.free, filled[i - 1])
                        last = mm(out[0:32, half * 512:(half + 1) * 512], QD[0:w, b, :],
                                  KTs[0:w, (i - 1) % 2, :], start=b == 0 and not masked, stop=b == NB - 1)
                        if i < len(jobs):
                            last.then_inc(sem("keys_used"), 1)
                last.then_inc(S.full, 2)

            def dec_probs_T(rows, tiles):
                pe.wait_ge(sem("dec_probs"), due("pe", "dec_probs"))
                pe.wait_ge(T.free, T.claim())
                tp = T.filling
                for j, (c, n) in enumerate(tiles):
                    last = tr(tp[0:n, j * rows:(j + 1) * rows], SR[0:rows, c:c + n])
                last.then_inc(T.full, 1)

            def dec_new_T(rows, n):
                pe.wait_ge(T.free, T.claim())
                tp = T.filling
                for g in range(n):
                    last = tr(tp[0:8, g * rows:(g + 1) * rows], PN[0:rows, g, :])
                last.then_inc(T.full, 1)

            def spread(kind):
                pe.wait_ge(sem("dec_head"), due("pe", "dec_head"))
                pe.wait_ge(O.free, O.claim())
                out = O.filling
                mm(out[0:8, :], C("bm32", 32), SM[0:32, 0, 0:512], start=True, stop=True).then_inc(O.full, 1)

            def dec_values(name, per_slot, tiles, z, v):
                pe.wait_ge(sem("dec_pd"), due("pe", "dec_pd"))
                pe.wait_ge(O.free, O.claim())
                out = O.filling
                for b in range(NB):
                    pe.wait_ge(*arrival[f"{name}_{b // per_slot}"])
                    slot = slot_of(f"{name}_{b // per_slot}")
                    for r in range(tiles):
                        c = ((b % per_slot) * tiles + r) * HD
                        last = mm(out[0:32, 0:HD], PD[:, r * 256 + b * 32:r * 256 + b * 32 + 32],
                                  slot[:, c:c + HD], start=b == 0 and r == 0, stop=False)
                mm(out[0:32, 0:HD], PNT[0:8, 0, 0:32], z[0:8, v:v + HD], start=False, stop=True).then_inc(O.full, 1)
                for s in range(NB // per_slot):
                    release(f"{name}_{s}", O.full, O.made)
                spread(name)

            def dec_shared(z, name, per_slot, tiles, q, k, v, masked, new_query, vper):
                if new_query:
                    dec_query(z, q, HD, k, HD)
                else:
                    pe.wait_ge(T.free, T.claim())
                    tp = T.filling
                    tr(tp[0:HD, 0:8], z[0:8, k:k + HD]).then_inc(T.full, 1)
                    pe.wait_ge(T.free, T.made)
                dec_own_key(HD)
                dec_scores(name + "k", per_slot, tiles, HD, masked)
                dec_probs_T(32, [(r * 128, 128) for r in range(tiles)])
                dec_new_T(32, 1)
                dec_values(name + "v", vper, tiles, z, v)

            def cache_rows(kv):
                for half in range(2):
                    pe.wait_ge(*arrival[f"rows{kv}_{half}"])
                    slot = slot_of(f"rows{kv}_{half}")
                    for i in range(8):
                        b, rq = i // 2, i % 2
                        pe.wait_ge(T.free, T.claim())
                        tp = T.filling
                        for j in range(4):
                            c = b * 1024 + (rq * 4 + j) * 128
                            last = tr(tp[:, j * 128:(j + 1) * 128], slot[:, c:c + 128])
                        last.then_inc(T.full, 1)
                    release(f"rows{kv}_{half}", T.full, T.made)
                pe.wait_ge(T.free, T.made)

            def broadcast_query(zs, q, b):
                pe.wait_ge(O.free, O.claim())
                out = O.filling
                mm(out[:, :], ap(C("one8", 8)[:, b:b + 1], [0, 128]), zs[0:8, q:q + 512],
                   start=True, stop=True).then_inc(O.full, 1)

            pe.wait_ge(sem("const_in"), 16 * N_SMALL)
            pe.wait_ge(T.free, T.claim())
            tp = T.filling
            tr(tp[:, 0:64], posr).then_inc(T.full, 1)
            for t in range(3):
                to_xT(0, "xn", lambda t, k: PD[:, k * 128:(k + 1) * 128], t)
            cache_rows(0)

            for l in (0, 1):
                z, zs = zt[l], zt[l][2]
                if l == 0:
                    def between(i):
                        if i == 2:
                            pe.wait_ge(sem("own_a"), due("pe", "own_a"))
                            pe.wait_ge(O.free, O.claim())
                            out = O.filling
                            mm(out[0:64, 0:8], C("e64", 8), small[0:8, 32:40], start=True, stop=True)\
                                .then_inc(O.full, 1)
                        if i >= 2:
                            broadcast_query(zs, 0, i - 2)
                    project(0, between)
                    pe.wait_ge(sem("roped"), due("pe", "roped"))
                    dec_query(zs, EVEN["qi"], 64, EVEN["ki"], 64)
                    dec_own_key(64)
                    pe.wait_ge(O.free, O.claim())
                    out = O.filling
                    mm(out[0:32, 0:4], C("e32", 8), zs[0:8, EVEN["wi"]:EVEN["wi"] + 4],
                       start=True, stop=True).then_inc(O.full, 1)
                    dec_scores("idx", 8, 8, 64, False)
                    broadcast_query(zs, 0, 6)
                    broadcast_query(zs, 0, 7)
                    folded(0, "w1s", lambda r: posT[:, r:r + 1], 1)
                    pe.wait_ge(sem("relu_rows"), due("pe", "relu_rows"))
                    pe.wait_ge(S.free, S.claim(2))
                    out = S.filling
                    for half in range(2):
                        last = mm(out[0:8, half * 512:(half + 1) * 512], small[0:32, 16:24],
                                  SR[0:32, half * 512:(half + 1) * 512], start=True, stop=True)
                    last.then_inc(S.full, 2)
                    pe.wait_ge(O.free, O.claim())
                    out = O.filling
                    mm(out[0:8, 0:1], small[0:32, 16:24], SR[0:32, 1024:1025], start=True, stop=True)\
                        .then_inc(O.full, 1)
                    mark("index_rows", O.full, O.made)
                    filler = compress(0)
                    attention(0, units[0][0:8], 0, lambda: fill(filler, 5))
                    index_prompt()
                    fill(filler)
                    cache_rows(1)
                    folded(1, "w1s", lambda r: posT[:, CB + r:CB + r + 1], 1)
                    second(0, hid, 512, NB, NC_S)
                    filler = compress(1)
                    fill(filler, 4)
                    pe.wait_ge(sem("kc_roped"), due("pe", "kc_roped"))
                    for half in range(2):
                        pe.wait_ge(T.free, T.claim())
                        tp = T.filling
                        for j in range(4):
                            b = half * 4 + j
                            last = tr(tp[:, j * 128:j * 128 + NC_S], kc_rows[0:NC_S, b * HD:(b + 1) * HD])
                        last.then_inc(T.full, 1)
                    pe.wait_ge(sem("topk_prompt"), due("pe", "topk_prompt"))
                    attention(0, units[0][8:12], 8, lambda: fill(filler, 6))
                    pe.wait_ge(sem("scores_a"), due("pe", "scores_a"))
                    pe.wait_ge(S.free, S.claim(2))
                    out = S.filling
                    for r in range(ROWS):
                        last = tr(out[0:64, r * 128:(r + 1) * 128], SA[:, r * 64:(r + 1) * 64])
                    last.then_inc(S.full, 2)
                    fill(filler)
                    dec_probs_T(64, [(r * 128, 128) for r in range(ROWS)])
                    dec_new_T(64, 1)
                    second(1, hid, 512, NB, NC_S)
                    pe.wait_ge(sem("pd_pairs"), due("pe", "pd_pairs"))
                    pe.wait_ge(O.free, O.claim())
                    out = O.filling
                    for b in range(NB):
                        pe.wait_ge(*arrival[f"av_{b}"])
                        slot = slot_of(f"av_{b}")
                        for r in range(ROWS):
                            last = mm(out[0:32, :], PD[:, r * 256 + b * 32:r * 256 + b * 32 + 32],
                                      slot[:, r * 512:(r + 1) * 512], start=b == 0 and r == 0, stop=False)
                        last.then_inc(sem("av_used"), 1)
                        release(f"av_{b}", sem("av_used"), b + 1)
                    mm(out[0:32, :], PNT[0:8, 1, 0:32], zs[0:8, EVEN["va"]:EVEN["va"] + 512],
                       start=False, stop=True).then_inc(O.full, 1)
                    spread("a")
                    pe.wait_ge(O.free, O.claim())
                    out = O.filling
                    pe.wait_ge(sem("own_mask"), due("pe", "own_mask"))
                    mm(out[0:32, 0:1], C("e32", 8), small[0:8, 50:51], start=True, stop=True).then_inc(O.full, 1)
                    dec_shared(zs, "b", 4, 8, EVEN["qb"], EVEN["kb"], EVEN["vb"], True, True, 4)
                else:
                    def between(i):
                        if i != CMP_AT:
                            return
                        pe.wait_ge(P.free, P.made - 2)
                        pe.wait_ge(T.free, T.claim())
                        tp = T.filling
                        for j in range(4):
                            c = ODD["kcr"] if j < 2 else ODD["vcr"]
                            last = tr(tp[:, j * 128:(j + 1) * 128], z[j % 2][:, c:c + 128])
                        last.then_inc(T.full, 1)
                        pe.wait_ge(T.free, T.made)
                        for kv in range(2):
                            folded(kv, "w1p", lambda r: ap(QK[:, 5, kv * 256 + r:kv * 256 + r + 1], [CS, NC_P]), NC_P)
                            release(f"w1p{kv}_0", P.full, P.made)
                            release(f"w1p{kv}_1", P.full, P.made)
                            second(kv, BM[:, 0:80], 16, 1, NC_P)
                        pe.wait_ge(sem("kcp_roped"), due("pe", "kcp_roped"))
                        pe.wait_ge(T.free, T.claim())
                        tp = T.filling
                        tr(tp[:, 0:NC_P], BM[0:NC_P, 128:256]).then_inc(T.full, 1)
                    project(1, between)
                    pe.wait_ge(sem("roped"), due("pe", "roped"))
                    attention(1, units[1], 12, lambda: None)
                    dec_query(zs, ODD["qc"], HD, None, 0)
                    pe.wait_ge(S.free, S.claim(2))
                    out = S.filling
                    for b in range(NB):
                        last = mm(out[0:32, 0:NC_S], QD[:, b, :], kcT[:, b, 0:NC_S], start=b == 0, stop=b == NB - 1)
                    last.then_inc(S.full, 2)
                    dec_probs_T(32, [(0, NC_S)])
                    pe.wait_ge(sem("imp_in"), due("pe", "imp_in"))
                    pe.wait_ge(O.free, O.claim())
                    out = O.filling
                    mm(out[0:8, 0:NSEL], small[0:NC_S, 24:32], C("overlap", NC_S), start=True, stop=True)\
                        .then_inc(O.full, 1)
                    pe.wait_ge(sem("dec_pd"), due("pe", "dec_pd"))
                    pe.wait_ge(O.free, O.claim())
                    out = O.filling
                    for b in range(NB):
                        last = mm(out[0:32, 0:HD], PD[0:NC_S, b * 32:b * 32 + 32], VC[0:NC_S, b, :],
                                  start=b == 0, stop=b == NB - 1)
                    last.then_inc(O.full, 1)
                    spread("cmp")
                    dec_shared(zs, "c", 4, 8, None, ODD["ksel"], ODD["vsel"], True, False, 4)
                    dec_shared(zs, "w", 8, 4, None, ODD["kwin"], ODD["vwin"], False, False, 8)
                    pe.wait_ge(O.free, O.claim())
                    out = O.filling
                    pe.wait_ge(sem("own_d"), due("pe", "own_d"))
                    mm(out[0:32, 0:12], C("e32", 8), small[0:8, 32:44], start=True, stop=True).then_inc(O.full, 1)
                    for g in range(3):
                        for b in range(NB):
                            broadcast_query(zs, ODD[f"qd{g}"], b)
                    pe.wait_ge(sem("scores_d"), due("pe", "scores_d"))
                    pe.wait_ge(S.free, S.claim(2))
                    out = S.filling
                    for g in range(3):
                        last = tr(out[0:32, g * 128:g * 128 + DN[g]], SA[0:DN[g], g * 32:(g + 1) * 32])
                    last.then_inc(S.full, 2)
                    dec_probs_T(32, [(g * 128, DN[g]) for g in range(3)])
                    dec_new_T(32, 3)
                    pe.wait_ge(sem("dec_pd"), due("pe", "dec_pd"))
                    pe.wait_ge(O.free, O.claim())
                    out = O.filling
                    for g in range(3):
                        pe.wait_ge(*arrival[f"dv_{g}"])
                        slot = slot_of(f"dv_{g}")
                        n = DN[g]
                        for b in range(NB):
                            mm(out[0:32, :], PD[0:n, g * 256 + b * 32:g * 256 + b * 32 + 32],
                               slot[0:n, b * 512:(b + 1) * 512], start=g == 0 and b == 0, stop=False)
                        last = mm(out[0:32, :], PNT[0:8, g, 0:32], zs[0:8, ODD[f"vd{g}"]:ODD[f"vd{g}"] + 512],
                                  start=False, stop=g == 2)
                        if g < 2:
                            last.then_inc(sem("dv_used"), 1)
                            release(f"dv_{g}", sem("dv_used"), g + 1)
                    last.then_inc(O.full, 1)
                    release("dv_2", O.full, O.made)
                    spread("d")
                gates = (EVEN["ga"], EVEN["gb"]) if l == 0 else (ODD["gc"], ODD["gd"])
                for t in range(3):
                    to_xT(l, "mix", lambda t, k: z[t][:, gates[k // 4] + (k % 4) * 128:gates[k // 4] + (k % 4 + 1) * 128], t)
                pe.wait_ge(T.free, T.made)

                def next_rows(t):
                    if t:
                        to_xT(1, "xn", lambda t, k: PD[:, k * 128:(k + 1) * 128], t - 1)
                project_out(l, next_rows if l == 0 else lambda t: None)
                if l == 0:
                    to_xT(1, "xn", lambda t, k: PD[:, k * 128:(k + 1) * 128], 2)
                    pe.wait_ge(T.free, T.made)

        @block.scalar
        def _(eng):
            act = nc.scalar.activation
            copy = nc.scalar.copy


            def hidden(kv, n, out, one_bank):
                for h in range(2):
                    if h == 0 or not one_bank:
                        eng.wait_ge(P.full, P.arrive())
                        hp = P.reading
                    src = hp[:, h * 16:h * 16 + n] if one_bank else hp[:, 0:n]
                    signal, by = (sem("act_chain"), 1) if one_bank and h == 0 else (P.free, 1)
                    act(out[h], src, ACT.Identity, bias=bias1[:, kv, h:h + 1]).then_inc(signal, by)
                    eng.wait_ge(signal, count(signal, by))
                eng.sem_inc(sem("hid"), 1)
                count(sem("hid"))
                eng.wait_ge(sem("gelu_in"), due("act", "gelu_in"))

            def partials(n):
                eng.wait_ge(P.full, P.arrive())
                pp = P.reading
                copy(PT[:, 0:n], pp[:, 0:n]).then_inc(P.free, 1)
                eng.wait_ge(P.free, count(P.free))
                eng.sem_inc(sem("partials"), 1)
                count(sem("partials"))

            def hid_partials():
                eng.wait_ge(P.full, P.arrive())
                pp = P.reading
                copy(PT[:, 512:512 + CH], pp[:, 0:CH]).then_inc(P.free, 1)
                eng.wait_ge(P.free, count(P.free))
                eng.sem_inc(sem("hid_partials"), 1)
                count(sem("hid_partials"))

            def position(kv):
                hid_partials()
                eng.wait_ge(P.full, P.arrive())
                pp = P.reading
                copy(bias1[:, kv, :], ap(pp[:, 0:1], [16, 2])).then_inc(P.free, 1)
                eng.wait_ge(P.free, count(P.free))

            def norm(t, src):
                n = TOK[t][1]
                act(PD[0:n, 1024:2048], src[0:n], ACT.Square, accum_out=stat[0:n, 60 + t:61 + t])\
                    .then_inc(sem("squares"), 1)
                eng.wait_ge(sem("squares"), count(sem("squares")))
                eng.wait_ge(sem("mean_square"), due("act", "mean_square"))
                act(stat[0:n, 56 + t:57 + t], stat[0:n, 52 + t:53 + t], ACT.Sqrt).then_inc(sem("rms"), 1)
                eng.wait_ge(sem("rms"), count(sem("rms")))

            def to_xT(t):
                n = TOK[t][1]
                for half in range(2):
                    eng.wait_ge(T.full, T.arrive())
                    tp = T.reading
                    if t < 2:
                        dst = xT[:, half * 4:half * 4 + 4, t * 128:t * 128 + n]
                    else:
                        dst = xTs[:, half * 4:half * 4 + 4, 0:n]
                    copy(dst, ap(tp[:, 0:1], [128, 4], [1, n])).then_inc(T.free, 1)
                    eng.wait_ge(T.free, count(T.free))

            def rows_out(dst, n):
                eng.wait_ge(P.full, P.arrive())
                pp = P.reading
                copy(dst, pp[0:dst.shape[0], 0:n]).then_inc(P.free, 1)
                eng.wait_ge(P.free, count(P.free))

            def gate(l, name):
                c = (EVEN if l == 0 else ODD)[name]
                for t, (_, n) in enumerate(TOK):
                    eng.wait_ge(sem("gate_next"), due("act", "gate_next"))
                    act(SM[0:n, 0, 0:512], zt[l][t][0:n, c:c + 512], ACT.Tanh, scale=0.5)\
                        .then_inc(sem("gate_tanh"), 1)
                    eng.wait_ge(sem("gate_tanh"), count(sem("gate_tanh")))
                    if name == "gc":
                        g = zt[l][t][0:n, ODD["gl"]:ODD["gl"] + 12]
                        act(g, g, ACT.Tanh, scale=0.5).then_inc(sem("gl_tanh"), 1)
                        eng.wait_ge(sem("gl_tanh"), count(sem("gl_tanh")))

            def project(l, between):
                cs = chunks(l)
                z = zt[l]
                for i in range(len(cs) + 1):
                    if i < len(cs):
                        c, n = cs[i]
                        rows_out(z[0][:, c:c + n], n)
                    if i:
                        cp, np_ = cs[i - 1]
                        rows_out(z[2][0:8, cp:cp + np_], np_)
                        mark(("z", l, i - 1), *latest)
                    if i < len(cs):
                        rows_out(z[1][:, c:c + n], n)
                        partials(n)
                    if i:
                        for name in GATES[l].get(i - 1, ()):
                            gate(l, name)
                    if i < len(cs):
                        between(i)

            def project_out(l, tile_done):
                for t in range(3):
                    for c in (0, 512):
                        if t == 2:
                            partials(512)
                        rows_out(Y[t][0:TOK[t][1], c:c + 512], 512)
                    tile_done(t)

            def do_prep(l, p):
                eng.wait_ge(T.full, T.arrive())
                tp = T.reading
                n = p["n"]
                if ("qk", n - 6) in marks:
                    eng.wait_ge(*marks[("qk", n - 6)])
                if n == 6:
                    eng.wait_ge(*marks["index_prompt"])
                w = 128 * len(p["blocks"])
                copy(QK[0:p["rows"], p["slot"], 0:w], tp[0:p["rows"], 0:w]).then_inc(T.free, 1)
                eng.wait_ge(T.free, count(T.free))

            def exps(u, n):
                eng.wait_ge(*marks[("s", n)])
                nk = u["nk"]
                for m in range(u["maps"]):
                    x = SM[:, n % 2, m * nk:(m + 1) * nk]
                    signal, by = (sem("exp_a" if u["kind"] == "a" else "probs"), 1) if m == u["maps"] - 1 else (sem("act_chain"), 1)
                    act(x, x, ACT.Exp, scale=-1.0, bias=stat[:, (n % 2) * 4 + m:(n % 2) * 4 + m + 1],
                        accum_out=stat[:, 64 + (n % 4) * 4 + m:65 + (n % 4) * 4 + m]).then_inc(signal, by)
                    eng.wait_ge(signal, count(signal, by))

            def probs_T(u, n):
                blocks = u["pmaps"] * u["kt"]
                for i0 in range(0, blocks, 4):
                    k = min(4, blocks - i0)
                    eng.wait_ge(T.full, T.arrive())
                    tp = T.reading
                    if i0 == 0 and n:
                        eng.wait_ge(*marks[("o", n - 1)])
                    copy(PT[0:u["kw"], i0 * 128:(i0 + k) * 128], tp[0:u["kw"], 0:k * 128]).then_inc(T.free, 1)
                    eng.wait_ge(T.free, count(T.free))

            def attention(l, us, n0):
                for i in range(len(us) + 1):
                    for p in preps[l]:
                        if p["at"] == FIRST_UNIT[n0] + i and i < len(us):
                            do_prep(l, p)
                    if i:
                        probs_T(us[i - 1], n0 + i - 1)
                    if i < len(us):
                        exps(us[i], n0 + i)

            def dec_query(w, with_key, dense=True):
                eng.wait_ge(T.full, T.arrive())
                tp = T.reading
                copy(ap(QD[0:w, 0, 0:1], [36, NB], [1, H]), ap(tp[0:w, 0:1], [1, NB], [8, H]))\
                    .then_inc(sem("act_chain"), 1)
                eng.wait_ge(sem("act_chain"), count(sem("act_chain")))
                signal, by = (sem("act_chain"), 1) if with_key else (T.free, 1)
                copy(ap(QF[0:w, 0:1], [4, NB], [1, H]), ap(tp[0:w, 0:1], [1, NB], [8, H])).then_inc(signal, by)
                eng.wait_ge(signal, count(signal, by))
                if with_key:
                    copy(KN[0:w, :], tp[0:w, 32:40]).then_inc(T.free, 1)
                    eng.wait_ge(T.free, count(T.free))

            def dec_scores(tiles, w):
                n = NB * tiles // 4
                base = seen.get(("act", "keys_used"), 0)
                for i in range(n):
                    eng.wait_ge(T.full, T.arrive())
                    tp = T.reading
                    if i >= 2:
                        eng.wait_ge(sem("keys_used"), base + i - 1)
                    copy(KTs[0:w, i % 2, :], tp[0:w, :]).then_inc(T.free, 1)
                    eng.wait_ge(T.free, count(T.free))
                seen["act", "keys_used"] = base + n - 1

            def dec_exp(rows, n):
                eng.wait_ge(sem("dec_scaled"), due("act", "dec_scaled"))
                act(SR[0:rows, 0:n], SR[0:rows, 0:n], ACT.Exp, scale=-1.0, bias=stat[0:rows, 20:21],
                    accum_out=stat[0:rows, 21:22]).then_inc(sem("dec_exp"), 1)
                eng.wait_ge(sem("dec_exp"), count(sem("dec_exp")))

            def dec_pd(tiles):
                eng.wait_ge(T.full, T.arrive())
                tp = T.reading
                eng.wait_ge(sem("pd_zero"), due("act", "pd_zero"))
                copy(ap(PD[:, 0:1], [256, tiles], [36, NB], [1, H]),
                     ap(tp[:, 0:1], [32, tiles], [4, NB], [1, H])).then_inc(T.free, 1)
                eng.wait_ge(T.free, count(T.free))

            def dec_new(rows, n, s):
                eng.wait_ge(T.full, T.arrive())
                tp = T.reading
                copy(PNT[:, 0:n, 0:rows], ap(tp[0:8, 0:1], [rows, n], [1, rows])).then_inc(T.free, 1)
                eng.wait_ge(T.free, count(T.free))
                eng.sem_inc(sem(s), 1)
                count(sem(s))

            def dec_shared(tiles, n, new_query):
                if new_query:
                    dec_query(HD, True)
                else:
                    eng.wait_ge(T.full, T.arrive())
                    tp = T.reading
                    copy(KN[:, :], tp[:, 0:8]).then_inc(T.free, 1)
                    eng.wait_ge(T.free, count(T.free))
                dec_scores(tiles, HD)
                dec_exp(32, n)
                dec_pd(tiles)
                dec_new(32, 1, "dec_pd")

            def cache_rows(kv):
                for b in range(NB):
                    for rq in range(2):
                        eng.wait_ge(T.full, T.arrive())
                        tp = T.reading
                        copy(ap(rowsT[:, b * 1024 + rq * 4:b * 1024 + rq * 4 + 1], [1, 4], [8, 128]),
                             ap(tp[:, 0:1], [128, 4], [1, 128])).then_inc(T.free, 1)
                        eng.wait_ge(T.free, count(T.free))

            eng.wait_ge(sem("stat_zero"), due("act", "stat_zero"))
            eng.wait_ge(sem("const_in"), 16 * N_SMALL)
            eng.wait_ge(T.full, T.arrive())
            tp = T.reading
            copy(posT[:, :], tp[:, 0:64]).then_inc(T.free, 1)
            eng.wait_ge(T.free, count(T.free))
            eng.wait_ge(sem("lam_in"), due("act", "lam_in"))
            act(lam[:, 2:4], lam[:, 0:2], ACT.Exp).then_inc(sem("lam_exp"), 1)
            eng.wait_ge(sem("lam_exp"), count(sem("lam_exp")))
            for t in range(3):
                norm(t, X[:, t, :])
                to_xT(t)
            cache_rows(0)
            for l in (0, 1):
                z, zs = zt[l], zt[l][2]
                if l == 1:
                    eng.wait_ge(sem("out0"), 16 * len(OUTS0))
                if l == 0:
                    project(0, lambda i: None)
                    dec_query(64, True)
                    dec_scores(8, 64)
                    position(0)
                    attention(0, units[0][0:8], 0)
                    for j in range(3):
                        eng.wait_ge(T.full, T.arrive())
                        tp = T.reading
                        w = 512 if j < 2 else 256
                        if j == 0:
                            eng.wait_ge(*marks[("qk", 2)])
                        copy(QK[0:64, j, 0:w], tp[0:64, 0:w]).then_inc(T.free, 1)
                        eng.wait_ge(T.free, count(T.free))
                    hidden(0, 512, [hid[:, 0:512], hid[:, 512:1024]], False)
                    act(hid2, hid2, ACT.Tanh, scale=GELU_C).then_inc(sem("gelu_tanh"), 1)
                    eng.wait_ge(sem("gelu_tanh"), count(sem("gelu_tanh")))
                    cache_rows(1)
                    position(1)
                    for half in range(2):
                        eng.wait_ge(T.full, T.arrive())
                        tp = T.reading
                        copy(kcT[:, half * 4:half * 4 + 4, 0:NC_S],
                             ap(tp[:, 0:1], [128, 4], [1, NC_S])).then_inc(T.free, 1)
                        eng.wait_ge(T.free, count(T.free))
                    attention(0, units[0][8:12], 8)
                    dec_exp(64, 1025)
                    hidden(1, 512, [hid[:, 0:512], hid[:, 512:1024]], False)
                    act(hid2, hid2, ACT.Tanh, scale=GELU_C).then_inc(sem("gelu_tanh"), 1)
                    eng.wait_ge(sem("gelu_tanh"), count(sem("gelu_tanh")))
                    eng.wait_ge(T.full, T.arrive())
                    tp = T.reading
                    copy(SA[:, :], tp[:, :]).then_inc(T.free, 1)
                    eng.wait_ge(T.free, count(T.free))
                    dec_new(64, 1, "pair_in")
                    dec_shared(8, 1025, True)
                else:
                    def between(i):
                        if i != CMP_AT:
                            return
                        eng.wait_ge(T.full, T.arrive())
                        tp = T.reading
                        copy(QK[:, 5, :], tp[:, :]).then_inc(T.free, 1)
                        eng.wait_ge(T.free, count(T.free))
                        for kv in range(2):
                            hid_partials()
                            hidden(kv, NC_P, [BM[:, 0:NC_P], BM[:, 16:16 + NC_P]], True)
                            for h in range(2):
                                x = BM[:, 32 + 16 * h:32 + 16 * h + NC_P]
                                signal, by = (sem("gelu_tanh"), 1) if h else (sem("act_chain"), 1)
                                act(x, x, ACT.Tanh, scale=GELU_C).then_inc(signal, by)
                                eng.wait_ge(signal, count(signal, by))
                        eng.wait_ge(T.full, T.arrive())
                        tp = T.reading
                        copy(kcTp[:, 0:NC_P], tp[:, 0:NC_P]).then_inc(T.free, 1)
                        eng.wait_ge(T.free, count(T.free))
                    project(1, between)
                    attention(1, units[1], 12)
                    dec_query(HD, False)
                    dec_exp(32, NC_S)
                    eng.wait_ge(T.full, T.arrive())
                    tp = T.reading
                    eng.wait_ge(sem("pd_zero"), due("act", "pd_zero"))
                    copy(ap(PD[0:NC_S, 0:1], [36, NB], [1, H]), ap(tp[0:NC_S, 0:1], [4, NB], [1, H]))\
                        .then_inc(sem("act_chain"), 1)
                    eng.wait_ge(sem("act_chain"), count(sem("act_chain")))
                    copy(SA[0:NC_S, 0:32], tp[0:NC_S, 0:32]).then_inc(T.free, 1)
                    eng.wait_ge(T.free, count(T.free))
                    eng.sem_inc(sem("imp_T"), 1)
                    count(sem("imp_T"))
                    eng.sem_inc(sem("dec_pd"), 1)
                    count(sem("dec_pd"))
                    dec_shared(8, 1025, False)
                    dec_shared(4, 513, False)
                    dec_exp(32, 387)
                    eng.wait_ge(T.full, T.arrive())
                    tp = T.reading
                    eng.wait_ge(sem("pd_zero"), due("act", "pd_zero"))
                    for g in range(3):
                        n = DN[g]
                        signal, by = (T.free, 1) if g == 2 else (sem("act_chain"), 1)
                        copy(ap(PD[0:n, g * 256:g * 256 + 1], [36, NB], [1, H]),
                             ap(tp[0:n, g * 32:g * 32 + 1], [4, NB], [1, H])).then_inc(signal, by)
                        eng.wait_ge(signal, count(signal, by))
                    dec_new(32, 3, "dec_pd")
                if l == 0:
                    eng.wait_ge(sem("o_a"), due("act", "o_a"))
                    for t, (_, n) in enumerate(TOK):
                        act(stat[0:n, 44:48], stat[0:n, 24 + t * 4:28 + t * 4], ACT.Sqrt)\
                            .then_inc(sem("act_chain"), 1)
                        eng.wait_ge(sem("act_chain"), count(sem("act_chain")))
                        copy(stat[0:n, 24 + t * 4:28 + t * 4], stat[0:n, 44:48]).then_inc(sem("a_rms"), 1)
                        eng.wait_ge(sem("a_rms"), count(sem("a_rms")))
                for t in range(3):
                    to_xT(t)
                eng.wait_ge(sem("y_free"), due("act", "y_free"))
                if l == 1:
                    eng.wait_ge(sem("out0"), 16 * (len(OUTS0) + len(OUTS1)))

                def tile_done(t):
                    norm(t, Y[t])
                    if l == 0:
                        eng.wait_ge(sem("x_next"), due("act", "x_next"))
                        norm(t, X[:, t, :])
                        if t:
                            to_xT(t - 1)
                project_out(l, tile_done)
                if l == 0:
                    to_xT(2)

        @block.vector
        def _(eng):
            V = nc.vector
            tt, ts, stt = V.tensor_tensor, V.tensor_scalar, V.scalar_tensor_tensor
            mul, add, sub = ALU.mult, ALU.add, ALU.subtract


            def rope(x, heads, step, half, table):
                n = x.shape[0]
                both = ap(x, [step, heads], [half, 2], [1, half])
                lo, hi = ap(x, [step, heads], [1, half]), ap(x, [step, heads], [1, half], at=half)
                cos = ap(table[:, 0:1], [0, heads], [0, 2], [1, half])
                sin = ap(table[:, half:half + 1], [0, heads], [0, 2], [1, half])
                tmp = RT[0:n, 0:heads * 2 * half]
                w = 2 * half
                tt(ap(tmp, [w, heads], [half, 2], [1, half]), both, sin, mul).then_inc(sem("dve_chain"), 1)
                eng.wait_ge(sem("dve_chain"), count(sem("dve_chain")))
                tt(both, both, cos, mul).then_inc(sem("dve_chain"), 1)
                eng.wait_ge(sem("dve_chain"), count(sem("dve_chain")))
                tt(lo, lo, ap(RT[0:n, half:half + 1], [w, heads], [1, half]), sub).then_inc(sem("dve_chain"), 1)
                eng.wait_ge(sem("dve_chain"), count(sem("dve_chain")))
                tt(hi, hi, ap(RT[0:n, 0:1], [w, heads], [1, half]), add).then_inc(sem("dve_chain"), 1)
                eng.wait_ge(sem("dve_chain"), count(sem("dve_chain")))

            def gelu(hx, x2, both):
                eng.wait_ge(sem("hid"), due("dve", "hid"))
                for x, y in zip(hx, x2):
                    tt(y, x, x, mul).then_inc(sem("dve_chain"), 1)
                    eng.wait_ge(sem("dve_chain"), count(sem("dve_chain")))
                    ts(y, y, 0.044715, 1.0, mul, add).then_inc(sem("dve_chain"), 1)
                    eng.wait_ge(sem("dve_chain"), count(sem("dve_chain")))
                    tt(y, y, x, mul).then_inc(sem("dve_chain"), 1)
                    eng.wait_ge(sem("dve_chain"), count(sem("dve_chain")))
                eng.sem_inc(sem("gelu_in"), 1)
                count(sem("gelu_in"))
                eng.wait_ge(sem("gelu_tanh"), due("dve", "gelu_tanh"))
                for x, y in zip(hx, x2):
                    ts(y, y, 1.0, 0.5, add, mul).then_inc(sem("dve_chain"), 1)
                    eng.wait_ge(sem("dve_chain"), count(sem("dve_chain")))
                    tt(x, x, y, mul).then_inc(sem("dve_chain"), 1)
                    eng.wait_ge(sem("dve_chain"), count(sem("dve_chain")))
                eng.sem_inc(sem("gelu"), 1)
                count(sem("gelu"))

            def norm(t):
                n = TOK[t][1]
                ms, r, x = (stat[0:n, c + t:c + t + 1] for c in (52, 49, 56))
                eng.wait_ge(sem("squares"), due("dve", "squares"))
                ts(ms, stat[0:n, 60 + t:61 + t], 1.0 / D, EPS, mul, add).then_inc(sem("mean_square"), 1)
                eng.wait_ge(sem("mean_square"), count(sem("mean_square")))
                eng.wait_ge(sem("rms"), due("dve", "rms"))
                V.reciprocal(r, x).then_inc(sem("dve_chain"), 1)
                eng.wait_ge(sem("dve_chain"), count(sem("dve_chain")))
                tt(x, r, r, mul).then_inc(sem("dve_chain"), 1)
                eng.wait_ge(sem("dve_chain"), count(sem("dve_chain")))
                tt(x, x, ms, mul).then_inc(sem("dve_chain"), 1)
                eng.wait_ge(sem("dve_chain"), count(sem("dve_chain")))
                ts(x, x, -0.5, 1.5, mul, add).then_inc(sem("dve_chain"), 1)
                eng.wait_ge(sem("dve_chain"), count(sem("dve_chain")))
                tt(r, r, x, mul).then_inc(sem("dve_chain"), 1)
                eng.wait_ge(sem("dve_chain"), count(sem("dve_chain")))
                return r

            def xn(l, t):
                r = norm(t)
                n = TOK[t][1]
                if t:
                    eng.wait_ge(*marks[f"xn_read{l}_{t - 1}"])
                eng.wait_ge(sem("pre_in"), 16 * (l + 1))
                stt(PD[0:n, 0:1024], X[0:n, t, :], r, NWP[0:n, :], mul, mul).then_inc(sem("xn"), 1)
                eng.wait_ge(sem("xn"), count(sem("xn")))

            def gate(l, name):
                c = (EVEN if l == 0 else ODD)[name]
                for t, (_, n) in enumerate(TOK):
                    eng.sem_inc(sem("gate_next"), 1)
                    count(sem("gate_next"))
                    eng.wait_ge(sem("gate_tanh"), due("dve", "gate_tanh"))
                    g = zt[l][t][0:n, c:c + 512]
                    ts(SM[0:n, 0, 0:512], SM[0:n, 0, 0:512], 1.0, 0.5, add, mul).then_inc(sem("dve_chain"), 1)
                    eng.wait_ge(sem("dve_chain"), count(sem("dve_chain")))
                    tt(g, g, SM[0:n, 0, 0:512], mul).then_inc(sem("dve_chain"), 1)
                    eng.wait_ge(sem("dve_chain"), count(sem("dve_chain")))
                    if name == "gc":
                        eng.wait_ge(sem("gl_tanh"), due("dve", "gl_tanh"))
                        g = zt[l][t][0:n, ODD["gl"]:ODD["gl"] + 12]
                        ts(g, g, 1.0, 0.5, add, mul).then_inc(sem("dve_chain"), 1)
                        eng.wait_ge(sem("dve_chain"), count(sem("dve_chain")))

            def rope_tiles(l, c, heads, step, half):
                for t, (_, n) in enumerate(TOK):
                    tab = C("rope", n)[:, 48 * t:48 * t + 48]
                    rope(zt[l][t][0:n, c:c + 1], heads, step, half, tab[:, 0:16] if half == 8 else tab[:, 16:48])

            def score_a(b):
                eng.wait_ge(*arrival[f"ak_{b}"])
                slot = slot_of(f"ak_{b}")
                eng.wait_ge(O.full, O.arrive())
                o = O.reading
                kv3 = ap(slot[:, 0:1], [512, ROWS], [1, 512])
                tt(kv3, kv3, ap(o[:, 0:1], [0, ROWS], [1, 512]), mul).then_inc(O.free, 1)
                eng.wait_ge(O.free, count(O.free))
                V.tensor_reduce(ap(SA[:, b * 8:b * 8 + 1], [64, ROWS], [1, 8]),
                                ap(slot[:, 0:1], [512, ROWS], [64, 8], [1, 64]), AX.X, add)\
                    .then_inc(sem("dve_chain"), 1)
                eng.wait_ge(sem("dve_chain"), count(sem("dve_chain")))
                release(f"ak_{b}", *latest)

            def soft(u, n):
                eng.wait_ge(S.full, S.arrive(u["banks"]))
                s = S.reading
                if n >= 2:
                    eng.wait_ge(*marks[("p", n - 2)])
                nk = u["nk"]
                step = 512 if u["kind"] == "a" else nk
                for m in range(u["maps"]):
                    signal, by = (S.free, u["banks"]) if m == u["maps"] - 1 else (sem("dve_chain"), 1)
                    V.tensor_tensor_reduce(out=SM[:, n % 2, m * nk:(m + 1) * nk], in0=s[:, m * step:m * step + nk],
                                           in1=u["mask"], scale=-u["scale"], scalar=BIG, op0=add, op1=ALU.min,
                                           accum_out=stat[:, (n % 2) * 4 + m:(n % 2) * 4 + m + 1]).then_inc(signal, by)
                    eng.wait_ge(signal, count(signal, by))

            def combine(u, n):
                eng.wait_ge(sem("exp_a"), due("dve", "exp_a"))
                nk, x = u["nk"], SM[:, n % 2, :]
                den = stat[:, 64 + (n % 4) * 4:66 + (n % 4) * 4]
                V.reciprocal(stat[:, 16:18], den).then_inc(sem("dve_chain"), 1)
                eng.wait_ge(sem("dve_chain"), count(sem("dve_chain")))
                ts(stat[:, 17:18], stat[:, 17:18], lam[:, 5:6], None, mul).then_inc(sem("dve_chain"), 1)
                eng.wait_ge(sem("dve_chain"), count(sem("dve_chain")))
                ts(x[:, nk:2 * nk], x[:, nk:2 * nk], stat[:, 17:18], None, mul).then_inc(sem("dve_chain"), 1)
                eng.wait_ge(sem("dve_chain"), count(sem("dve_chain")))
                stt(x[:, 0:nk], x[:, 0:nk], stat[:, 16:17], x[:, nk:2 * nk], mul, add).then_inc(sem("diffs"), 1)
                eng.wait_ge(sem("diffs"), count(sem("diffs")))

            def finish(u, n, l):
                eng.wait_ge(O.full, O.arrive())
                o = O.reading
                t, h, kind, z = u["t"], u["h"], u["kind"], zt[l][u["t"]]
                k = u["pmaps"]
                den = stat[:, 64 + (n % 4) * 4:64 + (n % 4) * 4 + k]
                if kind == "a":
                    V.tensor_copy(z[:, EVEN["qa"] + 128 * h:EVEN["qa"] + 128 * h + 128], o[:, 0:128])\
                        .then_inc(O.free, 1)
                    eng.wait_ge(O.free, count(O.free))
                    return
                r = stat[:, 16:16 + k]
                V.reciprocal(r, den).then_inc(sem("dve_chain"), 1)
                eng.wait_ge(sem("dve_chain"), count(sem("dve_chain")))
                if kind in ("cmp", "sel", "win"):
                    j = ("cmp", "sel", "win").index(kind)
                    tt(r, r, ap(z[:, ODD["gl"] + 3 * h + j:ODD["gl"] + 3 * h + j + 1], [3, k]), mul)\
                        .then_inc(sem("dve_chain"), 1)
                    eng.wait_ge(sem("dve_chain"), count(sem("dve_chain")))
                if kind == "cmp":
                    ts(r, r, C("cmpok")[:, t:t + 1], None, mul).then_inc(sem("dve_chain"), 1)
                    eng.wait_ge(sem("dve_chain"), count(sem("dve_chain")))
                rb = ap(stat[:, 16:17], [1, k], [0, 128])
                ov = ap(o[:, 0:1], [128, k], [1, 128])
                if kind == "cmp":
                    acc = z[:, ODD["qc"]:ODD["qc"] + 512]
                    tt(ap(acc[:, 0:1], [128, 4], [1, 128]), ov, rb, mul).then_inc(O.free, 1)
                    eng.wait_ge(O.free, count(O.free))
                    return
                tt(ap(RT[:, 0:1], [128, k], [1, 128]), ov, rb, mul).then_inc(O.free, 1)
                eng.wait_ge(O.free, count(O.free))
                if kind in ("sel", "win"):
                    acc = z[:, ODD["qc"] + 128 * h:ODD["qc"] + 128 * h + 128 * k]
                    tt(acc, acc, RT[:, 0:128 * k], add).then_inc(sem("dve_chain"), 1)
                    eng.wait_ge(sem("dve_chain"), count(sem("dve_chain")))
                else:
                    c = (EVEN["gb"] if kind == "b" else ODD["gd"]) + 128 * h
                    g = z[:, c:c + 128 * k]
                    tt(g, g, RT[:, 0:128 * k], mul).then_inc(sem("dve_chain"), 1)
                    eng.wait_ge(sem("dve_chain"), count(sem("dve_chain")))

            def attention(l, us, n0, between=lambda: None):
                for i in range(len(us) + 2):
                    if i < len(us):
                        soft(us[i], n0 + i)
                        between()
                    if 1 <= i <= len(us) and us[i - 1]["kind"] == "a":
                        combine(us[i - 1], n0 + i - 1)
                    if i >= 2:
                        finish(us[i - 2], n0 + i - 2, l)

            def topk(work, k, w8):
                for _ in range(0, k, 8):
                    V.max(w8, work).then_inc(sem("dve_chain"), 1)
                    eng.wait_ge(sem("dve_chain"), count(sem("dve_chain")))
                    V.match_replace(work, w8, work, -BIG).then_inc(sem("dve_chain"), 1)
                    eng.wait_ge(sem("dve_chain"), count(sem("dve_chain")))
                    yield

            def fill(steps, n=1000):
                for _ in range(n):
                    if next(steps, "end") == "end":
                        break

            def dec_own(w, dst):
                eng.wait_ge(O.full, O.arrive())
                o = O.reading
                V.tensor_tensor_reduce(out=small[0:32, 0:8], in0=o[0:32, 0:8], in1=C("bm32", 32), scale=1.0,
                                       scalar=0.0, op0=mul, op1=add, accum_out=dst)\
                    .then_inc(O.free, 1)
                eng.wait_ge(O.free, count(O.free))

            def dec_soft(rows, src, n, scale, own):
                k, o = own
                m = n - k
                if src is not None:
                    ts(SR[0:rows, 0:m], src, -scale, None, mul).then_inc(S.free, 2)
                    eng.wait_ge(S.free, count(S.free, 2))
                if k:
                    ts(SR[0:rows, m:n], o, -scale, None, mul).then_inc(sem("dve_chain"), 1)
                    eng.wait_ge(sem("dve_chain"), count(sem("dve_chain")))
                V.tensor_reduce(stat[0:rows, 20:21], SR[0:rows, 0:n], AX.X, ALU.min).then_inc(sem("dec_scaled"), 1)
                eng.wait_ge(sem("dec_scaled"), count(sem("dec_scaled")))
                eng.wait_ge(sem("dec_exp"), due("dve", "dec_exp"))
                V.reciprocal(stat[0:rows, 22:23], stat[0:rows, 21:22]).then_inc(sem("dve_chain"), 1)
                eng.wait_ge(sem("dve_chain"), count(sem("dve_chain")))

            def dec_new(rows, cols, bm):
                for g, c in enumerate(cols):
                    ts(PN[0:rows, g, :], bm, SR[0:rows, c:c + 1], None, mul).then_inc(sem("dve_chain"), 1)
                    eng.wait_ge(sem("dve_chain"), count(sem("dve_chain")))

            def zero_pd():
                V.memset(PD[:, :], 0.0).then_inc(sem("pd_zero"), 1)
                eng.wait_ge(sem("pd_zero"), count(sem("pd_zero")))

            def head_rows(kind, wide):
                eng.wait_ge(O.full, O.arrive())
                o = O.reading
                src = ap(o[0:32, 0:1], [128 if wide else 0, H], [1, 128])
                hm = ap(C("hm32", 32)[:, 0:1], [1, H], [0, 128])
                tt(ap(SM[0:32, 0, 0:1], [128, H], [1, 128]), src, hm, mul).then_inc(O.free, 1)
                eng.wait_ge(O.free, count(O.free))
                eng.sem_inc(sem("dec_head"), 1)
                count(sem("dec_head"))

            def dec_finish(kind, z):
                eng.wait_ge(O.full, O.arrive())
                o = O.reading
                z = z[0:8]
                o = o[0:8, :]
                if kind == "a":
                    V.tensor_copy(z[:, 0:512], o).then_inc(O.free, 1)
                    eng.wait_ge(O.free, count(O.free))
                elif kind in ("cmp", "c", "w"):
                    j = ("cmp", "c", "w").index(kind)
                    g = ap(z[:, ODD["gl"] + j:ODD["gl"] + j + 1], [3, H], [0, 128])
                    acc = z[:, ODD["qc"]:ODD["qc"] + 512]
                    dst = acc if kind == "cmp" else SM[0:8, 0, 0:512]
                    tt(ap(dst[:, 0:1], [128, H], [1, 128]), ap(o[:, 0:1], [128, H], [1, 128]), g, mul)\
                        .then_inc(O.free, 1)
                    eng.wait_ge(O.free, count(O.free))
                    if kind != "cmp":
                        tt(acc, acc, dst, add).then_inc(sem("dve_chain"), 1)
                        eng.wait_ge(sem("dve_chain"), count(sem("dve_chain")))
                else:
                    c = EVEN["gb"] if kind == "b" else ODD["gd"]
                    tt(z[:, c:c + 512], z[:, c:c + 512], o, mul).then_inc(O.free, 1)
                    eng.wait_ge(O.free, count(O.free))

            def dec_shared(kind, z, tiles, masked):
                n = tiles * 128
                dec_own(HD, small[0:32, 8:9])
                if kind == "b":
                    tt(small[0:32, 8:9], small[0:32, 8:9], small[0:32, 51:52], add).then_inc(sem("dve_chain"), 1)
                    eng.wait_ge(sem("dve_chain"), count(sem("dve_chain")))
                eng.wait_ge(S.full, S.arrive(2))
                s = S.reading
                dec_soft(32, s[0:32, 0:n], n + 1, HD ** -0.5, (1, small[0:32, 8:9]))
                ts(SR[0:32, 0:n + 1], SR[0:32, 0:n + 1], stat[0:32, 22:23], None, mul).then_inc(sem("dve_chain"), 1)
                eng.wait_ge(sem("dve_chain"), count(sem("dve_chain")))
                dec_new(32, [n], C("bm32", 32))
                eng.sem_inc(sem("dec_probs"), 1)
                count(sem("dec_probs"))
                zero_pd()
                head_rows(kind, False)
                dec_finish(kind, z)

            eng.wait_ge(sem("const_in"), 16 * N_SMALL)
            ts(index[:, :], ptab[:, :], float(SUB), C("sub"), mul, add).then_inc(sem("index"), 1)
            eng.wait_ge(sem("index"), count(sem("index")))
            V.memset(rowsT[:, 8192:8208], 0.0).then_inc(sem("rows_tail"), 1)
            eng.wait_ge(sem("rows_tail"), count(sem("rows_tail")))
            V.memset(QD[:, :, :], 0.0).then_inc(sem("dve_chain"), 1)
            eng.wait_ge(sem("dve_chain"), count(sem("dve_chain")))
            V.memset(xTs[:, :, :], 0.0).then_inc(sem("dve_chain"), 1)
            eng.wait_ge(sem("dve_chain"), count(sem("dve_chain")))
            V.memset(small[:, :], 0.0).then_inc(sem("dve_chain"), 1)
            eng.wait_ge(sem("dve_chain"), count(sem("dve_chain")))
            V.memset(stat[:, :], 0.0).then_inc(sem("stat_zero"), 1)
            eng.wait_ge(sem("stat_zero"), count(sem("stat_zero")))
            for j in range(2):
                V.tensor_tensor_reduce(out=RT[:, 128:192], in0=lamr[:, j * 128:j * 128 + 64],
                                       in1=lamr[:, j * 128 + 64:j * 128 + 128], scale=1.0, scalar=0.0,
                                       op0=mul, op1=add, accum_out=lam[:, j:j + 1])\
                    .then_inc(sem("dve_chain"), 1)
                eng.wait_ge(sem("dve_chain"), count(sem("dve_chain")))
            eng.sem_inc(sem("lam_in"), 1)
            count(sem("lam_in"))
            for t in range(3):
                xn(0, t)
            eng.wait_ge(sem("lam_exp"), due("dve", "lam_exp"))
            tt(lam[:, 4:5], lam[:, 2:3], lam[:, 3:4], sub).then_inc(sem("dve_chain"), 1)
            eng.wait_ge(sem("dve_chain"), count(sem("dve_chain")))
            ts(lam[:, 5:6], lam[:, 4:5], LAM_INIT, -1.0, add, mul).then_inc(sem("dve_chain"), 1)
            eng.wait_ge(sem("dve_chain"), count(sem("dve_chain")))
            ts(coef[:, 0:1], C("mone", 64), lam[0:64, 5:6], None, mul).then_inc(sem("dve_chain"), 1)
            eng.wait_ge(sem("dve_chain"), count(sem("dve_chain")))
            tt(coef[:, 1:2], coef[:, 0:1], C("mzero", 64), add).then_inc(sem("dve_chain"), 1)
            eng.wait_ge(sem("dve_chain"), count(sem("dve_chain")))

            for l in (0, 1):
                z, zs = zt[l], zt[l][2]
                n_chunks = len(chunks(l))
                for i in range(n_chunks):
                    eng.wait_ge(*marks[("z", l, i)])
                    for c, heads, step, half in ROTATED[l].get(i, ()):
                        rope_tiles(l, c, heads, step, half)
                    for name in GATES[l].get(i, ()):
                        gate(l, name)
                    if l == 0 and i == 1:
                        tt(RT[0:8, 0:256], zs[0:8, 0:256], zs[0:8, 512:768], mul).then_inc(sem("dve_chain"), 1)
                        eng.wait_ge(sem("dve_chain"), count(sem("dve_chain")))
                        V.tensor_reduce(small[0:8, 32:36], ap(RT[0:8, 0:1], [64, 4], [1, 64]), AX.X, add)\
                            .then_inc(sem("dve_chain"), 1)
                        eng.wait_ge(sem("dve_chain"), count(sem("dve_chain")))
                        tt(RT[0:8, 0:256], zs[0:8, 256:512], zs[0:8, 768:1024], mul).then_inc(sem("dve_chain"), 1)
                        eng.wait_ge(sem("dve_chain"), count(sem("dve_chain")))
                        V.tensor_reduce(small[0:8, 36:40], ap(RT[0:8, 0:1], [64, 4], [1, 64]), AX.X, add)\
                            .then_inc(sem("own_a"), 1)
                        eng.wait_ge(sem("own_a"), count(sem("own_a")))
                        eng.wait_ge(O.full, O.arrive())
                        o = O.reading
                        V.tensor_tensor_reduce(out=small[0:64, 0:8], in0=o[0:64, 0:8], in1=C("hm64", 64), scale=1.0,
                                               scalar=0.0, op0=mul, op1=add, accum_out=small[0:64, 11:12])\
                            .then_inc(O.free, 1)
                        eng.wait_ge(O.free, count(O.free))
                    if l == 0 and i >= 2:
                        score_a(i - 2)
                    if l == 1 and i == CMP_AT - 1:
                        hx = [BM[:, 0:NC_P], BM[:, 16:16 + NC_P]]
                        x2 = [BM[:, 32:32 + NC_P], BM[:, 48:48 + NC_P]]
                        for kv in range(2):
                            gelu(hx, x2, False)
                            eng.wait_ge(S.full, S.arrive(2))
                            s = S.reading
                            if kv == 0:
                                V.tensor_copy(BM[0:NC_P, 128:256], s[0:NC_P, 0:128]).then_inc(S.free, 2)
                                eng.wait_ge(S.free, count(S.free, 2))
                                rope(BM[0:NC_P, 128:129], 1, HD, 16, C("ropecp", NC_P))
                            else:
                                V.tensor_copy(VCp[0:NC_P, :], s[0:NC_P, 0:128]).then_inc(S.free, 2)
                                eng.wait_ge(S.free, count(S.free, 2))
                        eng.sem_inc(sem("kcp_roped"), 1)
                        count(sem("kcp_roped"))
                eng.sem_inc(sem("roped"), 1)
                count(sem("roped"))
                mark(f"roped{l}", *latest)
                if l == 0:
                    dec_own(64, small[0:32, 9:10])
                    eng.wait_ge(O.full, O.arrive())
                    o = O.reading
                    V.tensor_tensor_reduce(out=small[0:32, 0:4], in0=o[0:32, 0:4], in1=C("hm32", 32), scale=1.0,
                                           scalar=0.0, op0=mul, op1=add, accum_out=small[0:32, 10:11])\
                        .then_inc(O.free, 1)
                    eng.wait_ge(O.free, count(O.free))
                    ts(small[0:32, 16:24], C("bm32", 32), small[0:32, 10:11], None, mul).then_inc(sem("dve_chain"), 1)
                    eng.wait_ge(sem("dve_chain"), count(sem("dve_chain")))
                    eng.wait_ge(S.full, S.arrive(2))
                    s = S.reading
                    ts(ap(SR[0:32, 0:1], [1, ROWS], [ROWS, 128]), ap(s[0:32, 0:1], [128, ROWS], [1, 128]),
                       0.0, None, ALU.max).then_inc(S.free, 2)
                    eng.wait_ge(S.free, count(S.free, 2))
                    ts(SR[0:32, 1024:1025], small[0:32, 9:10], 0.0, None, ALU.max).then_inc(sem("relu_rows"), 1)
                    eng.wait_ge(sem("relu_rows"), count(sem("relu_rows")))
                    score_a(6)
                    score_a(7)
                    eng.sem_inc(sem("scores_a"), 1)
                    count(sem("scores_a"))
                    eng.wait_ge(S.full, S.arrive(2))
                    s = S.reading
                    work = PD[0:8, 0:1025]
                    V.tensor_copy(work[:, 0:1024], s[0:8, :]).then_inc(S.free, 2)
                    eng.wait_ge(S.free, count(S.free, 2))
                    eng.wait_ge(O.full, O.arrive())
                    o = O.reading
                    V.tensor_copy(work[:, 1024:1025], o[0:8, 0:1]).then_inc(O.free, 1)
                    eng.wait_ge(O.free, count(O.free))
                    filler = topk(work, TOPK_S, small[0:8, 52:60])
                    attention(0, units[0][0:8], 0, lambda: fill(filler, 2))
                    for t in (0, 1):
                        nk = 128 * (t + 1)
                        acc = SM[:, t, 0:nk]
                        for j in (0, 1):
                            eng.wait_ge(S.full, S.arrive())
                            s = S.reading
                            for i in (0, 1):
                                w = z[t][:, EVEN["wi"] + 2 * j + i:EVEN["wi"] + 2 * j + i + 1]
                                dst = acc if j + i == 0 else SM[:, t, 256:256 + nk]
                                signal, by = (S.free, 1) if i else (sem("dve_chain"), 1)
                                ts(dst, s[:, i * nk:(i + 1) * nk], 0.0, w, ALU.max, mul).then_inc(signal, by)
                                eng.wait_ge(signal, count(signal, by))
                                if j + i:
                                    tt(acc, acc, dst, add).then_inc(sem("dve_chain"), 1)
                                    eng.wait_ge(sem("dve_chain"), count(sem("dve_chain")))
                        tt(acc, acc, C(f"causal{t}"), add).then_inc(sem("dve_chain"), 1)
                        eng.wait_ge(sem("dve_chain"), count(sem("dve_chain")))
                    gelu([hid], [hid2], True)
                    eng.wait_ge(S.full, S.arrive(2))
                    s = S.reading
                    V.tensor_copy(kc_rows[0:NC_S, :], s[0:NC_S, :]).then_inc(S.free, 2)
                    eng.wait_ge(S.free, count(S.free, 2))
                    rope(kc_rows[0:NC_S, 0:1], NB, HD, 16, C("ropec", NC_S))
                    eng.sem_inc(sem("kc_roped"), 1)
                    count(sem("kc_roped"))
                    for t in (0, 1):
                        nk = 128 * (t + 1)
                        acc = SM[:, t, 0:nk]
                        fill(topk(acc, TOPK_P, stat[:, 32:40]))
                        bm = BM[:, 0:128] if t == 0 else BM[:, 128:384]
                        ts(bm, acc, -2e38, NEG, ALU.is_gt, mul).then_inc(sem("dve_chain"), 1)
                        eng.wait_ge(sem("dve_chain"), count(sem("dve_chain")))
                        tt(bm, bm, C(f"causal{t}"), add).then_inc(sem("dve_chain"), 1)
                        eng.wait_ge(sem("dve_chain"), count(sem("dve_chain")))
                    eng.sem_inc(sem("topk_prompt"), 1)
                    count(sem("topk_prompt"))
                    attention(0, units[0][8:12], 8, lambda: fill(filler, 4))
                    fill(filler)
                    ts(ap(kept_keys[:, 0:1], [128, ROWS], [1, 128]), ap(work[:, 0:1], [1, ROWS], [ROWS, 128]),
                       -2e38, NEG, ALU.is_gt, mul).then_inc(sem("dve_chain"), 1)
                    eng.wait_ge(sem("dve_chain"), count(sem("dve_chain")))
                    ts(small[0:8, 50:51], work[:, 1024:1025], -2e38, NEG, ALU.is_gt, mul)\
                        .then_inc(sem("dve_chain"), 1)
                    eng.wait_ge(sem("dve_chain"), count(sem("dve_chain")))
                    eng.wait_ge(S.full, S.arrive(2))
                    s = S.reading
                    dec_soft(64, s[0:64, :], 1025, 0.125, (1, small[0:64, 11:12]))
                    tt(stat[0:64, 22:23], stat[0:64, 22:23], coef[:, 1:2], mul).then_inc(sem("dve_chain"), 1)
                    eng.wait_ge(sem("dve_chain"), count(sem("dve_chain")))
                    ts(SR[0:64, 0:1025], SR[0:64, 0:1025], stat[0:64, 22:23], None, mul).then_inc(sem("dve_chain"), 1)
                    eng.wait_ge(sem("dve_chain"), count(sem("dve_chain")))
                    dec_new(64, [1024], C("bm64", 64))
                    eng.sem_inc(sem("dec_probs"), 1)
                    count(sem("dec_probs"))
                    V.memset(PD[:, :], 0.0).then_inc(sem("dve_chain"), 1)
                    eng.wait_ge(sem("dve_chain"), count(sem("dve_chain")))
                    gelu([hid], [hid2], True)
                    eng.wait_ge(sem("pair_in"), due("dve", "pair_in"))
                    tt(ap(PD[:, 0:1], [256, ROWS], [36, NB], [1, H]),
                       ap(SA[:, 0:1], [64, ROWS], [8, NB], [2, H]),
                       ap(SA[:, 1:2], [64, ROWS], [8, NB], [2, H]), add)\
                        .then_inc(sem("dve_chain"), 1)
                    eng.wait_ge(sem("dve_chain"), count(sem("dve_chain")))
                    tt(PNT[:, 1, 0:32], ap(PNT[:, 0, 0:1], [2, 32]), ap(PNT[:, 0, 1:2], [2, 32]), add)\
                        .then_inc(sem("pd_pairs"), 1)
                    eng.wait_ge(sem("pd_pairs"), count(sem("pd_pairs")))
                    eng.wait_ge(S.full, S.arrive(2))
                    s = S.reading
                    V.tensor_copy(VC[0:NC_S, :, :], ap(s[0:NC_S, 0:1], [HD, NB], [1, HD])).then_inc(S.free, 2)
                    eng.wait_ge(S.free, count(S.free, 2))
                    head_rows("a", True)
                    dec_finish("a", zs)
                    eng.sem_inc(sem("own_mask"), 1)
                    count(sem("own_mask"))
                    eng.wait_ge(O.full, O.arrive())
                    o = O.reading
                    V.tensor_copy(small[0:32, 51:52], o[0:32, 0:1]).then_inc(O.free, 1)
                    eng.wait_ge(O.free, count(O.free))
                    V.tensor_copy(SR[0:8, 0:1024], kept_keys).then_inc(sem("dec_mask"), 1)
                    eng.wait_ge(sem("dec_mask"), count(sem("dec_mask")))
                    dec_shared("b", zs, 8, True)
                    for t, (_, n) in enumerate(TOK):
                        o = z[t][0:n, 0:512]
                        tt(SM[0:n, 0, 0:512], o, o, mul).then_inc(sem("dve_chain"), 1)
                        eng.wait_ge(sem("dve_chain"), count(sem("dve_chain")))
                        V.tensor_reduce(stat[0:n, 24 + 4 * t:28 + 4 * t], ap(SM[0:n, 0, 0:1], [128, H], [1, 128]),
                                        AX.X, add).then_inc(sem("dve_chain"), 1)
                        eng.wait_ge(sem("dve_chain"), count(sem("dve_chain")))
                        ts(stat[0:n, 24 + 4 * t:28 + 4 * t], stat[0:n, 24 + 4 * t:28 + 4 * t], 1.0 / HD, EPS,
                           mul, add).then_inc(sem("dve_chain"), 1)
                        eng.wait_ge(sem("dve_chain"), count(sem("dve_chain")))
                    eng.sem_inc(sem("o_a"), 1)
                    count(sem("o_a"))
                    eng.wait_ge(sem("a_rms"), due("dve", "a_rms", 3))
                    for t, (_, n) in enumerate(TOK):
                        r = stat[0:n, 24 + 4 * t:28 + 4 * t]
                        V.reciprocal(r, r).then_inc(sem("dve_chain"), 1)
                        eng.wait_ge(sem("dve_chain"), count(sem("dve_chain")))
                        ts(r, r, 1.0 - LAM_INIT, None, mul).then_inc(sem("dve_chain"), 1)
                        eng.wait_ge(sem("dve_chain"), count(sem("dve_chain")))
                        o = ap(z[t][0:n, 0:1], [128, H], [1, 128])
                        tt(o, o, ap(r[:, 0:1], [1, H], [0, 128]), mul).then_inc(sem("dve_chain"), 1)
                        eng.wait_ge(sem("dve_chain"), count(sem("dve_chain")))
                        g = z[t][0:n, EVEN["ga"]:EVEN["ga"] + 512]
                        tt(g, g, z[t][0:n, 0:512], mul).then_inc(sem("dve_chain"), 1)
                        eng.wait_ge(sem("dve_chain"), count(sem("dve_chain")))
                else:
                    attention(1, units[1], 12)
                    eng.wait_ge(S.full, S.arrive(2))
                    s = S.reading
                    dec_soft(32, s[0:32, 0:NC_S], NC_S, HD ** -0.5, (0, None))
                    ts(SR[0:32, 0:NC_S], SR[0:32, 0:NC_S], stat[0:32, 22:23], None, mul).then_inc(sem("dec_probs"), 1)
                    eng.wait_ge(sem("dec_probs"), count(sem("dec_probs")))
                    zero_pd()
                    eng.wait_ge(sem("imp_T"), due("dve", "imp_T"))
                    V.tensor_reduce(small[0:NC_S, 24:32], ap(SA[0:NC_S, 0:1], [4, NB], [1, H]), AX.X, add)\
                        .then_inc(sem("imp_in"), 1)
                    eng.wait_ge(sem("imp_in"), count(sem("imp_in")))
                    eng.wait_ge(O.full, O.arrive())
                    o = O.reading
                    imp = RT[0:8, 0:NSEL]
                    tt(imp, o[0:8, 0:NSEL], C("bonus", 8), add).then_inc(O.free, 1)
                    eng.wait_ge(O.free, count(O.free))
                    fill(topk(imp, 16, stat[0:8, 32:40]))
                    ts(imp, imp, -2e38, NEG, ALU.is_gt, mul).then_inc(sem("dve_chain"), 1)
                    eng.wait_ge(sem("dve_chain"), count(sem("dve_chain")))
                    V.tensor_copy(ap(SR[0:8, 0:1], [128, ROWS], [8, 16], [1, 8]),
                                  ap(imp[:, 0:1], [0, ROWS], [1, 16], [0, 8]))\
                        .then_inc(sem("dve_chain"), 1)
                    eng.wait_ge(sem("dve_chain"), count(sem("dve_chain")))
                    head_rows("cmp", False)
                    dec_finish("cmp", zs)
                    eng.sem_inc(sem("dec_mask"), 1)
                    count(sem("dec_mask"))
                    dec_shared("c", zs, 8, True)
                    dec_shared("w", zs, 4, False)
                    for g in range(3):
                        q, k = ODD[f"qd{g}"], ODD[f"kd{g}"]
                        tt(SM[0:8, 0, 0:512], zs[0:8, q:q + 512], zs[0:8, k:k + 512], mul)\
                            .then_inc(sem("dve_chain"), 1)
                        eng.wait_ge(sem("dve_chain"), count(sem("dve_chain")))
                        V.tensor_reduce(small[0:8, 32 + 4 * g:36 + 4 * g],
                                        ap(SM[0:8, 0, 0:1], [128, H], [1, 128]), AX.X, add)\
                            .then_inc(sem("dve_chain"), 1)
                        eng.wait_ge(sem("dve_chain"), count(sem("dve_chain")))
                    eng.sem_inc(sem("own_d"), 1)
                    count(sem("own_d"))
                    eng.wait_ge(O.full, O.arrive())
                    o = O.reading
                    tt(ap(small[0:32, 0:1], [4, 3], [1, H]), ap(o[0:32, 0:1], [4, 3], [1, H]),
                       ap(C("hm32", 32)[:, 0:1], [0, 3], [1, H]), mul).then_inc(O.free, 1)
                    eng.wait_ge(O.free, count(O.free))
                    V.tensor_reduce(small[0:32, 12:15], ap(small[0:32, 0:1], [4, 3], [1, H]), AX.X, add)\
                        .then_inc(sem("dve_chain"), 1)
                    eng.wait_ge(sem("dve_chain"), count(sem("dve_chain")))
                    for g in range(3):
                        eng.wait_ge(*arrival[f"dk_{g}"])
                        slot = slot_of(f"dk_{g}")
                        n = DN[g]
                        for b in range(NB):
                            eng.wait_ge(O.full, O.arrive())
                            o = O.reading
                            k = slot[0:n, b * 512:(b + 1) * 512]
                            tt(k, k, o[0:n, :], mul).then_inc(O.free, 1)
                            eng.wait_ge(O.free, count(O.free))
                        V.tensor_reduce(SA[0:n, g * 32:(g + 1) * 32], ap(slot[0:n, 0:1], [128, 32], [1, 128]),
                                        AX.X, add).then_inc(sem("dve_chain"), 1)
                        eng.wait_ge(sem("dve_chain"), count(sem("dve_chain")))
                        release(f"dk_{g}", *latest)
                    eng.sem_inc(sem("scores_d"), 1)
                    count(sem("scores_d"))
                    eng.wait_ge(S.full, S.arrive(2))
                    s = S.reading
                    V.memset(SR[0:32, 0:384], BIG).then_inc(sem("dve_chain"), 1)
                    eng.wait_ge(sem("dve_chain"), count(sem("dve_chain")))
                    for g in range(3):
                        signal, by = (S.free, 2) if g == 2 else (sem("dve_chain"), 1)
                        ts(SR[0:32, g * 128:g * 128 + DN[g]], s[0:32, g * 128:g * 128 + DN[g]], -(HD ** -0.5),
                           None, mul).then_inc(signal, by)
                        eng.wait_ge(signal, count(signal, by))
                    dec_soft(32, None, 387, HD ** -0.5, (3, small[0:32, 12:15]))
                    ts(SR[0:32, 0:387], SR[0:32, 0:387], stat[0:32, 22:23], None, mul).then_inc(sem("dve_chain"), 1)
                    eng.wait_ge(sem("dve_chain"), count(sem("dve_chain")))
                    dec_new(32, [384, 385, 386], C("bm32", 32))
                    eng.sem_inc(sem("dec_probs"), 1)
                    count(sem("dec_probs"))
                    zero_pd()
                    head_rows("d", True)
                    dec_finish("d", zs)
                    for t, (_, n) in enumerate(TOK):
                        g = z[t][0:n, ODD["gc"]:ODD["gc"] + 512]
                        tt(g, g, z[t][0:n, 0:512], mul).then_inc(sem("dve_chain"), 1)
                        eng.wait_ge(sem("dve_chain"), count(sem("dve_chain")))
                for t in range(3):
                    eng.sem_inc(sem("mix"), 1)
                    count(sem("mix"))
                eng.sem_inc(sem("y_free"), 1)
                count(sem("y_free"))
                mark(f"mixed{l}", *latest)
                for t, (_, n) in enumerate(TOK):
                    r = norm(t)
                    eng.wait_ge(sem("post_in"), 16 * (l + 1))
                    stt(Y[t][0:n], Y[t][0:n], r, NW[0:n, :], mul, mul).then_inc(sem("dve_chain"), 1)
                    eng.wait_ge(sem("dve_chain"), count(sem("dve_chain")))
                    tt(X[0:n, t, :], X[0:n, t, :], Y[t][0:n], add).then_inc(sem("x_next"), 1)
                    eng.wait_ge(sem("x_next"), count(sem("x_next")))
                    mark(f"x_done{l}_{t}", *latest)
                    if l == 0:
                        xn(1, t)

        @block.sync
        def _(sp):
            small_in = sem("const_in")
            for out, src in SMALL:
                sp.dma_start(out, src, allow_slow_non_contiguous=True).then_inc(small_in, 16)
            def load_norm(dst, name, l, s):
                w = ins[name][l]
                sp.dma_start(dst, bass.AP(w.tensor, w.offset, [[0, 128], [1, D]])).then_inc(sem(s), 16)

            load_norm(NWP, "pre_norm", 0, "pre_in")
            load_norm(NW[:, :], "post_norm", 0, "post_in")
            last = {chunks(l)[-1][0]: l for l in (0, 1)}
            for i, (name, queue, parts) in enumerate(items):
                if queue == "sp":
                    stream(sp, i, name, parts)
                if name == "wout0_512":
                    sp.wait_ge(*marks["mixed0"])
                    load_norm(NWP, "pre_norm", 1, "pre_in")
                if name == "win1_2048":
                    sp.wait_ge(*marks["x_done0_2"])
                    load_norm(NW[:, :], "post_norm", 1, "post_in")
                for l, outs_l in ((0, OUTS0), (1, OUTS1)):
                    if name == f"win{l}_{chunks(l)[-1][0]}":
                        sp.wait_ge(*marks[f"roped{l}"])
                        for out, src in outs_l:
                            sp.dma_start(out, src).then_inc(sem("out0"), 16)
            for t in range(2):
                sp.wait_ge(*marks[f"x_done1_{t}"])
                sp.dma_start(outs["y_prompt"][0, t * 128:(t + 1) * 128, :], X[:, t, :]).then_inc(sem("out1"), 16)
            sp.wait_ge(*marks["x_done1_2"])
            sp.dma_start(outs["y_sample"].rearrange("b o d -> b (o d)"), X[0:8, 2, :]).then_inc(sem("out1"), 16)
            sp.wait_ge(sem("out1"), 48)
            sp.wait_ge(sem("out0"), 16 * (len(OUTS0) + len(OUTS1)))
            sp.wait_ge(sem("moved"), 16 * len(MOVES))

        @block.gpsimd
        def _(pool):
            pool.wait_ge(sem("index"), 1)
            moves = list(MOVES)
            for i, (name, queue, parts) in enumerate(items):
                if queue == "pool":
                    stream(pool, i, name, parts)
                if i > order["idx_0"]:
                    wait_slot(pool, i)
                    for _ in range(3 if name.startswith("win1") else 1):
                        if moves:
                            dst, src = moves.pop(0)
                            pool.dma_start(dst, src).then_inc(sem("moved"), 16)
            for dst, src in moves:
                pool.dma_start(dst, src).then_inc(sem("moved"), 16)


NAMES = ("x_prompt", "x_sample", "cache_a_k", "cache_a_v", "cache_b_k", "cache_b_v", "cache_b_idx",
         "cache_c_cmp_k", "cache_c_cmp_v", "cache_c_sel_k", "cache_c_sel_v", "state_c_win_k", "state_c_win_v",
         "state_d_k0", "state_d_v0", "state_d_k1", "state_d_v1", "state_d_k2", "state_d_v2", "page_table",
         "pre_norm", "post_norm", "w_in_even", "w_out_even", "diff_lambda", "w_in_odd", "w_out_odd", "cmp_pos",
         "cmp_w1", "cmp_w2")


def out_shapes():
    seq, dec = 256, NB
    o = [("y_prompt", (1, seq, D)), ("y_sample", (dec, 1, D))]
    for tag, n, t in (("p_", 1, seq), ("s_", dec, 1)):
        even = [("a_k", (1, n, t, H, 2, 64)), ("a_v", (1, n, t, H, HD)), ("b_k", (1, n, t, HD)),
                ("b_v", (1, n, t, HD)), ("b_idx", (1, n, t, 64))]
        o += [(tag + a, s) for a, s in even]
    def odd(tag, n, t, win, ds):
        r = [(tag + a, (1, n, t, HD)) for a in ("c_cmp_k", "c_cmp_v", "c_sel_k", "c_sel_v")]
        r += [(tag + a, (1, n, win, HD)) for a in ("c_win_k", "c_win_v")]
        for g, w in enumerate(ds):
            r += [(tag + f"d_{kv}{g}", (1, n, w, H, HD)) for kv in "kv"]
        return r
    p_even = [x for x in o if x[0].startswith("p_")]
    s_even = [x for x in o if x[0].startswith("s_")]
    head = o[:2]
    p_odd = odd("p_", 1, seq, min(WIN, seq), [min(w, seq) for w, _ in PAIRS])
    s_odd = odd("s_", dec, 1, WIN, [min(w, DW[g] + 1) for g, (w, _) in enumerate(PAIRS)])
    return head + p_even + p_odd + s_even + s_odd


def kernel(**inputs):
    import concourse.bacc as bacc
    from concourse.bass_utils import run_bass_kernel_spmd

    nc = bacc.Bacc("TRN2", target_bir_lowering=False, num_devices=1)
    arrays, ins, outs = {}, {}, {}
    for name in NAMES + ("const",):
        a = constants() if name == "const" else np.ascontiguousarray(inputs[name])
        arrays[f"in_{name}"] = a
        ins[name] = nc.dram_tensor(f"in_{name}", a.shape, mybir.dt.from_np(a.dtype), kind="ExternalInput").ap()
    shapes = out_shapes()
    for name, shape in shapes:
        outs[name] = nc.dram_tensor(f"out_{name}", shape, F32, kind="ExternalOutput").ap()
    build(nc, ins, outs)
    r = run_bass_kernel_spmd(nc, [arrays], core_ids=[0])
    return tuple(r.results[0][f"out_{name}"] for name, _ in shapes)
```

```python
import math
from contextlib import ExitStack

import numpy as np
import concourse.bass as bass
from concourse import mybir

F32 = mybir.dt.float32
I32 = mybir.dt.int32
ALU = mybir.AluOpType
ACT = mybir.ActivationFunctionType
AX = mybir.AxisListType

D = 1024
KT = D // 128
HD = 128
H = 4
NB = 8
L = 1024
PAGE = 128
ROWS = 8
SUB = PAGE // ROWS
NPG = L // PAGE
EPS = 1e-6
NEG = -1e30
BIG = 3e38
TOK = ((0, 128), (128, 128), (256, 8))
EVEN = dict(qa=0, ka=512, va=1024, ga=1536, qb=2048, kb=2560, vb=2688, gb=2816, qi=3328, ki=3584, wi=3648)
E_EVEN = 3652
ODD = dict(qc=0, kcr=512, vcr=640, ksel=768, vsel=896, kwin=1024, vwin=1152, gl=1280, gc=1292, gd=6412)
for _g in range(3):
    ODD[f"qd{_g}"], ODD[f"kd{_g}"], ODD[f"vd{_g}"] = (1804 + 1536 * _g + 512 * _j for _j in range(3))
E_ODD = 6924
PAIRS = ((128, 1), (512, 4), (2048, 16))
DW = tuple(min(w, L) for w, _ in PAIRS)
DN = tuple(w // d for w, (_, d) in zip(DW, PAIRS))
CB, CS, CH = 32, 16, 256
NC_S, NC_P = 63, 15
NSEL = 17
WIN = 512
TOPK_P, TOPK_S = 64, 256
CMP_AT = 4
SCORE_D = {7: 0, 10: 1, 13: 2}
STEPS = 3
MOVES_EARLY = {"rows1_1": 11, "w1s1_1": 8}
PAUSE, END = "pause", "end"
LAM_INIT = 0.8 - 0.6 * math.exp(0.0)
GELU_C = math.sqrt(2.0 / math.pi)
SLOTS = 3
SLOT = 4096

CONST = {}


def _layout():
    at = 0
    for name, n in (("ident", 128), ("causal0", 128), ("causal1", 256), ("dil0", 384), ("dil1", 768),
                    ("cmp0", 15), ("cmp1", 15), ("cmpok", 2), ("rope", 144), ("ropec", 32), ("ropecp", 32),
                    ("e64", 64), ("e32", 32), ("hm64", 8), ("bm64", 8), ("hm32", 4), ("bm32", 8),
                    ("one8", 8), ("fold", 16), ("mzero", 1), ("mone", 1), ("overlap", 17), ("bonus", 17), ("sub", 1)):
        CONST[name] = (at, n)
        at += n
    return at


N_CONST = _layout()


def constants():
    c = np.zeros((128, N_CONST), np.float32)

    def put(name, a):
        at, n = CONST[name]
        c[:a.shape[0], at:at + n] = a

    def table(pos, half):
        freqs = np.float32(500000.0) ** (-np.arange(half, dtype=np.float32) / np.float32(half))
        ang = (pos.astype(np.float32)[:, None] * freqs.astype(np.float32)).astype(np.float32)
        return np.concatenate([np.cos(ang), np.sin(ang)], 1)

    p = np.arange(128)
    put("ident", np.eye(128))
    for t in range(2):
        q, k = p[:, None] + 128 * t, np.arange(128 * (t + 1))[None]
        put(f"causal{t}", np.where(k <= q, 0.0, NEG))
        put(f"dil{t}", np.concatenate(
            [np.where((k <= q) & ((q - k) % d == 0) & (q - k <= w), 0.0, NEG) for w, d in PAIRS], 1))
        put(f"cmp{t}", np.where(np.arange(NC_P)[None] * CS + CB - 1 <= q, 0.0, NEG))
    put("cmpok", np.stack([(p >= CB - 1), p >= 0], 1))
    put("rope", np.concatenate([np.concatenate([table(pos, 8), table(pos, 16)], 1)
                                for pos in (p, p + 128, np.full(128, L))], 1))
    put("ropec", table(np.arange(NC_S) * CS + CB - 1, 16))
    put("ropecp", table(np.arange(NC_P) * CS + CB - 1, 16))
    b = np.arange(NB)
    put("e64", b[:, None] == np.arange(64)[None] // 8)
    put("e32", b[:, None] == np.arange(32)[None] // 4)
    r = np.arange(64)
    put("hm64", r[:, None] % 8 == b[None])
    put("bm64", r[:, None] // 8 == b[None])
    put("mzero", (r[:, None] % 2 == 0))
    put("mone", (r[:, None] % 2 == 1))
    put("hm32", p[:, None] % 4 == np.arange(4)[None])
    put("bm32", p[:, None] % 32 // 4 == b[None])
    put("one8", np.eye(8))
    put("fold", p[:, None] % 32 == np.arange(16)[None])
    cs, ss = np.arange(NC_S)[:, None] * CS, np.arange(NSEL)[None] * 64
    put("overlap", (cs < ss + 64) & (cs + CB > ss))
    j = np.arange(NSEL)
    put("bonus", np.broadcast_to(np.where((j == 0) | (j >= NSEL - 2), 1e4, 0.0), (8, NSEL)))
    put("sub", p[:, None] % SUB)
    return c


class Ring:

    def __init__(self, full, free, view, banks):
        self.full, self.free, self.view, self.banks = full, free, view, banks
        self.made = self.read = 0

    def claim(self, k=1):
        at = self.made % self.banks
        self.made += k
        self.filling = self.view[:, at * 512:(at + k) * 512]
        return max(0, self.made - self.banks)

    def arrive(self, k=1):
        at = self.read % self.banks
        self.read += k
        self.reading = self.view[:, at * 512:(at + k) * 512]
        return self.read


def ap(view, *dims, at=0):
    return bass.AP(view.tensor, view.offset + at, [list(view.ap[0])] + [list(d) for d in dims])


def build(nc, ins, outs):
    ctx = ExitStack()
    with ctx:
        def sb(name, shape, dt=F32):
            return ctx.enter_context(nc.sbuf_tensor(name, shape, dt))

        sems = {}

        def sem(name):
            if name not in sems:
                sems[name] = ctx.enter_context(nc.semaphore(name))
            return sems[name]

        const = sb("const", [128, N_CONST])

        def C(name, rows=128):
            at, n = CONST[name]
            return const[0:rows, at:at + n]

        ring = sb("ring", [128, SLOTS * SLOT])
        Z = sb("Z", [128, 3 * E_ODD])
        XB = sb("XB", [128, 2064 + KT * 32])
        xT = XB[:, 0:2048].rearrange("p (k c) -> p k c", k=KT)
        xTs = XB[:, 2064:2064 + KT * 32].rearrange("p (k c) -> p k c", k=KT)
        X = sb("X", [128, 3, D])
        NW = sb("NW", [128, D])
        PD = sb("PD", [128, 2048])
        QD = sb("QD", [128, NB, 32])
        QF = sb("QF", [128, 32])
        KN = sb("KN", [128, 8])
        QK = sb("QK", [128, 6, 512])
        flat = QK[:, :, :].rearrange("p a b -> p (a b)")
        SR = [m[0:64, 0:1040] for m in (flat, XB)]
        IR = XB[0:32, 0:1040]
        KTs = [m[:, 1040:2064].rearrange("p (a b) -> p a b", a=2) for m in (flat, XB)]
        NWP = flat[:, 2048:3072]
        SM = sb("SM", [128, 2, 768])
        HR = [SM[:, 0, 0:512], PD[:, 0:512]]
        HS = [SM[0:8, 0, 0:512], PD[0:8, 512:1024]]
        SA = sb("SA", [128, 512])
        PT = sb("PT", [128, 768])
        BM = sb("BM", [128, 384])
        kcT = sb("kcT", [128, NB, 64])
        VC = sb("VC", [64, NB, HD])
        kcTp = sb("kcTp", [128, 16])
        VCp = sb("VCp", [16, HD])
        posT = sb("posT", [128, 64])
        W2 = sb("W2", [128, 2, 2, HD])
        bias1 = sb("bias1", [128, 2, 2])
        lamr = SA[:, 0:256]
        lam = sb("lam", [128, 8])
        coef = sb("coef", [64, 2])
        stat = sb("stat", [128, 80])
        small = sb("small", [64, 64])
        PN = sb("PN", [64, 3, 8])
        PNT = sb("PNT", [8, 3, 64])
        RT = sb("RT", [128, 256])
        ptab = sb("ptab", [128, NB], I32)
        index = sb("index", [128, NB], I32)
        posr = RT[0:64, 0:128]

        psum = ctx.enter_context(nc.psum_tensor("psum", [128, 8 * 512], F32))
        T = Ring(sem("T_full"), sem("T_free"), psum[:, 0:1024], 2)
        S = Ring(sem("S_full"), sem("S_free"), psum[:, 1024:2048], 2)
        P = Ring(sem("P_full"), sem("P_free"), psum[:, 2048:3072], 2)
        Q = Ring(sem("Q_full"), sem("Q_free"), psum[:, 2048:3072], 2)
        O = Ring(sem("O_full"), sem("O_free"), psum[:, 3072:4096], 2)

        items, place, released = [], {}, {}

        def item(name, queue, parts):
            place[name] = (len(items) % SLOTS, None)
            items.append((name, queue, parts))

        def direct(src, rows, cols):
            return ("direct", src, rows, 0, cols)

        w_in = {0: ins["w_in_even"], 1: ins["w_in_odd"]}
        w_out = {0: ins["w_out_even"], 1: ins["w_out_odd"]}
        width = {0: E_EVEN, 1: E_ODD}

        def chunks(l):
            return [(c, min(512, width[l] - c)) for c in range(0, width[l], 512)]

        def weights(kind, l, w, cs):
            for c, n in cs:
                src = w[0].rearrange("(k p) n -> p k n", p=128)[:, :, c:c + n]
                item(f"{kind}{l}_{c}", "sp", [("w", src, n)])

        def gathered(name, cache, cols, per_slot):
            for s in range(0, NB, per_slot):
                item(f"{name}_{s // per_slot}", "pool",
                     [("gather", cache, b, (b - s) * ROWS * cols, ROWS * cols) for b in range(s, s + per_slot)])

        def w1(tag, kv, half):
            src = ins["cmp_w1"][0, kv, half * 16:half * 16 + 16].rearrange("r d h -> d r h")
            item(f"{tag}{kv}_{half}", "sp", [("full", src)])

        gathered("rows0", ins["cache_c_cmp_k"], HD, 4)
        def d_rows(kv, g):
            src = ins[f"state_d_{kv}{g}"][0].rearrange("b (n j) h e -> n j b (h e)", j=PAIRS[g][1])[:, 0]
            item(f"d{kv}_{g}", "sp", [("rows", src, DN[g])])

        def gathered_one(name, cache, b):
            item(f"{name}_{b}", "pool", [("gather", cache, b, 0, ROWS * 512)])

        for i, c in enumerate(chunks(0)):
            weights("win", 0, w_in[0], [c])
            if i >= 2:
                gathered_one("ak", ins["cache_a_k"], i - 2)
        gathered_one("ak", ins["cache_a_k"], 6)
        w1("w1s", 0, 0)
        gathered("idx", ins["cache_b_idx"], 64, 8)
        gathered_one("ak", ins["cache_a_k"], 7)
        w1("w1s", 0, 1)
        gathered("rows1", ins["cache_c_cmp_v"], HD, 4)
        w1("w1s", 1, 0)
        w1("w1s", 1, 1)
        gathered("av", ins["cache_a_v"], 512, 1)
        gathered("bk", ins["cache_b_k"], HD, 4)
        gathered("bv", ins["cache_b_v"], HD, 4)
        weights("wout", 0, w_out[0], [(0, 512), (512, 512)])
        for i, c in enumerate(chunks(1)):
            weights("win", 1, w_in[1], [c])
            if i in SCORE_D:
                d_rows("k", SCORE_D[i])
            if i == CMP_AT:
                for kv in range(2):
                    for half in range(2):
                        w1("w1p", kv, half)
        gathered("ck", ins["cache_c_sel_k"], HD, 4)
        gathered("cv", ins["cache_c_sel_v"], HD, 4)
        for n, w in (("wk", "state_c_win_k"), ("wv", "state_c_win_v")):
            item(n + "_0", "sp", [("full", ins[w][0].rearrange("b (p r) d -> p b (r d)", r=4))])
        for g in range(3):
            d_rows("v", g)
        weights("wout", 1, w_out[1], [(0, 512), (512, 512)])
        order = {n: i for i, (n, _, _) in enumerate(items)}
        arrival, arrived = {}, {}
        for i, (n, queue, parts) in enumerate(items):
            s = f"slot_{'loaded' if queue == 'sp' else 'gathered'}{i % SLOTS}"
            arrived[s] = arrived.get(s, 0) + 16 * len(parts)
            arrival[n] = (sem(s), arrived[s])


        def slot_of(name):
            s = order[name] % SLOTS
            return ring[:, s * SLOT:(s + 1) * SLOT]

        level, seen, marks, latest = {}, {}, {}, [None, 0]

        def count(s, by=1):
            level[s.name] = level.get(s.name, 0) + by
            latest[:] = [s, level[s.name]]
            return level[s.name]

        def due(who, name, k=1):
            seen[who, name] = seen.get((who, name), 0) + k
            return seen[who, name]

        def mark(name, s, value):
            marks[name] = (s, value)


        def release(name, s, value):
            released[name] = (s, value)



        zt = {0: [Z[:, t * E_EVEN:(t + 1) * E_EVEN] for t in range(3)],
              1: [Z[:, t * E_ODD:(t + 1) * E_ODD] for t in range(3)]}
        R0 = 3 * E_EVEN
        rowsT = Z[:, R0:R0 + 8208]
        Y = [Z[:, R0 + t * D:R0 + (t + 1) * D] for t in range(3)]
        kc_rows = Z[:, R0 + 8208:R0 + 8208 + 1024]
        hid = XB[:, 0:1024]
        hid2 = XB[:, 1024:2048]
        kept_keys = SM[:, :, :].rearrange("p a c -> p (a c)")[0:8, 512:1536]

        preps, units = {0: [], 1: []}, {0: [], 1: []}
        prep_n = [0]

        def prep(l, blocks, rows):
            n = prep_n[0]
            prep_n[0] += 1
            preps[l].append(dict(n=n, at=len(units[l]), blocks=blocks, rows=rows, slot=n % 6))
            return n % 6, n

        def unit(l, **u):
            u["deps"] = sorted(set(u["deps"]))
            units[l].append(u)

        sc = HD ** -0.5
        for h in range(H):
            s, n = prep(0, [(t, EVEN["qa"] + 128 * h, 128) for t in (0, 1)]
                        + [(t, EVEN["ka"] + 128 * h, 128) for t in (0, 1)], 128)
            for t in (0, 1):
                nk = 128 * (t + 1)
                unit(0, kind="a", t=t, h=h, nk=nk, maps=2, banks=2, scale=0.125, mask=C(f"causal{t}"),
                     scores=[(m * 512, QK[64 * m:64 * m + 64, s, t * 128:t * 128 + 128],
                              QK[64 * m:64 * m + 64, s, 256:256 + nk]) for m in (0, 1)],
                     deps=[n], pmaps=1, kt=t + 1, kw=128,
                     v=[[zt[0][k][:, EVEN["va"] + 128 * h:EVEN["va"] + 128 * h + 128] for k in range(t + 1)]])

        def pair_units(l, kind, q, k, v, mask, deps_k):
            ks, kn = deps_k
            for h in (0, 2):
                s, n = prep(l, [(t, q + 128 * (h + j), 128) for j in (0, 1) for t in (0, 1)], 128)
                for t in (0, 1):
                    nk = 128 * (t + 1)
                    unit(l, kind=kind, t=t, h=h, nk=nk, maps=2, banks=1, scale=sc, mask=mask[t],
                         scores=[(m * nk, QK[:, s, m * 256 + t * 128:m * 256 + t * 128 + 128],
                                  QK[:, ks, 0:nk]) for m in (0, 1)],
                         deps=[n, kn], pmaps=2, kt=t + 1, kw=128,
                         v=[[zt[l][kk][:, v:v + 128] for kk in range(t + 1)]] * 2)

        kb_dep = prep(0, [(t, EVEN["kb"], 128) for t in (0, 1)], 128)
        pair_units(0, "b", EVEN["qb"], EVEN["kb"], EVEN["vb"], [BM[:, 0:128], BM[:, 128:384]], kb_dep)
        cs = [prep(1, [(t, ODD["qc"] + 128 * (h + j), 128) for j in (0, 1) for t in (0, 1)], 128) for h in (0, 2)]
        for t in (0, 1):
            unit(1, kind="cmp", t=t, h=0, nk=NC_P, maps=4, banks=1, scale=sc, mask=C(f"cmp{t}"),
                 scores=[(h * NC_P, QK[:, cs[h // 2][0], (h % 2) * 256 + t * 128:(h % 2) * 256 + t * 128 + 128],
                          kcTp[:, 0:NC_P]) for h in range(H)],
                 deps=[cs[0][1], cs[1][1]], pmaps=4, kt=1, kw=NC_P, v=[[VCp[0:NC_P, :]]] * 4)
        mc = [C("causal0"), C("causal1")]
        for kind in ("sel", "win"):
            kd = prep(1, [(t, ODD["k" + kind], 128) for t in (0, 1)], 128)
            ks, kn = kd
            for h in (0, 2):
                s, n = cs[h // 2]
                for t in (0, 1):
                    nk = 128 * (t + 1)
                    unit(1, kind=kind, t=t, h=h, nk=nk, maps=2, banks=1, scale=sc, mask=mc[t],
                         scores=[(m * nk, QK[:, s, m * 256 + t * 128:m * 256 + t * 128 + 128],
                                  QK[:, ks, 0:nk]) for m in (0, 1)],
                         deps=[n, kn], pmaps=2, kt=t + 1, kw=128,
                         v=[[zt[1][kk][:, ODD["v" + kind]:ODD["v" + kind] + 128] for kk in range(t + 1)]] * 2)
        while prep_n[0] % 6:
            prep_n[0] += 1
        for h in range(H):
            s3 = [prep(1, [(t, ODD[f"qd{g}"] + 128 * h, 128) for t in (0, 1)]
                       + [(t, ODD[f"kd{g}"] + 128 * h, 128) for t in (0, 1)], 128) for g in range(3)]
            for t in (0, 1):
                nk = 128 * (t + 1)
                unit(1, kind="d", t=t, h=h, nk=3 * nk, maps=1, banks=2, scale=sc, mask=C(f"dil{t}"),
                     scores=[(g * nk, QK[:, s3[g][0], t * 128:t * 128 + 128], QK[:, s3[g][0], 256:256 + nk])
                             for g in range(3)],
                     deps=[n for _, n in s3], pmaps=1, kt=3 * (t + 1), kw=128,
                     v=[[zt[1][kk][:, ODD[f"vd{g}"] + 128 * h:ODD[f"vd{g}"] + 128 * h + 128]
                         for g in range(3) for kk in range(t + 1)]])

        def fill(steps, n=1000):
            for _ in range(n):
                step = next(steps, END)
                if step == END or (step == PAUSE and n < 1000):
                    break

        GATES = {0: {3: ["ga"], 6: ["gb"]}, 1: {3: ["gc"], 13: ["gd"]}}
        ROTATED = {0: {1: [(EVEN["qa"], 16, 64, 8)], 5: [(EVEN["qb"], 5, 128, 16)], 7: [(EVEN["qi"], 5, 64, 8)]},
                   1: {0: [(ODD["qc"], 4, 128, 16)], 2: [(ODD["ksel"], 2, 256, 16)], 5: [(ODD["qd0"], 8, 128, 16)],
                       8: [(ODD["qd1"], 8, 128, 16)], 11: [(ODD["qd2"], 8, 128, 16)]}}
        FIRST_UNIT = {0: 0, 8: 8, 12: 0}

        def wait_slot(eng, i):
            if i >= SLOTS:
                eng.wait_ge(*released[items[i - SLOTS][0]])

        def stream(eng, i, name, parts):
            wait_slot(eng, i)
            slot = ring[:, (i % SLOTS) * SLOT:(i % SLOTS + 1) * SLOT]
            arrived = arrival[name][0]
            for part in parts:
                if part[0] == "w":
                    _, src, n = part
                    eng.dma_start(ap(slot[:, 0:1], [n, KT], [1, n]), src).then_inc(arrived, 16)
                elif part[0] == "full":
                    _, src = part
                    a, b = src.shape[1:]
                    eng.dma_start(ap(slot[:, 0:1], [b, a], [1, b]), src).then_inc(arrived, 16)
                elif part[0] == "rows":
                    _, src, n = part
                    eng.dma_start(ap(slot[0:n, 0:1], [512, NB], [1, 512]), src).then_inc(arrived, 16)
                else:
                    _, cache, b, at, n = part
                    rows = bass.AP(cache.tensor, cache.offset, [[n, cache.shape[1] * SUB], [1, n]])
                    nc.gpsimd.indirect_dma_start(out=slot[:, at:at + n], out_offset=None, in_=rows,
                                                 in_offset=bass.IndirectOffsetOnAxis(ap=index[:, b:b + 1], axis=0))\
                        .then_inc(arrived, 16)

        SMALL = [(const[:, :], ins["const"]),
                 (X[:, 0:2, :], ins["x_prompt"][0].rearrange("(t p) d -> p t d", p=128)),
                 (X[0:8, 2, :], ins["x_sample"].rearrange("b o d -> b (o d)")),
                 (W2[:, :, :, :].rearrange("p k h d -> p (k h) d"),
                  ins["cmp_w2"][0].rearrange("k (h p) d -> p (k h) d", p=128)),
                 (posr, ins["cmp_pos"][0].rearrange("k r d -> (k r) d")),
                 (lamr[:, :], bass.AP(ins["diff_lambda"].tensor, ins["diff_lambda"].offset, [[0, 128], [1, 256]]))]
        table = ins["page_table"]
        for pg in range(NPG):
            SMALL.append((ptab[pg * SUB:(pg + 1) * SUB, :],
                          bass.AP(table.tensor, table.offset + pg, [[0, SUB], [NPG, NB]])))
        N_SMALL = len(SMALL)

        OUTS = {0: [], 1: []}

        def state(l, name, c, n):
            o = outs["p_" + name]
            keep = o.shape[2]
            o2 = bass.AP(o.tensor, o.offset, [[n, keep], [1, n]])
            for t in range(2):
                if keep == 128 and t == 0:
                    continue
                at = t * 128 - (256 - keep)
                OUTS[l].append((o2[at:at + 128, :], zt[l][t][:, c:c + n]))
            o = outs["s_" + name]
            rows = o.shape[2]
            OUTS[l].append((bass.AP(o.tensor, o.offset + (rows - 1) * n, [[rows * n, NB], [1, n]]),
                            zt[l][2][0:8, c:c + n]))

        for name, c, n in (("a_k", "ka", 512), ("a_v", "va", 512), ("b_k", "kb", 128), ("b_v", "vb", 128),
                           ("b_idx", "ki", 64)):
            state(0, name, EVEN[c], n)
        for name, c in (("c_cmp_k", "kcr"), ("c_cmp_v", "vcr"), ("c_sel_k", "ksel"), ("c_sel_v", "vsel"),
                        ("c_win_k", "kwin"), ("c_win_v", "vwin")):
            state(1, name, ODD[c], 128)
        for g in range(3):
            state(1, f"d_k{g}", ODD[f"kd{g}"], 512)
            state(1, f"d_v{g}", ODD[f"vd{g}"], 512)
        OUTS0, OUTS1 = OUTS[0], OUTS[1]

        MOVES = []
        for name, n in [(f"d_{kv}{g}", 512) for g in (2, 1, 0) for kv in "kv"] + [("c_win_k", 128), ("c_win_v", 128)]:
            src, dst = ins["state_" + name], outs["s_" + name]
            old, new = src.shape[2], dst.shape[2]
            kept = new - 1
            for b in range(NB):
                m = kept * n // 16
                MOVES.append((bass.AP(dst.tensor, dst.offset + b * new * n, [[m, 16], [1, m]]),
                              bass.AP(src.tensor, src.offset + (b * old + old - kept) * n, [[m, 16], [1, m]])))

        block = ctx.enter_context(nc.Block())

        @block.tensor
        def _(pe):
            mm = nc.tensor.matmul

            def tr(out, in_):
                n = in_.shape[0]
                return nc.tensor.transpose(out, in_, C("ident", n)[:, 0:n])

            def folded(kv, tag, lhs, m, rs=range(CB)):
                pe.wait_ge(T.free, T.claim())
                out = T.filling
                for r in rs:
                    if r % 16 == 0:
                        pe.wait_ge(*arrival[f"{tag}{kv}_{r // 16}"])
                        w = slot_of(f"{tag}{kv}_{r // 16}")
                    g = 32 * (r % 4)
                    last = mm(out[g:g + m, 0:CH], lhs(r), w[:, (r % 16) * CH:(r % 16 + 1) * CH],
                              start=r < rs[0] + 4, stop=r > rs[-1] - 4)
                last.then_inc(T.full, 1)
                pe.wait_ge(sem("hid_partials"), due("pe", "hid_partials"))
                pe.wait_ge(T.free, T.claim())
                out = T.filling
                for h in range(2):
                    last = mm(out[:, h * 16:h * 16 + m], PT[:, 512 + h * 128:512 + (h + 1) * 128], C("fold")[:, 0:m],
                              start=True, stop=True)
                last.then_inc(T.full, 1)

            def compress(kv):
                pe.wait_ge(P.free, P.claim(2))
                out = P.filling
                for r in range(CB):
                    if r % 16 == 0:
                        pe.wait_ge(*arrival[f"w1s{kv}_{r // 16}"])
                        w = slot_of(f"w1s{kv}_{r // 16}")
                    for h in range(2):
                        last = mm(out[:, h * 512:(h + 1) * 512],
                                  w[:, (r % 16) * CH + h * 128:(r % 16) * CH + h * 128 + 128],
                                  ap(rowsT[:, r:r + 1], [CS, 512]), start=r == 0, stop=r == CB - 1)
                        if r == 15 and h == 1:
                            last.then_inc(sem("w1_used"), 1)
                            release(f"w1s{kv}_0", sem("w1_used"), kv + 1)
                        if r == CB - 1 and h == 1:
                            last.then_inc(P.full, 2)
                            release(f"w1s{kv}_1", P.full, P.made)
                        yield

            def second(kv, hid, step, nb, n):
                pe.wait_ge(sem("gelu"), due("pe", "gelu"))
                pe.wait_ge(S.free, S.claim(2))
                out = S.filling
                for b in range(nb):
                    for h in range(2):
                        last = mm(out[0:n, b * HD:(b + 1) * HD], hid[:, h * step + b * 64:h * step + b * 64 + n],
                                  W2[:, kv, h, :], start=h == 0, stop=h == 1)
                last.then_inc(S.full, 2)
                mark(f"second{kv}_{nb}", S.full, S.made)

            def to_xT(l, what, view_of, t):
                n = TOK[t][1]
                pe.wait_ge(sem(what), due("pe", what))
                for half in range(2):
                    pe.wait_ge(T.free, T.claim())
                    tp = T.filling
                    for j in range(4):
                        last = tr(tp[:, j * 128:j * 128 + n], view_of(t, half * 4 + j)[0:n])
                    last.then_inc(T.full, 1)
                mark(f"{what}_read{l}_{t}", T.full, T.made)

            def prompt_rows(t, w, n):
                pe.wait_ge(P.free, P.claim())
                out = P.filling
                for k in range(KT):
                    last = mm(out[:, 0:n], xT[:, k, t * 128:(t + 1) * 128], w[:, k * n:(k + 1) * n],
                              start=k == 0, stop=k == KT - 1)
                last.then_inc(P.full, 1)

            def decode_rows(w, n):
                pe.wait_ge(P.free, P.claim())
                out = P.filling
                for k in range(KT):
                    g = 32 * (k % 4)
                    last = mm(out[g:g + 32, 0:n], xTs[:, k, :], w[:, k * n:(k + 1) * n], start=k < 4, stop=k >= 4)
                last.then_inc(P.full, 1)

            def decode_sum(n):
                pe.wait_ge(sem("partials"), due("pe", "partials"))
                pe.wait_ge(P.free, P.claim())
                out = P.filling
                mm(out[0:8, 0:n], C("fold")[:, 0:8], PT[:, 0:n], start=True, stop=True).then_inc(P.full, 1)

            def project(l, between, halfway=lambda i: None):
                cs = chunks(l)
                for i, (c, n) in enumerate(cs):
                    pe.wait_ge(*arrival[f"win{l}_{c}"])
                    w = slot_of(f"win{l}_{c}")
                    prompt_rows(0, w, n)
                    if i:
                        decode_sum(cs[i - 1][1])
                        halfway(i)
                    prompt_rows(1, w, n)
                    decode_rows(w, n)
                    release(f"win{l}_{c}", P.full, P.made)
                    between(i)
                decode_sum(cs[-1][1])

            def project_out(l, tile_done):
                ws = []
                for c in (0, 512):
                    pe.wait_ge(*arrival[f"wout{l}_{c}"])
                    w = slot_of(f"wout{l}_{c}")
                    ws.append(w)
                for t in (0, 1):
                    for w in ws:
                        prompt_rows(t, w, 512)
                    tile_done(t)
                for i, w in enumerate(ws):
                    decode_rows(w, 512)
                    release(f"wout{l}_{i * 512}", P.full, P.made)
                    decode_sum(512)
                tile_done(2)

            evacuated = {}

            def do_prep(l, p):
                pe.wait_ge(T.free, T.claim())
                tp = T.filling
                for j, (t, c, w) in enumerate(p["blocks"]):
                    last = tr(tp[0:w, j * 128:(j + 1) * 128], zt[l][t][:, c:c + w])
                last.then_inc(T.full, 1)
                evacuated[p["n"]] = T.made

            def scores(u, n):
                for d in u["deps"]:
                    pe.wait_ge(T.free, evacuated[d])
                pe.wait_ge(S.free, S.claim(u["banks"]))
                out = S.filling
                for i, (c, q, k) in enumerate(u["scores"]):
                    w = k.shape[-1]
                    last = mm(out[:, c:c + w], q, k, start=True, stop=True)
                last.then_inc(S.full, u["banks"])
                mark(("s", n), S.free, S.made)
                for d in u["deps"]:
                    mark(("qk", d), S.full, S.made)

            def output(u, n):
                pe.wait_ge(sem("probs" if u["kind"] != "a" else "diffs"), due("pe", "probs" if u["kind"] != "a" else "diffs"))
                blocks = [(m, k) for m in range(u["pmaps"]) for k in range(u["kt"])]
                for i0 in range(0, len(blocks), 4):
                    pe.wait_ge(T.free, T.claim())
                    tp = T.filling
                    for j, (m, k) in enumerate(blocks[i0:i0 + 4]):
                        c = m * u["nk"] + k * u["kw"]
                        last = tr(tp[0:u["kw"], j * 128:(j + 1) * 128], SM[:, n % 2, c:c + u["kw"]])
                    last.then_inc(T.full, 1)
                mark(("p", n), T.full, T.made)
                pe.wait_ge(T.free, T.made)
                pe.wait_ge(O.free, O.claim())
                out = O.filling
                for m in range(u["pmaps"]):
                    for k in range(u["kt"]):
                        i = m * u["kt"] + k
                        last = mm(out[:, m * HD:(m + 1) * HD], PT[0:u["kw"], i * 128:(i + 1) * 128],
                                  u["v"][m][k], start=k == 0, stop=k == u["kt"] - 1)
                last.then_inc(O.full, 1)
                mark(("o", n), O.full, O.made)

            def attention(l, us, n0, between):
                for i in range(len(us) + 1):
                    for p in preps[l]:
                        if p["at"] == FIRST_UNIT[n0] + i and i < len(us):
                            do_prep(l, p)
                    if i < len(us):
                        scores(us[i], n0 + i)
                    if i:
                        between(i)
                        output(us[i - 1], n0 + i - 1)

            def index_prompt():
                z = zt[0]
                for j in (0, 1):
                    pe.wait_ge(T.free, T.claim())
                    tp = T.filling
                    for i in range(4):
                        h, t = 2 * j + i // 2, i % 2
                        last = tr(tp[0:64, i * 128:(i + 1) * 128],
                                  z[t][:, EVEN["qi"] + 64 * h:EVEN["qi"] + 64 * h + 64])
                    last.then_inc(T.full, 1)
                pe.wait_ge(T.free, T.claim())
                tp = T.filling
                for t in (0, 1):
                    last = tr(tp[0:64, t * 128:(t + 1) * 128], z[t][:, EVEN["ki"]:EVEN["ki"] + 64])
                last.then_inc(T.full, 1)
                pe.wait_ge(T.free, T.made)
                for t in (0, 1):
                    nk = 128 * (t + 1)
                    for j in (0, 1):
                        pe.wait_ge(S.free, S.claim())
                        out = S.filling
                        for i in (0, 1):
                            last = mm(out[:, i * nk:(i + 1) * nk], QK[0:64, j, i * 256 + t * 128:i * 256 + t * 128 + 128],
                                      QK[0:64, 2, 0:nk], start=True, stop=True)
                        last.then_inc(S.full, 1)
                mark("index_prompt", S.full, S.made)

            def dec_query(z, q, w, k, wk):
                pe.wait_ge(T.free, T.claim())
                tp = T.filling
                for h in range(H):
                    last = tr(tp[0:w, h * 8:h * 8 + 8], z[0:8, q + w * h:q + w * h + w])
                if k is not None:
                    last = tr(tp[0:w, 32:40], z[0:8, k:k + wk])
                last.then_inc(T.full, 1)
                pe.wait_ge(T.free, T.made)

            def dec_own_key(w):
                pe.wait_ge(O.free, O.claim())
                out = O.filling
                mm(out[0:32, 0:8], QF[0:w, :], KN[0:w, :], start=True, stop=True).then_inc(O.full, 1)

            def dec_scores(name, per_slot, tiles, w, masked):
                bank = S if l == 0 else Q
                pe.wait_ge(bank.free, bank.claim(2))
                out = bank.filling
                if masked:
                    pe.wait_ge(sem("dec_mask"), due("pe", "dec_mask"))
                    for half in range(2):
                        mm(out[0:32, half * 512:(half + 1) * 512], C("e32", 8),
                           SR[l][0:8, half * 512:(half + 1) * 512], start=True, stop=False)
                jobs = [(b, half) for b in range(NB) for half in range(tiles // 4)]
                filled = [None] * len(jobs)
                for i in range(len(jobs) + 1):
                    if i < len(jobs):
                        b, half = jobs[i]
                        pe.wait_ge(*arrival[f"{name}_{b // per_slot}"])
                        slot = slot_of(f"{name}_{b // per_slot}")
                        pe.wait_ge(T.free, T.claim())
                        tp = T.filling
                        for j in range(4):
                            c = (b % per_slot) * tiles * w + (half * 4 + j) * w
                            last = tr(tp[0:w, j * 128:(j + 1) * 128], slot[:, c:c + w])
                        last.then_inc(T.full, 1)
                        filled[i] = T.made
                        if b % per_slot == per_slot - 1 and half == tiles // 4 - 1:
                            release(f"{name}_{b // per_slot}", T.full, T.made)
                    yield
                    if i:
                        b, half = jobs[i - 1]
                        pe.wait_ge(T.free, filled[i - 1])
                        last = mm(out[0:32, half * 512:(half + 1) * 512], QD[0:w, b, :],
                                  KTs[l][0:w, (i - 1) % 2, :], start=b == 0 and not masked, stop=b == NB - 1)
                        if i < len(jobs):
                            last.then_inc(sem("keys_used"), 1)
                last.then_inc(bank.full, 2)

            def dec_probs_T(rows, tiles):
                pe.wait_ge(sem("dec_probs"), due("pe", "dec_probs"))
                pe.wait_ge(T.free, T.claim())
                tp = T.filling
                for j, (c, n) in enumerate(tiles):
                    last = tr(tp[0:n, j * rows:(j + 1) * rows], SR[l][0:rows, c:c + n])
                last.then_inc(T.full, 1)

            def dec_new_T(rows, n):
                pe.wait_ge(T.free, T.claim())
                tp = T.filling
                for g in range(n):
                    last = tr(tp[0:8, g * rows:(g + 1) * rows], PN[0:rows, g, :])
                last.then_inc(T.full, 1)

            def spread(kind):
                pe.wait_ge(sem("dec_head"), due("pe", "dec_head"))
                pe.wait_ge(O.free, O.claim())
                out = O.filling
                mm(out[0:8, :], C("bm32"), HR[l], start=True, stop=True).then_inc(O.full, 1)

            def dec_values(name, per_slot, tiles, z, v):
                pe.wait_ge(sem("dec_pd"), due("pe", "dec_pd"))
                pe.wait_ge(O.free, O.claim())
                out = O.filling
                mm(out[0:32, 0:HD], PNT[0:8, 0, 0:32], z[0:8, v:v + HD], start=True, stop=False)
                for b in range(NB):
                    pe.wait_ge(*arrival[f"{name}_{b // per_slot}"])
                    slot = slot_of(f"{name}_{b // per_slot}")
                    for r in range(tiles):
                        c = ((b % per_slot) * tiles + r) * HD
                        g = 32 * (r % 4)
                        last = mm(out[g:g + 32, 0:HD], PD[:, r * 256 + b * 32:r * 256 + b * 32 + 32],
                                  slot[:, c:c + HD], start=b == 0 and 0 < r < 4, stop=b == NB - 1 and r >= tiles - 4)
                last.then_inc(O.full, 1)
                for s in range(NB // per_slot):
                    release(f"{name}_{s}", O.full, O.made)

            def dec_shared(z, name, per_slot, tiles, q, k, v, masked, new_query, vper):
                if new_query:
                    dec_query(z, q, HD, k, HD)
                else:
                    pe.wait_ge(T.free, T.claim())
                    tp = T.filling
                    tr(tp[0:HD, 0:8], z[0:8, k:k + HD]).then_inc(T.full, 1)
                    pe.wait_ge(T.free, T.made)
                dec_own_key(HD)
                yield
                yield from dec_scores(name + "k", per_slot, tiles, HD, masked)
                yield PAUSE
                dec_probs_T(32, [(r * 128, 128) for r in range(tiles)])
                dec_new_T(32, 1)
                yield PAUSE
                dec_values(name + "v", vper, tiles, z, v)
                yield PAUSE
                spread(name)
                yield

            def cache_rows(kv, halves=(0, 1)):
                for half in halves:
                    pe.wait_ge(*arrival[f"rows{kv}_{half}"])
                    slot = slot_of(f"rows{kv}_{half}")
                    for i in range(8):
                        b, rq = i // 2, i % 2
                        pe.wait_ge(T.free, T.claim())
                        tp = T.filling
                        for j in range(4):
                            c = b * 1024 + (rq * 4 + j) * 128
                            last = tr(tp[:, j * 128:(j + 1) * 128], slot[:, c:c + 128])
                        last.then_inc(T.full, 1)
                    release(f"rows{kv}_{half}", T.full, T.made)
                pe.wait_ge(T.free, T.made)

            def broadcast_query(zs, q, b):
                pe.wait_ge(O.free, O.claim())
                out = O.filling
                mm(out[:, :], ap(C("one8", 8)[:, b:b + 1], [0, 128]), zs[0:8, q:q + 512],
                   start=True, stop=True).then_inc(O.full, 1)

            def decode(z, zs):
                dec_query(zs, ODD["qc"], HD, None, 0)
                pe.wait_ge(P.free, P.made)
                pe.wait_ge(Q.free, Q.claim(2))
                out = Q.filling
                for b in range(NB):
                    last = mm(out[0:32, 0:NC_S], QD[:, b, :], kcT[:, b, 0:NC_S], start=b == 0, stop=b == NB - 1)
                last.then_inc(Q.full, 2)
                yield PAUSE
                dec_probs_T(32, [(0, NC_S)])
                yield PAUSE
                pe.wait_ge(sem("imp_in"), due("pe", "imp_in"))
                pe.wait_ge(O.free, O.claim())
                out = O.filling
                mm(out[0:8, 0:NSEL], small[0:NC_S, 24:32], C("overlap", NC_S), start=True, stop=True)\
                    .then_inc(O.full, 1)
                pe.wait_ge(sem("dec_pd"), due("pe", "dec_pd"))
                pe.wait_ge(O.free, O.claim())
                out = O.filling
                for b in range(NB):
                    g = 32 * (b % 4)
                    last = mm(out[g:g + 32, 0:HD], PD[0:NC_S, b * 32:b * 32 + 32], VC[0:NC_S, b, :],
                              start=b < 4, stop=b >= NB - 4)
                last.then_inc(O.full, 1)
                yield PAUSE
                spread("cmp")
                yield
                yield from dec_shared(zs, "c", 4, 8, None, ODD["ksel"], ODD["vsel"], True, False, 4)
                yield from dec_shared(zs, "w", 8, 4, None, ODD["kwin"], ODD["vwin"], False, False, 8)
                yield PAUSE
                pe.wait_ge(O.free, O.claim())
                out = O.filling
                pe.wait_ge(sem("own_d"), due("pe", "own_d"))
                mm(out[0:32, 0:12], C("e32", 8), small[0:8, 32:44], start=True, stop=True).then_inc(O.full, 1)
                pe.wait_ge(sem("scores_d"), due("pe", "scores_d"))
                pe.wait_ge(Q.free, Q.claim(2))
                out = Q.filling
                for g in range(3):
                    last = tr(out[0:32, g * 128:g * 128 + DN[g]], SA[0:DN[g], g * 32:(g + 1) * 32])
                last.then_inc(Q.full, 2)
                yield PAUSE
                dec_probs_T(32, [(g * 128, DN[g]) for g in range(3)])
                dec_new_T(32, 3)
                yield PAUSE
                pe.wait_ge(sem("dec_pd"), due("pe", "dec_pd"))
                pe.wait_ge(O.free, O.claim())
                out = O.filling
                for g in range(3):
                    mm(out[32 * g:32 * g + 32, :], PNT[0:8, g, 0:32], zs[0:8, ODD[f"vd{g}"]:ODD[f"vd{g}"] + 512],
                       start=True, stop=False)
                for g in range(3):
                    pe.wait_ge(*arrival[f"dv_{g}"])
                    slot = slot_of(f"dv_{g}")
                    n = DN[g]
                    for b in range(NB):
                        c = 32 * (b % 4)
                        last = mm(out[c:c + 32, :], PD[0:n, g * 256 + b * 32:g * 256 + b * 32 + 32],
                                  slot[0:n, b * 512:(b + 1) * 512], start=g == 0 and b == 3,
                                  stop=g == 2 and b >= NB - 4)
                    if g < 2:
                        last.then_inc(sem("dv_used"), 1)
                        release(f"dv_{g}", sem("dv_used"), g + 1)
                last.then_inc(O.full, 1)
                release("dv_2", O.full, O.made)
                yield PAUSE
                spread("d")
                pe.wait_ge(Q.free, Q.made)

            pe.wait_ge(sem("const_in"), 16 * N_SMALL)
            pe.wait_ge(T.free, T.claim())
            tp = T.filling
            tr(tp[:, 0:64], posr).then_inc(T.full, 1)
            for t in range(3):
                to_xT(0, "xn", lambda t, k: PD[:, k * 128:(k + 1) * 128], t)
            cache_rows(0)

            for l in (0, 1):
                z, zs = zt[l], zt[l][2]
                if l == 0:
                    def between(i):
                        if i == 2:
                            pe.wait_ge(sem("own_a"), due("pe", "own_a"))
                            pe.wait_ge(O.free, O.claim())
                            out = O.filling
                            mm(out[0:64, 0:8], C("e64", 8), small[0:8, 32:40], start=True, stop=True)\
                                .then_inc(O.full, 1)
                            broadcast_query(zs, 0, 0)

                    def halfway(i):
                        if 3 <= i <= 6:
                            broadcast_query(zs, 0, i - 2)
                    project(0, between, halfway)
                    pe.wait_ge(sem("roped"), due("pe", "roped"))
                    dec_query(zs, EVEN["qi"], 64, EVEN["ki"], 64)
                    dec_own_key(64)
                    pe.wait_ge(O.free, O.claim())
                    out = O.filling
                    mm(out[0:32, 0:4], C("e32", 8), zs[0:8, EVEN["wi"]:EVEN["wi"] + 4],
                       start=True, stop=True).then_inc(O.full, 1)
                    broadcast_query(zs, 0, 5)
                    broadcast_query(zs, 0, 6)
                    folded(0, "w1s", lambda r: posT[:, r:r + 1], 1, range(0, 16))
                    filler = compress(0)
                    for _ in dec_scores("idx", 8, 8, 64, False):
                        fill(filler, 2)
                    broadcast_query(zs, 0, 7)
                    folded(0, "w1s", lambda r: posT[:, r:r + 1], 1, range(16, 32))
                    filler2 = compress(1)

                    def compress_between(i):
                        if i == 1:
                            pe.wait_ge(sem("relu_rows"), due("pe", "relu_rows"))
                            pe.wait_ge(S.free, S.claim(2))
                            out = S.filling
                            for half in range(2):
                                last = mm(out[0:8, half * 512:(half + 1) * 512], small[0:32, 16:24],
                                          IR[:, half * 512:(half + 1) * 512], start=True, stop=True)
                            last.then_inc(S.full, 2)
                            pe.wait_ge(O.free, O.claim())
                            out = O.filling
                            mm(out[0:8, 0:1], small[0:32, 16:24], IR[:, 1024:1025], start=True, stop=True)\
                                .then_inc(O.full, 1)
                        if i <= 4:
                            fill(filler, 8)
                        elif i <= 6:
                            cache_rows(1, (i - 5,))
                        elif i == 7:
                            folded(1, "w1s", lambda r: posT[:, CB + r:CB + r + 1], 1, range(0, 16))
                            fill(filler2, 8)
                        else:
                            fill(filler2, 8)
                    attention(0, units[0][0:8], 0, compress_between)
                    index_prompt()
                    fill(filler2, 16)
                    folded(1, "w1s", lambda r: posT[:, CB + r:CB + r + 1], 1, range(16, 32))
                    second(0, hid, 512, NB, NC_S)
                    pe.wait_ge(sem("kc_roped"), due("pe", "kc_roped"))
                    for half in range(2):
                        pe.wait_ge(T.free, T.claim())
                        tp = T.filling
                        for j in range(4):
                            b = half * 4 + j
                            last = tr(tp[:, j * 128:j * 128 + NC_S], kc_rows[0:NC_S, b * HD:(b + 1) * HD])
                        last.then_inc(T.full, 1)
                    fill(filler2, 8)
                    pe.wait_ge(sem("topk_prompt"), due("pe", "topk_prompt"))
                    attention(0, units[0][8:12], 8, lambda i: fill(filler2, 3))
                    pe.wait_ge(sem("scores_a"), due("pe", "scores_a"))
                    pe.wait_ge(S.free, S.claim(2))
                    out = S.filling
                    for r in range(ROWS):
                        last = tr(out[0:64, r * 128:(r + 1) * 128], SA[:, r * 64:(r + 1) * 64])
                    last.then_inc(S.full, 2)
                    fill(filler2)
                    dec_probs_T(64, [(r * 128, 128) for r in range(ROWS)])
                    dec_new_T(64, 1)
                    second(1, hid, 512, NB, NC_S)
                    pe.wait_ge(sem("pd_pairs"), due("pe", "pd_pairs"))
                    pe.wait_ge(O.free, O.claim())
                    out = O.filling
                    mm(out[0:32, :], PNT[0:8, 1, 0:32], zs[0:8, EVEN["va"]:EVEN["va"] + 512], start=True, stop=False)
                    for b in range(NB):
                        pe.wait_ge(*arrival[f"av_{b}"])
                        slot = slot_of(f"av_{b}")
                        for r in range(ROWS):
                            g = 32 * (r % 4)
                            last = mm(out[g:g + 32, :], PD[:, r * 256 + b * 32:r * 256 + b * 32 + 32],
                                      slot[:, r * 512:(r + 1) * 512], start=b == 0 and 0 < r < 4,
                                      stop=b == NB - 1 and r >= ROWS - 4)
                        if b < NB - 1:
                            last.then_inc(sem("av_used"), 1)
                            release(f"av_{b}", sem("av_used"), b + 1)
                    last.then_inc(O.full, 1)
                    release(f"av_{NB - 1}", O.full, O.made)
                    spread("a")
                    pe.wait_ge(O.free, O.claim())
                    out = O.filling
                    pe.wait_ge(sem("own_mask"), due("pe", "own_mask"))
                    mm(out[0:32, 0:1], C("e32", 8), small[0:8, 50:51], start=True, stop=True).then_inc(O.full, 1)
                    fill(dec_shared(zs, "b", 4, 8, EVEN["qb"], EVEN["kb"], EVEN["vb"], True, True, 4))
                else:
                    def between(i):
                        if i in SCORE_D:
                            pe.wait_ge(sem("qd_roped"), due("pe", "qd_roped"))
                            for b in range(NB):
                                broadcast_query(zs, ODD[f"qd{SCORE_D[i]}"], b)
                        if i != CMP_AT:
                            return
                        pe.wait_ge(P.free, P.made - 2)
                        pe.wait_ge(T.free, T.claim())
                        tp = T.filling
                        for j in range(4):
                            c = ODD["kcr"] if j < 2 else ODD["vcr"]
                            last = tr(tp[:, j * 128:(j + 1) * 128], z[j % 2][:, c:c + 128])
                        last.then_inc(T.full, 1)
                        pe.wait_ge(T.free, T.made)
                        for kv in range(2):
                            folded(kv, "w1p", lambda r: ap(QK[:, 5, kv * 256 + r:kv * 256 + r + 1], [CS, NC_P]), NC_P)
                            release(f"w1p{kv}_0", T.full, T.made)
                            release(f"w1p{kv}_1", T.full, T.made)
                            second(kv, BM[:, 0:80], 16, 1, NC_P)
                        pe.wait_ge(sem("kcp_roped"), due("pe", "kcp_roped"))
                        pe.wait_ge(T.free, T.claim())
                        tp = T.filling
                        tr(tp[:, 0:NC_P], BM[0:NC_P, 128:256]).then_inc(T.full, 1)
                    project(1, between)
                    steps = decode(z, zs)
                    attention(1, units[1], 12, lambda i: fill(steps, STEPS))
                    fill(steps)
                gates = (EVEN["ga"], EVEN["gb"]) if l == 0 else (ODD["gc"], ODD["gd"])
                for t in range(3):
                    to_xT(l, "mix", lambda t, k: z[t][:, gates[k // 4] + (k % 4) * 128:gates[k // 4] + (k % 4 + 1) * 128], t)
                pe.wait_ge(T.free, T.made)

                def next_rows(t):
                    if t:
                        to_xT(1, "xn", lambda t, k: PD[:, k * 128:(k + 1) * 128], t - 1)
                project_out(l, next_rows if l == 0 else lambda t: None)
                if l == 0:
                    to_xT(1, "xn", lambda t, k: PD[:, k * 128:(k + 1) * 128], 2)
                    pe.wait_ge(T.free, T.made)

        @block.scalar
        def _(eng):
            act = nc.scalar.activation
            copy = nc.scalar.copy


            def hidden(kv, hp, step, n, out, free, banks):
                for h in range(2):
                    signal, by = (free, banks) if h else (sem("act_chain"), 1)
                    act(out[h], hp[:, h * step:h * step + n], ACT.Identity, bias=bias1[:, kv, h:h + 1]).then_inc(signal, by)
                    eng.wait_ge(signal, count(signal, by))
                eng.sem_inc(sem("hid"), 1)
                count(sem("hid"))

            def partials(n):
                eng.wait_ge(P.full, P.arrive())
                pp = P.reading
                copy(PT[:, 0:n], pp[:, 0:n]).then_inc(P.free, 1)
                eng.wait_ge(P.free, count(P.free))
                eng.sem_inc(sem("partials"), 1)
                count(sem("partials"))

            def hid_partials():
                eng.wait_ge(T.full, T.arrive())
                pp = T.reading
                copy(PT[:, 512:512 + CH], pp[:, 0:CH]).then_inc(T.free, 1)
                eng.wait_ge(T.free, count(T.free))
                eng.sem_inc(sem("hid_partials"), 1)
                count(sem("hid_partials"))

            def position(kv, half):
                hid_partials()
                eng.wait_ge(T.full, T.arrive())
                pp = T.reading
                if half == 0:
                    copy(bias1[:, kv, :], ap(pp[:, 0:1], [16, 2])).then_inc(T.free, 1)
                    eng.wait_ge(T.free, count(T.free))
                else:
                    act(bias1[:, kv, 0:1], pp[:, 0:1], ACT.Identity, bias=bias1[:, kv, 0:1])\
                        .then_inc(sem("act_chain"), 1)
                    eng.wait_ge(sem("act_chain"), count(sem("act_chain")))
                    act(bias1[:, kv, 1:2], pp[:, 16:17], ACT.Identity, bias=bias1[:, kv, 1:2]).then_inc(T.free, 1)
                    eng.wait_ge(T.free, count(T.free))

            def norm(t, src):
                n = TOK[t][1]
                act(PD[0:n, 1024:2048], src[0:n], ACT.Square, accum_out=stat[0:n, 60 + t:61 + t])\
                    .then_inc(sem("squares"), 1)
                eng.wait_ge(sem("squares"), count(sem("squares")))
                eng.wait_ge(sem("mean_square"), due("act", "mean_square"))
                act(stat[0:n, 56 + t:57 + t], stat[0:n, 52 + t:53 + t], ACT.Sqrt).then_inc(sem("rms"), 1)
                eng.wait_ge(sem("rms"), count(sem("rms")))

            def to_xT(t):
                n = TOK[t][1]
                for half in range(2):
                    eng.wait_ge(T.full, T.arrive())
                    tp = T.reading
                    if t < 2:
                        dst = xT[:, half * 4:half * 4 + 4, t * 128:t * 128 + n]
                    else:
                        dst = xTs[:, half * 4:half * 4 + 4, 0:n]
                    copy(dst, ap(tp[:, 0:1], [128, 4], [1, n])).then_inc(T.free, 1)
                    eng.wait_ge(T.free, count(T.free))

            def rows_out(dst, n):
                eng.wait_ge(P.full, P.arrive())
                pp = P.reading
                copy(dst, pp[0:dst.shape[0], 0:n]).then_inc(P.free, 1)
                eng.wait_ge(P.free, count(P.free))

            def gate(l, name):
                c = (EVEN if l == 0 else ODD)[name]
                for t, (_, n) in enumerate(TOK):
                    eng.wait_ge(sem("gate_next"), due("act", "gate_next"))
                    act(SM[0:n, 0, 0:512], zt[l][t][0:n, c:c + 512], ACT.Tanh, scale=0.5)\
                        .then_inc(sem("gate_tanh"), 1)
                    eng.wait_ge(sem("gate_tanh"), count(sem("gate_tanh")))
                    if name == "gc":
                        g = zt[l][t][0:n, ODD["gl"]:ODD["gl"] + 12]
                        act(g, g, ACT.Tanh, scale=0.5).then_inc(sem("gl_tanh"), 1)
                        eng.wait_ge(sem("gl_tanh"), count(sem("gl_tanh")))

            def project(l, between):
                cs = chunks(l)
                z = zt[l]
                for i in range(len(cs) + 1):
                    if i < len(cs):
                        c, n = cs[i]
                        rows_out(z[0][:, c:c + n], n)
                    if i:
                        cp, np_ = cs[i - 1]
                        rows_out(z[2][0:8, cp:cp + np_], np_)
                        mark(("z", l, i - 1), *latest)
                    if i < len(cs):
                        rows_out(z[1][:, c:c + n], n)
                        partials(n)
                    if i:
                        for name in GATES[l].get(i - 1, ()):
                            gate(l, name)
                    if i < len(cs):
                        between(i)

            def project_out(l, tile_done):
                for t in range(3):
                    for c in (0, 512):
                        if t == 2:
                            partials(512)
                        rows_out(Y[t][0:TOK[t][1], c:c + 512], 512)
                    tile_done(t)

            def do_prep(l, p):
                eng.wait_ge(T.full, T.arrive())
                tp = T.reading
                n = p["n"]
                if ("qk", n - 6) in marks:
                    eng.wait_ge(*marks[("qk", n - 6)])
                if n == 6:
                    eng.wait_ge(*marks["index_prompt"])
                w = 128 * len(p["blocks"])
                copy(QK[0:p["rows"], p["slot"], 0:w], tp[0:p["rows"], 0:w]).then_inc(T.free, 1)
                eng.wait_ge(T.free, count(T.free))

            def exps(u, n):
                eng.wait_ge(*marks[("s", n)])
                nk = u["nk"]
                for m in range(u["maps"]):
                    x = SM[:, n % 2, m * nk:(m + 1) * nk]
                    signal, by = (sem("exp_a" if u["kind"] == "a" else "probs"), 1) if m == u["maps"] - 1 else (sem("act_chain"), 1)
                    act(x, x, ACT.Exp, scale=-1.0, bias=stat[:, (n % 2) * 4 + m:(n % 2) * 4 + m + 1],
                        accum_out=stat[:, 64 + (n % 4) * 4 + m:65 + (n % 4) * 4 + m]).then_inc(signal, by)
                    eng.wait_ge(signal, count(signal, by))

            def probs_T(u, n):
                blocks = u["pmaps"] * u["kt"]
                for i0 in range(0, blocks, 4):
                    k = min(4, blocks - i0)
                    eng.wait_ge(T.full, T.arrive())
                    tp = T.reading
                    if i0 == 0 and n:
                        eng.wait_ge(*marks[("o", n - 1)])
                    copy(PT[0:u["kw"], i0 * 128:(i0 + k) * 128], tp[0:u["kw"], 0:k * 128]).then_inc(T.free, 1)
                    eng.wait_ge(T.free, count(T.free))

            def attention(l, us, n0, between=lambda i: None):
                for i in range(len(us) + 1):
                    for p in preps[l]:
                        if p["at"] == FIRST_UNIT[n0] + i and i < len(us):
                            do_prep(l, p)
                    if i:
                        between(i)
                        probs_T(us[i - 1], n0 + i - 1)
                    if i < len(us):
                        exps(us[i], n0 + i)

            def dec_query(w, with_key, dense=True):
                eng.wait_ge(T.full, T.arrive())
                tp = T.reading
                copy(ap(QD[0:w, 0, 0:1], [36, NB], [1, H]), ap(tp[0:w, 0:1], [1, NB], [8, H]))\
                    .then_inc(sem("act_chain"), 1)
                eng.wait_ge(sem("act_chain"), count(sem("act_chain")))
                signal, by = (sem("act_chain"), 1) if with_key else (T.free, 1)
                copy(ap(QF[0:w, 0:1], [4, NB], [1, H]), ap(tp[0:w, 0:1], [1, NB], [8, H])).then_inc(signal, by)
                eng.wait_ge(signal, count(signal, by))
                if with_key:
                    copy(KN[0:w, :], tp[0:w, 32:40]).then_inc(T.free, 1)
                    eng.wait_ge(T.free, count(T.free))

            def dec_scores(tiles, w):
                n = NB * tiles // 4
                base = seen.get(("act", "keys_used"), 0)
                for i in range(n + 1):
                    if i < n:
                        eng.wait_ge(T.full, T.arrive())
                        tp = T.reading
                        if i >= 2:
                            eng.wait_ge(sem("keys_used"), base + i - 1)
                        copy(KTs[l][0:w, i % 2, :], tp[0:w, :]).then_inc(T.free, 1)
                        eng.wait_ge(T.free, count(T.free))
                    yield
                seen["act", "keys_used"] = base + n - 1

            def dec_exp(rows, n):
                eng.wait_ge(sem("dec_scaled"), due("act", "dec_scaled"))
                act(SR[l][0:rows, 0:n], SR[l][0:rows, 0:n], ACT.Exp, scale=-1.0, bias=stat[0:rows, 20:21],
                    accum_out=stat[0:rows, 21:22]).then_inc(sem("dec_exp"), 1)
                eng.wait_ge(sem("dec_exp"), count(sem("dec_exp")))

            def dec_pd(tiles):
                eng.wait_ge(T.full, T.arrive())
                tp = T.reading
                eng.wait_ge(sem("pd_zero"), due("act", "pd_zero"))
                copy(ap(PD[:, 0:1], [256, tiles], [36, NB], [1, H]),
                     ap(tp[:, 0:1], [32, tiles], [4, NB], [1, H])).then_inc(T.free, 1)
                eng.wait_ge(T.free, count(T.free))

            def dec_new(rows, n, s):
                eng.wait_ge(T.full, T.arrive())
                tp = T.reading
                copy(PNT[:, 0:n, 0:rows], ap(tp[0:8, 0:1], [rows, n], [1, rows])).then_inc(T.free, 1)
                eng.wait_ge(T.free, count(T.free))
                eng.sem_inc(sem(s), 1)
                count(sem(s))

            def dec_shared(tiles, n, new_query):
                if new_query:
                    dec_query(HD, True)
                else:
                    eng.wait_ge(T.full, T.arrive())
                    tp = T.reading
                    copy(KN[:, :], tp[:, 0:8]).then_inc(T.free, 1)
                    eng.wait_ge(T.free, count(T.free))
                yield
                yield from dec_scores(tiles, HD)
                dec_exp(32, n)
                yield PAUSE
                dec_pd(tiles)
                dec_new(32, 1, "dec_pd")
                yield PAUSE
                yield PAUSE
                yield

            def decode():
                dec_query(HD, False)
                dec_exp(32, NC_S)
                yield PAUSE
                eng.wait_ge(T.full, T.arrive())
                tp = T.reading
                eng.wait_ge(sem("pd_zero"), due("act", "pd_zero"))
                copy(ap(PD[0:NC_S, 0:1], [36, NB], [1, H]), ap(tp[0:NC_S, 0:1], [4, NB], [1, H]))\
                    .then_inc(sem("act_chain"), 1)
                eng.wait_ge(sem("act_chain"), count(sem("act_chain")))
                copy(SA[0:NC_S, 96:128], tp[0:NC_S, 0:32]).then_inc(T.free, 1)
                eng.wait_ge(T.free, count(T.free))
                eng.sem_inc(sem("imp_T"), 1)
                count(sem("imp_T"))
                eng.sem_inc(sem("dec_pd"), 1)
                count(sem("dec_pd"))
                yield PAUSE
                yield PAUSE
                yield
                yield from dec_shared(8, 1025, False)
                yield from dec_shared(4, 513, False)
                yield PAUSE
                dec_exp(32, 387)
                yield PAUSE
                eng.wait_ge(T.full, T.arrive())
                tp = T.reading
                eng.wait_ge(sem("pd_zero"), due("act", "pd_zero"))
                for g in range(3):
                    n = DN[g]
                    signal, by = (T.free, 1) if g == 2 else (sem("act_chain"), 1)
                    copy(ap(PD[0:n, g * 256:g * 256 + 1], [36, NB], [1, H]),
                         ap(tp[0:n, g * 32:g * 32 + 1], [4, NB], [1, H])).then_inc(signal, by)
                    eng.wait_ge(signal, count(signal, by))
                dec_new(32, 3, "dec_pd")
                yield PAUSE
                yield PAUSE

            def cache_rows(kv, bs=range(NB)):
                for b in bs:
                    for rq in range(2):
                        eng.wait_ge(T.full, T.arrive())
                        tp = T.reading
                        copy(ap(rowsT[:, b * 1024 + rq * 4:b * 1024 + rq * 4 + 1], [1, 4], [8, 128]),
                             ap(tp[:, 0:1], [128, 4], [1, 128])).then_inc(T.free, 1)
                        eng.wait_ge(T.free, count(T.free))

            eng.wait_ge(sem("stat_zero"), due("act", "stat_zero"))
            eng.wait_ge(sem("const_in"), 16 * N_SMALL)
            eng.wait_ge(T.full, T.arrive())
            tp = T.reading
            copy(posT[:, :], tp[:, 0:64]).then_inc(T.free, 1)
            eng.wait_ge(T.free, count(T.free))
            eng.wait_ge(sem("lam_in"), due("act", "lam_in"))
            act(lam[:, 2:4], lam[:, 0:2], ACT.Exp).then_inc(sem("lam_exp"), 1)
            eng.wait_ge(sem("lam_exp"), count(sem("lam_exp")))
            for t in range(3):
                norm(t, X[:, t, :])
                to_xT(t)
            cache_rows(0)
            for l in (0, 1):
                z, zs = zt[l], zt[l][2]
                if l == 1:
                    eng.wait_ge(sem("out0"), 16 * len(OUTS0))
                if l == 0:
                    project(0, lambda i: None)
                    dec_query(64, True)
                    position(0, 0)
                    fill(dec_scores(8, 64))
                    position(0, 1)

                    def compress_between(i):
                        if i == 5:
                            eng.wait_ge(P.full, P.arrive(2))
                            hp = P.reading
                            hidden(0, hp, 512, 512, [hid[:, 0:512], hid[:, 512:1024]], P.free, 2)
                            cache_rows(1, range(0, 4))
                        if i == 6:
                            cache_rows(1, range(4, 8))
                        if i == 7:
                            position(1, 0)
                    attention(0, units[0][0:8], 0, compress_between)
                    for j in range(3):
                        eng.wait_ge(T.full, T.arrive())
                        tp = T.reading
                        w = 512 if j < 2 else 256
                        if j == 0:
                            eng.wait_ge(*marks[("qk", 2)])
                        copy(QK[0:64, j, 0:w], tp[0:64, 0:w]).then_inc(T.free, 1)
                        eng.wait_ge(T.free, count(T.free))
                    eng.wait_ge(sem("gelu_in"), due("act", "gelu_in"))
                    act(hid2, hid2, ACT.Tanh, scale=GELU_C).then_inc(sem("gelu_tanh"), 1)
                    eng.wait_ge(sem("gelu_tanh"), count(sem("gelu_tanh")))
                    position(1, 1)
                    for half in range(2):
                        eng.wait_ge(T.full, T.arrive())
                        tp = T.reading
                        copy(kcT[:, half * 4:half * 4 + 4, 0:NC_S],
                             ap(tp[:, 0:1], [128, 4], [1, NC_S])).then_inc(T.free, 1)
                        eng.wait_ge(T.free, count(T.free))
                    attention(0, units[0][8:12], 8)
                    dec_exp(64, 1025)
                    eng.wait_ge(P.full, P.arrive(2))
                    hp = P.reading
                    hidden(1, hp, 512, 512, [hid[:, 0:512], hid[:, 512:1024]], P.free, 2)
                    eng.wait_ge(sem("gelu_in"), due("act", "gelu_in"))
                    act(hid2, hid2, ACT.Tanh, scale=GELU_C).then_inc(sem("gelu_tanh"), 1)
                    eng.wait_ge(sem("gelu_tanh"), count(sem("gelu_tanh")))
                    eng.wait_ge(T.full, T.arrive())
                    tp = T.reading
                    copy(SA[:, :], tp[:, :]).then_inc(T.free, 1)
                    eng.wait_ge(T.free, count(T.free))
                    dec_new(64, 1, "pair_in")
                    steps = dec_shared(8, 1025, True)
                    fill(steps, 1 + 2 * NB)
                    eng.wait_ge(sem("o_a"), due("act", "o_a"))
                    for t, (_, n) in enumerate(TOK):
                        act(stat[0:n, 44:48], stat[0:n, 24 + t * 4:28 + t * 4], ACT.Sqrt)\
                            .then_inc(sem("act_chain"), 1)
                        eng.wait_ge(sem("act_chain"), count(sem("act_chain")))
                        copy(stat[0:n, 24 + t * 4:28 + t * 4], stat[0:n, 44:48]).then_inc(sem("a_rms"), 1)
                        eng.wait_ge(sem("a_rms"), count(sem("a_rms")))
                    fill(steps)
                else:
                    def between(i):
                        if i != CMP_AT:
                            return
                        eng.wait_ge(T.full, T.arrive())
                        tp = T.reading
                        copy(QK[:, 5, :], tp[:, :]).then_inc(T.free, 1)
                        eng.wait_ge(T.free, count(T.free))
                        for kv in range(2):
                            hid_partials()
                            eng.wait_ge(T.full, T.arrive())
                            hp = T.reading
                            hidden(kv, hp, 16, NC_P, [BM[:, 0:NC_P], BM[:, 16:16 + NC_P]], T.free, 1)
                            eng.wait_ge(sem("gelu_in"), due("act", "gelu_in"))
                            for h in range(2):
                                x = BM[:, 32 + 16 * h:32 + 16 * h + NC_P]
                                signal, by = (sem("gelu_tanh"), 1) if h else (sem("act_chain"), 1)
                                act(x, x, ACT.Tanh, scale=GELU_C).then_inc(signal, by)
                                eng.wait_ge(signal, count(signal, by))
                        eng.wait_ge(T.full, T.arrive())
                        tp = T.reading
                        copy(kcTp[:, 0:NC_P], tp[:, 0:NC_P]).then_inc(T.free, 1)
                        eng.wait_ge(T.free, count(T.free))
                    project(1, between)
                    steps = decode()
                    attention(1, units[1], 12, lambda i: fill(steps, STEPS))
                    fill(steps)
                for t in range(3):
                    to_xT(t)
                eng.wait_ge(sem("y_free"), due("act", "y_free"))
                if l == 1:
                    eng.wait_ge(sem("out0"), 16 * (len(OUTS0) + len(OUTS1)))

                def tile_done(t):
                    norm(t, Y[t])
                    if l == 0:
                        eng.wait_ge(sem("x_next"), due("act", "x_next"))
                        norm(t, X[:, t, :])
                        if t:
                            to_xT(t - 1)
                project_out(l, tile_done)
                if l == 0:
                    to_xT(2)

        @block.vector
        def _(eng):
            V = nc.vector
            tt, ts, stt = V.tensor_tensor, V.tensor_scalar, V.scalar_tensor_tensor
            mul, add, sub = ALU.mult, ALU.add, ALU.subtract


            def rope(x, heads, step, half, table):
                n = x.shape[0]
                both = ap(x, [step, heads], [half, 2], [1, half])
                lo, hi = ap(x, [step, heads], [1, half]), ap(x, [step, heads], [1, half], at=half)
                cos = ap(table[:, 0:1], [0, heads], [0, 2], [1, half])
                sin = ap(table[:, half:half + 1], [0, heads], [0, 2], [1, half])
                tmp = RT[0:n, 0:heads * 2 * half]
                w = 2 * half
                tt(ap(tmp, [w, heads], [half, 2], [1, half]), both, sin, mul).then_inc(sem("dve_chain"), 1)
                eng.wait_ge(sem("dve_chain"), count(sem("dve_chain")))
                tt(both, both, cos, mul).then_inc(sem("dve_chain"), 1)
                eng.wait_ge(sem("dve_chain"), count(sem("dve_chain")))
                tt(lo, lo, ap(RT[0:n, half:half + 1], [w, heads], [1, half]), sub).then_inc(sem("dve_chain"), 1)
                eng.wait_ge(sem("dve_chain"), count(sem("dve_chain")))
                tt(hi, hi, ap(RT[0:n, 0:1], [w, heads], [1, half]), add).then_inc(sem("dve_chain"), 1)
                eng.wait_ge(sem("dve_chain"), count(sem("dve_chain")))

            def gelu(hx, x2, both):
                eng.wait_ge(sem("hid"), due("dve", "hid"))
                for x, y in zip(hx, x2):
                    tt(y, x, x, mul).then_inc(sem("dve_chain"), 1)
                    eng.wait_ge(sem("dve_chain"), count(sem("dve_chain")))
                    ts(y, y, 0.044715, 1.0, mul, add).then_inc(sem("dve_chain"), 1)
                    eng.wait_ge(sem("dve_chain"), count(sem("dve_chain")))
                    tt(y, y, x, mul).then_inc(sem("dve_chain"), 1)
                    eng.wait_ge(sem("dve_chain"), count(sem("dve_chain")))
                eng.sem_inc(sem("gelu_in"), 1)
                count(sem("gelu_in"))
                eng.wait_ge(sem("gelu_tanh"), due("dve", "gelu_tanh"))
                for x, y in zip(hx, x2):
                    ts(y, y, 1.0, 0.5, add, mul).then_inc(sem("dve_chain"), 1)
                    eng.wait_ge(sem("dve_chain"), count(sem("dve_chain")))
                    tt(x, x, y, mul).then_inc(sem("dve_chain"), 1)
                    eng.wait_ge(sem("dve_chain"), count(sem("dve_chain")))
                eng.sem_inc(sem("gelu"), 1)
                count(sem("gelu"))

            def norm(t):
                n = TOK[t][1]
                ms, r, x = (stat[0:n, c + t:c + t + 1] for c in (52, 49, 56))
                eng.wait_ge(sem("squares"), due("dve", "squares"))
                ts(ms, stat[0:n, 60 + t:61 + t], 1.0 / D, EPS, mul, add).then_inc(sem("mean_square"), 1)
                eng.wait_ge(sem("mean_square"), count(sem("mean_square")))
                eng.wait_ge(sem("rms"), due("dve", "rms"))
                V.reciprocal(r, x).then_inc(sem("dve_chain"), 1)
                eng.wait_ge(sem("dve_chain"), count(sem("dve_chain")))
                tt(x, r, r, mul).then_inc(sem("dve_chain"), 1)
                eng.wait_ge(sem("dve_chain"), count(sem("dve_chain")))
                tt(x, x, ms, mul).then_inc(sem("dve_chain"), 1)
                eng.wait_ge(sem("dve_chain"), count(sem("dve_chain")))
                ts(x, x, -0.5, 1.5, mul, add).then_inc(sem("dve_chain"), 1)
                eng.wait_ge(sem("dve_chain"), count(sem("dve_chain")))
                tt(r, r, x, mul).then_inc(sem("dve_chain"), 1)
                eng.wait_ge(sem("dve_chain"), count(sem("dve_chain")))
                return r

            def xn(l, t):
                r = norm(t)
                n = TOK[t][1]
                if t:
                    eng.wait_ge(*marks[f"xn_read{l}_{t - 1}"])
                eng.wait_ge(sem("pre_in"), 16 * (l + 1))
                stt(PD[0:n, 0:1024], X[0:n, t, :], r, NWP[0:n, :], mul, mul).then_inc(sem("xn"), 1)
                eng.wait_ge(sem("xn"), count(sem("xn")))

            def gate(l, name):
                c = (EVEN if l == 0 else ODD)[name]
                for t, (_, n) in enumerate(TOK):
                    eng.sem_inc(sem("gate_next"), 1)
                    count(sem("gate_next"))
                    eng.wait_ge(sem("gate_tanh"), due("dve", "gate_tanh"))
                    g = zt[l][t][0:n, c:c + 512]
                    ts(SM[0:n, 0, 0:512], SM[0:n, 0, 0:512], 1.0, 0.5, add, mul).then_inc(sem("dve_chain"), 1)
                    eng.wait_ge(sem("dve_chain"), count(sem("dve_chain")))
                    tt(g, g, SM[0:n, 0, 0:512], mul).then_inc(sem("dve_chain"), 1)
                    eng.wait_ge(sem("dve_chain"), count(sem("dve_chain")))
                    if name == "gc":
                        eng.wait_ge(sem("gl_tanh"), due("dve", "gl_tanh"))
                        g = zt[l][t][0:n, ODD["gl"]:ODD["gl"] + 12]
                        ts(g, g, 1.0, 0.5, add, mul).then_inc(sem("dve_chain"), 1)
                        eng.wait_ge(sem("dve_chain"), count(sem("dve_chain")))

            def rope_tiles(l, c, heads, step, half):
                for t, (_, n) in enumerate(TOK):
                    tab = C("rope", n)[:, 48 * t:48 * t + 48]
                    rope(zt[l][t][0:n, c:c + 1], heads, step, half, tab[:, 0:16] if half == 8 else tab[:, 16:48])

            def score_a(b):
                eng.wait_ge(*arrival[f"ak_{b}"])
                slot = slot_of(f"ak_{b}")
                eng.wait_ge(O.full, O.arrive())
                o = O.reading
                kv3 = ap(slot[:, 0:1], [512, ROWS], [1, 512])
                tt(kv3, kv3, ap(o[:, 0:1], [0, ROWS], [1, 512]), mul).then_inc(O.free, 1)
                eng.wait_ge(O.free, count(O.free))
                V.tensor_reduce(ap(SA[:, b * 8:b * 8 + 1], [64, ROWS], [1, 8]),
                                ap(slot[:, 0:1], [512, ROWS], [64, 8], [1, 64]), AX.X, add)\
                    .then_inc(sem("dve_chain"), 1)
                eng.wait_ge(sem("dve_chain"), count(sem("dve_chain")))
                release(f"ak_{b}", *latest)

            def score_d(g):
                eng.sem_inc(sem("qd_roped"), 1)
                count(sem("qd_roped"))
                eng.wait_ge(*arrival[f"dk_{g}"])
                slot = slot_of(f"dk_{g}")
                n = DN[g]
                for b in range(NB):
                    eng.wait_ge(O.full, O.arrive())
                    o = O.reading
                    k = slot[0:n, b * 512:(b + 1) * 512]
                    tt(k, k, o[0:n, :], mul).then_inc(O.free, 1)
                    eng.wait_ge(O.free, count(O.free))
                V.tensor_reduce(SA[0:n, g * 32:(g + 1) * 32], ap(slot[0:n, 0:1], [128, 32], [1, 128]), AX.X, add)\
                    .then_inc(sem("dve_chain"), 1)
                eng.wait_ge(sem("dve_chain"), count(sem("dve_chain")))
                release(f"dk_{g}", *latest)
                if g == 2:
                    eng.sem_inc(sem("scores_d"), 1)
                    count(sem("scores_d"))

            def soft(u, n):
                eng.wait_ge(S.full, S.arrive(u["banks"]))
                s = S.reading
                if n >= 2:
                    eng.wait_ge(*marks[("p", n - 2)])
                nk = u["nk"]
                step = 512 if u["kind"] == "a" else nk
                for m in range(u["maps"]):
                    signal, by = (S.free, u["banks"]) if m == u["maps"] - 1 else (sem("dve_chain"), 1)
                    V.tensor_tensor_reduce(out=SM[:, n % 2, m * nk:(m + 1) * nk], in0=s[:, m * step:m * step + nk],
                                           in1=u["mask"], scale=-u["scale"], scalar=BIG, op0=add, op1=ALU.min,
                                           accum_out=stat[:, (n % 2) * 4 + m:(n % 2) * 4 + m + 1]).then_inc(signal, by)
                    eng.wait_ge(signal, count(signal, by))

            def combine(u, n):
                eng.wait_ge(sem("exp_a"), due("dve", "exp_a"))
                nk, x = u["nk"], SM[:, n % 2, :]
                den = stat[:, 64 + (n % 4) * 4:66 + (n % 4) * 4]
                V.reciprocal(stat[:, 16:18], den).then_inc(sem("dve_chain"), 1)
                eng.wait_ge(sem("dve_chain"), count(sem("dve_chain")))
                ts(stat[:, 17:18], stat[:, 17:18], lam[:, 5:6], None, mul).then_inc(sem("dve_chain"), 1)
                eng.wait_ge(sem("dve_chain"), count(sem("dve_chain")))
                ts(x[:, nk:2 * nk], x[:, nk:2 * nk], stat[:, 17:18], None, mul).then_inc(sem("dve_chain"), 1)
                eng.wait_ge(sem("dve_chain"), count(sem("dve_chain")))
                stt(x[:, 0:nk], x[:, 0:nk], stat[:, 16:17], x[:, nk:2 * nk], mul, add).then_inc(sem("diffs"), 1)
                eng.wait_ge(sem("diffs"), count(sem("diffs")))

            def finish(u, n, l):
                eng.wait_ge(O.full, O.arrive())
                o = O.reading
                t, h, kind, z = u["t"], u["h"], u["kind"], zt[l][u["t"]]
                k = u["pmaps"]
                den = stat[:, 64 + (n % 4) * 4:64 + (n % 4) * 4 + k]
                if kind == "a":
                    V.tensor_copy(z[:, EVEN["qa"] + 128 * h:EVEN["qa"] + 128 * h + 128], o[:, 0:128])\
                        .then_inc(O.free, 1)
                    eng.wait_ge(O.free, count(O.free))
                    return
                r = stat[:, 16:16 + k]
                V.reciprocal(r, den).then_inc(sem("dve_chain"), 1)
                eng.wait_ge(sem("dve_chain"), count(sem("dve_chain")))
                if kind in ("cmp", "sel", "win"):
                    j = ("cmp", "sel", "win").index(kind)
                    tt(r, r, ap(z[:, ODD["gl"] + 3 * h + j:ODD["gl"] + 3 * h + j + 1], [3, k]), mul)\
                        .then_inc(sem("dve_chain"), 1)
                    eng.wait_ge(sem("dve_chain"), count(sem("dve_chain")))
                if kind == "cmp":
                    ts(r, r, C("cmpok")[:, t:t + 1], None, mul).then_inc(sem("dve_chain"), 1)
                    eng.wait_ge(sem("dve_chain"), count(sem("dve_chain")))
                rb = ap(stat[:, 16:17], [1, k], [0, 128])
                ov = ap(o[:, 0:1], [128, k], [1, 128])
                if kind == "cmp":
                    acc = z[:, ODD["qc"]:ODD["qc"] + 512]
                    tt(ap(acc[:, 0:1], [128, 4], [1, 128]), ov, rb, mul).then_inc(O.free, 1)
                    eng.wait_ge(O.free, count(O.free))
                    return
                tt(ap(RT[:, 0:1], [128, k], [1, 128]), ov, rb, mul).then_inc(O.free, 1)
                eng.wait_ge(O.free, count(O.free))
                if kind in ("sel", "win"):
                    acc = z[:, ODD["qc"] + 128 * h:ODD["qc"] + 128 * h + 128 * k]
                    tt(acc, acc, RT[:, 0:128 * k], add).then_inc(sem("dve_chain"), 1)
                    eng.wait_ge(sem("dve_chain"), count(sem("dve_chain")))
                else:
                    c = (EVEN["gb"] if kind == "b" else ODD["gd"]) + 128 * h
                    g = z[:, c:c + 128 * k]
                    tt(g, g, RT[:, 0:128 * k], mul).then_inc(sem("dve_chain"), 1)
                    eng.wait_ge(sem("dve_chain"), count(sem("dve_chain")))

            def attention(l, us, n0, between=lambda i: None, steps=None):
                for i in range(len(us) + 2):
                    if i < len(us):
                        soft(us[i], n0 + i)
                        between(i)
                    if 1 <= i <= len(us) and us[i - 1]["kind"] == "a":
                        combine(us[i - 1], n0 + i - 1)
                    if i >= 2:
                        finish(us[i - 2], n0 + i - 2, l)
                    if steps and 1 <= i <= len(us):
                        fill(steps, STEPS)

            def topk(work, k, w8):
                for _ in range(0, k, 8):
                    V.max(w8, work).then_inc(sem("dve_chain"), 1)
                    eng.wait_ge(sem("dve_chain"), count(sem("dve_chain")))
                    V.match_replace(work, w8, work, -BIG).then_inc(sem("dve_chain"), 1)
                    eng.wait_ge(sem("dve_chain"), count(sem("dve_chain")))
                    yield

            def dec_own(w, dst):
                eng.wait_ge(O.full, O.arrive())
                o = O.reading
                V.tensor_tensor_reduce(out=small[0:32, 0:8], in0=o[0:32, 0:8], in1=C("bm32", 32), scale=1.0,
                                       scalar=0.0, op0=mul, op1=add, accum_out=dst)\
                    .then_inc(O.free, 1)
                eng.wait_ge(O.free, count(O.free))

            def dec_soft(rows, src, n, scale, own):
                k, o = own
                m = n - k
                if src is not None:
                    bank = S if l == 0 else Q
                    ts(SR[l][0:rows, 0:m], src, -scale, None, mul).then_inc(bank.free, 2)
                    eng.wait_ge(bank.free, count(bank.free, 2))
                if k:
                    ts(SR[l][0:rows, m:n], o, -scale, None, mul).then_inc(sem("dve_chain"), 1)
                    eng.wait_ge(sem("dve_chain"), count(sem("dve_chain")))
                V.tensor_reduce(stat[0:rows, 20:21], SR[l][0:rows, 0:n], AX.X, ALU.min).then_inc(sem("dec_scaled"), 1)
                eng.wait_ge(sem("dec_scaled"), count(sem("dec_scaled")))
                eng.wait_ge(sem("dec_exp"), due("dve", "dec_exp"))
                V.reciprocal(stat[0:rows, 22:23], stat[0:rows, 21:22]).then_inc(sem("dve_chain"), 1)
                eng.wait_ge(sem("dve_chain"), count(sem("dve_chain")))

            def dec_new(rows, cols, bm):
                for g, c in enumerate(cols):
                    ts(PN[0:rows, g, :], bm, SR[l][0:rows, c:c + 1], None, mul).then_inc(sem("dve_chain"), 1)
                    eng.wait_ge(sem("dve_chain"), count(sem("dve_chain")))

            def zero_pd():
                V.memset(PD[:, :], 0.0).then_inc(sem("pd_zero"), 1)
                eng.wait_ge(sem("pd_zero"), count(sem("pd_zero")))

            def head_rows(kind, wide):
                eng.wait_ge(O.full, O.arrive())
                o = O.reading
                src = ap(o[:, 0:1], [128 if wide else 0, H], [1, 128])
                hm = ap(C("hm32")[:, 0:1], [1, H], [0, 128])
                tt(ap(HR[l][:, 0:1], [128, H], [1, 128]), src, hm, mul).then_inc(O.free, 1)
                eng.wait_ge(O.free, count(O.free))
                eng.sem_inc(sem("dec_head"), 1)
                count(sem("dec_head"))

            def dec_finish(kind, z):
                eng.wait_ge(O.full, O.arrive())
                o = O.reading
                z = z[0:8]
                o = o[0:8, :]
                if kind == "a":
                    V.tensor_copy(z[:, 0:512], o).then_inc(O.free, 1)
                    eng.wait_ge(O.free, count(O.free))
                elif kind in ("cmp", "c", "w"):
                    j = ("cmp", "c", "w").index(kind)
                    g = ap(z[:, ODD["gl"] + j:ODD["gl"] + j + 1], [3, H], [0, 128])
                    acc = z[:, ODD["qc"]:ODD["qc"] + 512]
                    dst = acc if kind == "cmp" else HS[l]
                    tt(ap(dst[:, 0:1], [128, H], [1, 128]), ap(o[:, 0:1], [128, H], [1, 128]), g, mul)\
                        .then_inc(O.free, 1)
                    eng.wait_ge(O.free, count(O.free))
                    if kind != "cmp":
                        tt(acc, acc, dst, add).then_inc(sem("dve_chain"), 1)
                        eng.wait_ge(sem("dve_chain"), count(sem("dve_chain")))
                else:
                    c = EVEN["gb"] if kind == "b" else ODD["gd"]
                    tt(z[:, c:c + 512], z[:, c:c + 512], o, mul).then_inc(O.free, 1)
                    eng.wait_ge(O.free, count(O.free))

            def dec_shared(kind, z, tiles, masked):
                n = tiles * 128
                dec_own(HD, small[0:32, 8:9])
                if kind == "b":
                    tt(small[0:32, 8:9], small[0:32, 8:9], small[0:32, 51:52], add).then_inc(sem("dve_chain"), 1)
                    eng.wait_ge(sem("dve_chain"), count(sem("dve_chain")))
                yield
                for _ in range(NB * tiles // 4 + 1):
                    yield
                bank = S if l == 0 else Q
                eng.wait_ge(bank.full, bank.arrive(2))
                s = bank.reading
                dec_soft(32, s[0:32, 0:n], n + 1, HD ** -0.5, (1, small[0:32, 8:9]))
                ts(SR[l][0:32, 0:n + 1], SR[l][0:32, 0:n + 1], stat[0:32, 22:23], None, mul)\
                    .then_inc(sem("dve_chain"), 1)
                eng.wait_ge(sem("dve_chain"), count(sem("dve_chain")))
                dec_new(32, [n], C("bm32", 32))
                eng.sem_inc(sem("dec_probs"), 1)
                count(sem("dec_probs"))
                zero_pd()
                yield PAUSE
                yield PAUSE
                head_rows(kind, False)
                yield PAUSE
                dec_finish(kind, z)
                yield

            def decode(zs):
                eng.wait_ge(Q.full, Q.arrive(2))
                s = Q.reading
                dec_soft(32, s[0:32, 0:NC_S], NC_S, HD ** -0.5, (0, None))
                ts(SR[l][0:32, 0:NC_S], SR[l][0:32, 0:NC_S], stat[0:32, 22:23], None, mul)\
                    .then_inc(sem("dec_probs"), 1)
                eng.wait_ge(sem("dec_probs"), count(sem("dec_probs")))
                zero_pd()
                yield PAUSE
                eng.wait_ge(sem("imp_T"), due("dve", "imp_T"))
                V.tensor_reduce(small[0:NC_S, 24:32], ap(SA[0:NC_S, 96:97], [4, NB], [1, H]), AX.X, add)\
                    .then_inc(sem("imp_in"), 1)
                eng.wait_ge(sem("imp_in"), count(sem("imp_in")))
                yield PAUSE
                eng.wait_ge(O.full, O.arrive())
                o = O.reading
                imp = RT[0:8, 0:NSEL]
                tt(imp, o[0:8, 0:NSEL], C("bonus", 8), add).then_inc(O.free, 1)
                eng.wait_ge(O.free, count(O.free))
                fill(topk(imp, 16, stat[0:8, 32:40]))
                ts(imp, imp, -2e38, NEG, ALU.is_gt, mul).then_inc(sem("dve_chain"), 1)
                eng.wait_ge(sem("dve_chain"), count(sem("dve_chain")))
                V.tensor_copy(ap(SR[l][0:8, 0:1], [128, ROWS], [8, 16], [1, 8]),
                              ap(imp[:, 0:1], [0, ROWS], [1, 16], [0, 8]))\
                    .then_inc(sem("dve_chain"), 1)
                eng.wait_ge(sem("dve_chain"), count(sem("dve_chain")))
                head_rows("cmp", False)
                yield PAUSE
                dec_finish("cmp", zs)
                eng.sem_inc(sem("dec_mask"), 1)
                count(sem("dec_mask"))
                yield
                yield from dec_shared("c", zs, 8, True)
                yield from dec_shared("w", zs, 4, False)
                for g in range(3):
                    q, k = ODD[f"qd{g}"], ODD[f"kd{g}"]
                    tt(HR[l][0:8], zs[0:8, q:q + 512], zs[0:8, k:k + 512], mul).then_inc(sem("dve_chain"), 1)
                    eng.wait_ge(sem("dve_chain"), count(sem("dve_chain")))
                    V.tensor_reduce(small[0:8, 32 + 4 * g:36 + 4 * g],
                                    ap(HR[l][0:8, 0:1], [128, H], [1, 128]), AX.X, add)\
                        .then_inc(sem("dve_chain"), 1)
                    eng.wait_ge(sem("dve_chain"), count(sem("dve_chain")))
                eng.sem_inc(sem("own_d"), 1)
                count(sem("own_d"))
                yield PAUSE
                eng.wait_ge(O.full, O.arrive())
                o = O.reading
                tt(ap(small[0:32, 0:1], [4, 3], [1, H]), ap(o[0:32, 0:1], [4, 3], [1, H]),
                   ap(C("hm32", 32)[:, 0:1], [0, 3], [1, H]), mul).then_inc(O.free, 1)
                eng.wait_ge(O.free, count(O.free))
                V.tensor_reduce(small[0:32, 12:15], ap(small[0:32, 0:1], [4, 3], [1, H]), AX.X, add)\
                    .then_inc(sem("dve_chain"), 1)
                eng.wait_ge(sem("dve_chain"), count(sem("dve_chain")))
                eng.wait_ge(Q.full, Q.arrive(2))
                s = Q.reading
                V.memset(SR[l][0:32, 0:384], BIG).then_inc(sem("dve_chain"), 1)
                eng.wait_ge(sem("dve_chain"), count(sem("dve_chain")))
                for g in range(3):
                    signal, by = (Q.free, 2) if g == 2 else (sem("dve_chain"), 1)
                    ts(SR[l][0:32, g * 128:g * 128 + DN[g]], s[0:32, g * 128:g * 128 + DN[g]], -(HD ** -0.5),
                       None, mul).then_inc(signal, by)
                    eng.wait_ge(signal, count(signal, by))
                dec_soft(32, None, 387, HD ** -0.5, (3, small[0:32, 12:15]))
                ts(SR[l][0:32, 0:387], SR[l][0:32, 0:387], stat[0:32, 22:23], None, mul).then_inc(sem("dve_chain"), 1)
                eng.wait_ge(sem("dve_chain"), count(sem("dve_chain")))
                dec_new(32, [384, 385, 386], C("bm32", 32))
                eng.sem_inc(sem("dec_probs"), 1)
                count(sem("dec_probs"))
                zero_pd()
                yield PAUSE
                yield PAUSE
                head_rows("d", True)
                yield PAUSE
                dec_finish("d", zs)

            eng.wait_ge(sem("const_in"), 16 * N_SMALL)
            ts(index[:, :], ptab[:, :], float(SUB), C("sub"), mul, add).then_inc(sem("index"), 1)
            eng.wait_ge(sem("index"), count(sem("index")))
            V.memset(rowsT[:, 8192:8208], 0.0).then_inc(sem("rows_tail"), 1)
            eng.wait_ge(sem("rows_tail"), count(sem("rows_tail")))
            V.memset(QD[:, :, :], 0.0).then_inc(sem("dve_chain"), 1)
            eng.wait_ge(sem("dve_chain"), count(sem("dve_chain")))
            V.memset(xTs[:, :, :], 0.0).then_inc(sem("dve_chain"), 1)
            eng.wait_ge(sem("dve_chain"), count(sem("dve_chain")))
            V.memset(small[:, :], 0.0).then_inc(sem("dve_chain"), 1)
            eng.wait_ge(sem("dve_chain"), count(sem("dve_chain")))
            V.memset(stat[:, :], 0.0).then_inc(sem("stat_zero"), 1)
            eng.wait_ge(sem("stat_zero"), count(sem("stat_zero")))
            for j in range(2):
                V.tensor_tensor_reduce(out=RT[:, 128:192], in0=lamr[:, j * 128:j * 128 + 64],
                                       in1=lamr[:, j * 128 + 64:j * 128 + 128], scale=1.0, scalar=0.0,
                                       op0=mul, op1=add, accum_out=lam[:, j:j + 1])\
                    .then_inc(sem("dve_chain"), 1)
                eng.wait_ge(sem("dve_chain"), count(sem("dve_chain")))
            eng.sem_inc(sem("lam_in"), 1)
            count(sem("lam_in"))
            for t in range(3):
                xn(0, t)
            eng.wait_ge(sem("lam_exp"), due("dve", "lam_exp"))
            tt(lam[:, 4:5], lam[:, 2:3], lam[:, 3:4], sub).then_inc(sem("dve_chain"), 1)
            eng.wait_ge(sem("dve_chain"), count(sem("dve_chain")))
            ts(lam[:, 5:6], lam[:, 4:5], LAM_INIT, -1.0, add, mul).then_inc(sem("dve_chain"), 1)
            eng.wait_ge(sem("dve_chain"), count(sem("dve_chain")))
            ts(coef[:, 0:1], C("mone", 64), lam[0:64, 5:6], None, mul).then_inc(sem("dve_chain"), 1)
            eng.wait_ge(sem("dve_chain"), count(sem("dve_chain")))
            tt(coef[:, 1:2], coef[:, 0:1], C("mzero", 64), add).then_inc(sem("dve_chain"), 1)
            eng.wait_ge(sem("dve_chain"), count(sem("dve_chain")))

            for l in (0, 1):
                z, zs = zt[l], zt[l][2]
                n_chunks = len(chunks(l))
                for i in range(n_chunks):
                    eng.wait_ge(*marks[("z", l, i)])
                    if l == 0 and 2 <= i <= 5:
                        score_a(i - 1)
                    for c, heads, step, half in ROTATED[l].get(i, ()):
                        rope_tiles(l, c, heads, step, half)
                    for name in GATES[l].get(i, ()):
                        gate(l, name)
                    if l == 0 and i == 1:
                        tt(RT[0:8, 0:256], zs[0:8, 0:256], zs[0:8, 512:768], mul).then_inc(sem("dve_chain"), 1)
                        eng.wait_ge(sem("dve_chain"), count(sem("dve_chain")))
                        V.tensor_reduce(small[0:8, 32:36], ap(RT[0:8, 0:1], [64, 4], [1, 64]), AX.X, add)\
                            .then_inc(sem("dve_chain"), 1)
                        eng.wait_ge(sem("dve_chain"), count(sem("dve_chain")))
                        tt(RT[0:8, 0:256], zs[0:8, 256:512], zs[0:8, 768:1024], mul).then_inc(sem("dve_chain"), 1)
                        eng.wait_ge(sem("dve_chain"), count(sem("dve_chain")))
                        V.tensor_reduce(small[0:8, 36:40], ap(RT[0:8, 0:1], [64, 4], [1, 64]), AX.X, add)\
                            .then_inc(sem("own_a"), 1)
                        eng.wait_ge(sem("own_a"), count(sem("own_a")))
                        eng.wait_ge(O.full, O.arrive())
                        o = O.reading
                        V.tensor_tensor_reduce(out=small[0:64, 0:8], in0=o[0:64, 0:8], in1=C("hm64", 64), scale=1.0,
                                               scalar=0.0, op0=mul, op1=add, accum_out=small[0:64, 11:12])\
                            .then_inc(O.free, 1)
                        eng.wait_ge(O.free, count(O.free))
                    if l == 0 and i == 1:
                        score_a(0)
                    if l == 1 and i + 1 in SCORE_D:
                        score_d(SCORE_D[i + 1])
                    if l == 1 and i == CMP_AT - 1:
                        hx = [BM[:, 0:NC_P], BM[:, 16:16 + NC_P]]
                        x2 = [BM[:, 32:32 + NC_P], BM[:, 48:48 + NC_P]]
                        for kv in range(2):
                            gelu(hx, x2, False)
                            eng.wait_ge(S.full, S.arrive(2))
                            s = S.reading
                            if kv == 0:
                                V.tensor_copy(BM[0:NC_P, 128:256], s[0:NC_P, 0:128]).then_inc(S.free, 2)
                                eng.wait_ge(S.free, count(S.free, 2))
                                rope(BM[0:NC_P, 128:129], 1, HD, 16, C("ropecp", NC_P))
                            else:
                                V.tensor_copy(VCp[0:NC_P, :], s[0:NC_P, 0:128]).then_inc(S.free, 2)
                                eng.wait_ge(S.free, count(S.free, 2))
                        eng.sem_inc(sem("kcp_roped"), 1)
                        count(sem("kcp_roped"))
                eng.sem_inc(sem("roped"), 1)
                count(sem("roped"))
                mark(f"roped{l}", *latest)
                if l == 0:
                    dec_own(64, small[0:32, 9:10])
                    eng.wait_ge(O.full, O.arrive())
                    o = O.reading
                    V.tensor_tensor_reduce(out=small[0:32, 0:4], in0=o[0:32, 0:4], in1=C("hm32", 32), scale=1.0,
                                           scalar=0.0, op0=mul, op1=add, accum_out=small[0:32, 10:11])\
                        .then_inc(O.free, 1)
                    eng.wait_ge(O.free, count(O.free))
                    ts(small[0:32, 16:24], C("bm32", 32), small[0:32, 10:11], None, mul).then_inc(sem("dve_chain"), 1)
                    eng.wait_ge(sem("dve_chain"), count(sem("dve_chain")))
                    score_a(5)
                    score_a(6)
                    eng.wait_ge(S.full, S.arrive(2))
                    s = S.reading
                    ts(ap(IR[:, 0:1], [1, ROWS], [ROWS, 128]), ap(s[0:32, 0:1], [128, ROWS], [1, 128]),
                       0.0, None, ALU.max).then_inc(S.free, 2)
                    eng.wait_ge(S.free, count(S.free, 2))
                    ts(IR[:, 1024:1025], small[0:32, 9:10], 0.0, None, ALU.max).then_inc(sem("relu_rows"), 1)
                    eng.wait_ge(sem("relu_rows"), count(sem("relu_rows")))
                    score_a(7)
                    eng.sem_inc(sem("scores_a"), 1)
                    count(sem("scores_a"))
                    work = PD[0:8, 0:1025]
                    filler = topk(work, TOPK_S, small[0:8, 52:60])

                    def index_between(i):
                        if i == 1:
                            eng.wait_ge(S.full, S.arrive(2))
                            s = S.reading
                            V.tensor_copy(work[:, 0:1024], s[0:8, :]).then_inc(S.free, 2)
                            eng.wait_ge(S.free, count(S.free, 2))
                            eng.wait_ge(O.full, O.arrive())
                            o = O.reading
                            V.tensor_copy(work[:, 1024:1025], o[0:8, 0:1]).then_inc(O.free, 1)
                            eng.wait_ge(O.free, count(O.free))
                        if i:
                            fill(filler, 3)
                    attention(0, units[0][0:8], 0, index_between)
                    for t in (0, 1):
                        nk = 128 * (t + 1)
                        acc = SM[:, t, 0:nk]
                        for j in (0, 1):
                            eng.wait_ge(S.full, S.arrive())
                            s = S.reading
                            for i in (0, 1):
                                w = z[t][:, EVEN["wi"] + 2 * j + i:EVEN["wi"] + 2 * j + i + 1]
                                dst = acc if j + i == 0 else SM[:, t, 256:256 + nk]
                                signal, by = (S.free, 1) if i else (sem("dve_chain"), 1)
                                ts(dst, s[:, i * nk:(i + 1) * nk], 0.0, w, ALU.max, mul).then_inc(signal, by)
                                eng.wait_ge(signal, count(signal, by))
                                if j + i:
                                    tt(acc, acc, dst, add).then_inc(sem("dve_chain"), 1)
                                    eng.wait_ge(sem("dve_chain"), count(sem("dve_chain")))
                        tt(acc, acc, C(f"causal{t}"), add).then_inc(sem("dve_chain"), 1)
                        eng.wait_ge(sem("dve_chain"), count(sem("dve_chain")))
                    gelu([hid], [hid2], True)
                    eng.wait_ge(S.full, S.arrive(2))
                    s = S.reading
                    V.tensor_copy(kc_rows[0:NC_S, :], s[0:NC_S, :]).then_inc(S.free, 2)
                    eng.wait_ge(S.free, count(S.free, 2))
                    rope(kc_rows[0:NC_S, 0:1], NB, HD, 16, C("ropec", NC_S))
                    eng.sem_inc(sem("kc_roped"), 1)
                    count(sem("kc_roped"))
                    for t in (0, 1):
                        nk = 128 * (t + 1)
                        acc = SM[:, t, 0:nk]
                        fill(topk(acc, TOPK_P, stat[:, 32:40]))
                        bm = BM[:, 0:128] if t == 0 else BM[:, 128:384]
                        ts(bm, acc, -2e38, NEG, ALU.is_gt, mul).then_inc(sem("dve_chain"), 1)
                        eng.wait_ge(sem("dve_chain"), count(sem("dve_chain")))
                        tt(bm, bm, C(f"causal{t}"), add).then_inc(sem("dve_chain"), 1)
                        eng.wait_ge(sem("dve_chain"), count(sem("dve_chain")))
                    eng.sem_inc(sem("topk_prompt"), 1)
                    count(sem("topk_prompt"))
                    attention(0, units[0][8:12], 8, lambda i: fill(filler, 2))
                    fill(filler)
                    ts(ap(kept_keys[:, 0:1], [128, ROWS], [1, 128]), ap(work[:, 0:1], [1, ROWS], [ROWS, 128]),
                       -2e38, NEG, ALU.is_gt, mul).then_inc(sem("dve_chain"), 1)
                    eng.wait_ge(sem("dve_chain"), count(sem("dve_chain")))
                    ts(small[0:8, 50:51], work[:, 1024:1025], -2e38, NEG, ALU.is_gt, mul)\
                        .then_inc(sem("dve_chain"), 1)
                    eng.wait_ge(sem("dve_chain"), count(sem("dve_chain")))
                    eng.wait_ge(S.full, S.arrive(2))
                    s = S.reading
                    dec_soft(64, s[0:64, :], 1025, 0.125, (1, small[0:64, 11:12]))
                    tt(stat[0:64, 22:23], stat[0:64, 22:23], coef[:, 1:2], mul).then_inc(sem("dve_chain"), 1)
                    eng.wait_ge(sem("dve_chain"), count(sem("dve_chain")))
                    ts(SR[l][0:64, 0:1025], SR[l][0:64, 0:1025], stat[0:64, 22:23], None, mul)\
                        .then_inc(sem("dve_chain"), 1)
                    eng.wait_ge(sem("dve_chain"), count(sem("dve_chain")))
                    dec_new(64, [1024], C("bm64", 64))
                    eng.sem_inc(sem("dec_probs"), 1)
                    count(sem("dec_probs"))
                    V.memset(PD[:, :], 0.0).then_inc(sem("dve_chain"), 1)
                    eng.wait_ge(sem("dve_chain"), count(sem("dve_chain")))
                    gelu([hid], [hid2], True)
                    eng.wait_ge(sem("pair_in"), due("dve", "pair_in"))
                    tt(ap(PD[:, 0:1], [256, ROWS], [36, NB], [1, H]),
                       ap(SA[:, 0:1], [64, ROWS], [8, NB], [2, H]),
                       ap(SA[:, 1:2], [64, ROWS], [8, NB], [2, H]), add)\
                        .then_inc(sem("dve_chain"), 1)
                    eng.wait_ge(sem("dve_chain"), count(sem("dve_chain")))
                    tt(PNT[:, 1, 0:32], ap(PNT[:, 0, 0:1], [2, 32]), ap(PNT[:, 0, 1:2], [2, 32]), add)\
                        .then_inc(sem("pd_pairs"), 1)
                    eng.wait_ge(sem("pd_pairs"), count(sem("pd_pairs")))
                    eng.wait_ge(S.full, S.arrive(2))
                    s = S.reading
                    V.tensor_copy(VC[0:NC_S, :, :], ap(s[0:NC_S, 0:1], [HD, NB], [1, HD])).then_inc(S.free, 2)
                    eng.wait_ge(S.free, count(S.free, 2))
                    head_rows("a", True)
                    dec_finish("a", zs)
                    eng.sem_inc(sem("own_mask"), 1)
                    count(sem("own_mask"))
                    eng.wait_ge(O.full, O.arrive())
                    o = O.reading
                    V.tensor_copy(small[0:32, 51:52], o[0:32, 0:1]).then_inc(O.free, 1)
                    eng.wait_ge(O.free, count(O.free))
                    V.tensor_copy(SR[l][0:8, 0:1024], kept_keys).then_inc(sem("dec_mask"), 1)
                    eng.wait_ge(sem("dec_mask"), count(sem("dec_mask")))
                    steps = dec_shared("b", zs, 8, True)
                    fill(steps, 1)
                    for t, (_, n) in enumerate(TOK):
                        o = z[t][0:n, 0:512]
                        tt(SM[0:n, 0, 0:512], o, o, mul).then_inc(sem("dve_chain"), 1)
                        eng.wait_ge(sem("dve_chain"), count(sem("dve_chain")))
                        V.tensor_reduce(stat[0:n, 24 + 4 * t:28 + 4 * t], ap(SM[0:n, 0, 0:1], [128, H], [1, 128]),
                                        AX.X, add).then_inc(sem("dve_chain"), 1)
                        eng.wait_ge(sem("dve_chain"), count(sem("dve_chain")))
                        ts(stat[0:n, 24 + 4 * t:28 + 4 * t], stat[0:n, 24 + 4 * t:28 + 4 * t], 1.0 / HD, EPS,
                           mul, add).then_inc(sem("dve_chain"), 1)
                        eng.wait_ge(sem("dve_chain"), count(sem("dve_chain")))
                    eng.sem_inc(sem("o_a"), 1)
                    count(sem("o_a"))
                    fill(steps, 2 * NB + 2)
                    eng.wait_ge(sem("a_rms"), due("dve", "a_rms", 3))
                    for t, (_, n) in enumerate(TOK):
                        r = stat[0:n, 24 + 4 * t:28 + 4 * t]
                        V.reciprocal(r, r).then_inc(sem("dve_chain"), 1)
                        eng.wait_ge(sem("dve_chain"), count(sem("dve_chain")))
                        ts(r, r, 1.0 - LAM_INIT, None, mul).then_inc(sem("dve_chain"), 1)
                        eng.wait_ge(sem("dve_chain"), count(sem("dve_chain")))
                        o = ap(z[t][0:n, 0:1], [128, H], [1, 128])
                        tt(o, o, ap(r[:, 0:1], [1, H], [0, 128]), mul).then_inc(sem("dve_chain"), 1)
                        eng.wait_ge(sem("dve_chain"), count(sem("dve_chain")))
                        g = z[t][0:n, EVEN["ga"]:EVEN["ga"] + 512]
                        tt(g, g, z[t][0:n, 0:512], mul).then_inc(sem("dve_chain"), 1)
                        eng.wait_ge(sem("dve_chain"), count(sem("dve_chain")))
                    fill(steps)
                else:
                    steps = decode(zs)
                    attention(1, units[1], 12, steps=steps)
                    fill(steps)
                    for t, (_, n) in enumerate(TOK):
                        g = z[t][0:n, ODD["gc"]:ODD["gc"] + 512]
                        tt(g, g, z[t][0:n, 0:512], mul).then_inc(sem("dve_chain"), 1)
                        eng.wait_ge(sem("dve_chain"), count(sem("dve_chain")))
                for t in range(3):
                    eng.sem_inc(sem("mix"), 1)
                    count(sem("mix"))
                eng.sem_inc(sem("y_free"), 1)
                count(sem("y_free"))
                mark(f"mixed{l}", *latest)
                for t, (_, n) in enumerate(TOK):
                    r = norm(t)
                    eng.wait_ge(sem("post_in"), 16 * (l + 1))
                    stt(Y[t][0:n], Y[t][0:n], r, NW[0:n, :], mul, mul).then_inc(sem("dve_chain"), 1)
                    eng.wait_ge(sem("dve_chain"), count(sem("dve_chain")))
                    tt(X[0:n, t, :], X[0:n, t, :], Y[t][0:n], add).then_inc(sem("x_next"), 1)
                    eng.wait_ge(sem("x_next"), count(sem("x_next")))
                    mark(f"x_done{l}_{t}", *latest)
                    if l == 0:
                        xn(1, t)

        @block.sync
        def _(sp):
            small_in = sem("const_in")
            for out, src in SMALL:
                sp.dma_start(out, src, allow_slow_non_contiguous=True).then_inc(small_in, 16)
            def load_norm(dst, name, l, s):
                w = ins[name][l]
                sp.dma_start(dst, bass.AP(w.tensor, w.offset, [[0, 128], [1, D]])).then_inc(sem(s), 16)

            load_norm(NWP, "pre_norm", 0, "pre_in")
            load_norm(NW[:, :], "post_norm", 0, "post_in")
            last = {chunks(l)[-1][0]: l for l in (0, 1)}
            for i, (name, queue, parts) in enumerate(items):
                if queue == "sp":
                    stream(sp, i, name, parts)
                if name == "wout0_512":
                    sp.wait_ge(*marks["mixed0"])
                    load_norm(NWP, "pre_norm", 1, "pre_in")
                if name == "win1_2048":
                    sp.wait_ge(*marks["x_done0_2"])
                    load_norm(NW[:, :], "post_norm", 1, "post_in")
                for l, outs_l in ((0, OUTS0), (1, OUTS1)):
                    if name == (f"win0_{chunks(0)[-1][0]}" if l == 0 else "dk_2"):
                        sp.wait_ge(*marks[f"roped{l}"])
                        for out, src in outs_l:
                            sp.dma_start(out, src).then_inc(sem("out0"), 16)
            for t in range(2):
                sp.wait_ge(*marks[f"x_done1_{t}"])
                sp.dma_start(outs["y_prompt"][0, t * 128:(t + 1) * 128, :], X[:, t, :]).then_inc(sem("out1"), 16)
            sp.wait_ge(*marks["x_done1_2"])
            sp.dma_start(outs["y_sample"].rearrange("b o d -> b (o d)"), X[0:8, 2, :]).then_inc(sem("out1"), 16)
            sp.wait_ge(sem("out1"), 48)
            sp.wait_ge(sem("out0"), 16 * (len(OUTS0) + len(OUTS1)))
            sp.wait_ge(sem("moved"), 16 * len(MOVES))

        @block.gpsimd
        def _(pool):
            pool.wait_ge(sem("index"), 1)
            moves = list(MOVES)
            for i, (name, queue, parts) in enumerate(items):
                if queue == "pool":
                    stream(pool, i, name, parts)
                if name in MOVES_EARLY or name.startswith("win1"):
                    pool.wait_ge(*arrival[items[i - SLOTS][0]])
                    wait_slot(pool, i)
                    for _ in range(MOVES_EARLY.get(name, 3)):
                        if moves:
                            dst, src = moves.pop(0)
                            pool.dma_start(dst, src).then_inc(sem("moved"), 16)
            for dst, src in moves:
                pool.dma_start(dst, src).then_inc(sem("moved"), 16)


NAMES = ("x_prompt", "x_sample", "cache_a_k", "cache_a_v", "cache_b_k", "cache_b_v", "cache_b_idx",
         "cache_c_cmp_k", "cache_c_cmp_v", "cache_c_sel_k", "cache_c_sel_v", "state_c_win_k", "state_c_win_v",
         "state_d_k0", "state_d_v0", "state_d_k1", "state_d_v1", "state_d_k2", "state_d_v2", "page_table",
         "pre_norm", "post_norm", "w_in_even", "w_out_even", "diff_lambda", "w_in_odd", "w_out_odd", "cmp_pos",
         "cmp_w1", "cmp_w2")


def out_shapes():
    seq, dec = 256, NB
    o = [("y_prompt", (1, seq, D)), ("y_sample", (dec, 1, D))]
    for tag, n, t in (("p_", 1, seq), ("s_", dec, 1)):
        even = [("a_k", (1, n, t, H, 2, 64)), ("a_v", (1, n, t, H, HD)), ("b_k", (1, n, t, HD)),
                ("b_v", (1, n, t, HD)), ("b_idx", (1, n, t, 64))]
        o += [(tag + a, s) for a, s in even]
    def odd(tag, n, t, win, ds):
        r = [(tag + a, (1, n, t, HD)) for a in ("c_cmp_k", "c_cmp_v", "c_sel_k", "c_sel_v")]
        r += [(tag + a, (1, n, win, HD)) for a in ("c_win_k", "c_win_v")]
        for g, w in enumerate(ds):
            r += [(tag + f"d_{kv}{g}", (1, n, w, H, HD)) for kv in "kv"]
        return r
    p_even = [x for x in o if x[0].startswith("p_")]
    s_even = [x for x in o if x[0].startswith("s_")]
    head = o[:2]
    p_odd = odd("p_", 1, seq, min(WIN, seq), [min(w, seq) for w, _ in PAIRS])
    s_odd = odd("s_", dec, 1, WIN, [min(w, DW[g] + 1) for g, (w, _) in enumerate(PAIRS)])
    return head + p_even + p_odd + s_even + s_odd


def kernel(**inputs):
    import concourse.bacc as bacc
    from concourse.bass_utils import run_bass_kernel_spmd

    nc = bacc.Bacc("TRN2", target_bir_lowering=False, num_devices=1)
    arrays, ins, outs = {}, {}, {}
    for name in NAMES + ("const",):
        a = constants() if name == "const" else np.ascontiguousarray(inputs[name])
        arrays[f"in_{name}"] = a
        ins[name] = nc.dram_tensor(f"in_{name}", a.shape, mybir.dt.from_np(a.dtype), kind="ExternalInput").ap()
    shapes = out_shapes()
    for name, shape in shapes:
        outs[name] = nc.dram_tensor(f"out_{name}", shape, F32, kind="ExternalOutput").ap()
    build(nc, ins, outs)
    r = run_bass_kernel_spmd(nc, [arrays], core_ids=[0])
    return tuple(r.results[0][f"out_{name}"] for name, _ in shapes)
```
